# Optimizing a Trainium2 kernel written in Bass

```python
import jax, jax.numpy as jnp
from jax import lax
import numpy as np

D_MODEL = 1024
BATCH = 1
SEQ = 256
DEPTH = 1

CHUNK = 64
N_META = 16
ROPE_THETA = 10000.0
RMS_EPS = 1e-6
D_MIX = D_MODEL
HEAD_DIM = 64
D_ATTN = D_MIX // 2
ATTN_HEADS = D_ATTN // HEAD_DIM
IDX_HEADS = 8
IDX_DIM = 64
TOPK_MAX = 256
Q_BLOCK = 128
POOL_WINDOWS = (2, 4, 8, 16)
POOL_GROUPS = 4
D_POOL = D_MIX - D_ATTN
POOL_CH = D_POOL // POOL_GROUPS
OFF_Q = 0
OFF_K = OFF_Q + D_ATTN
OFF_V = OFF_K + D_ATTN
OFF_POOL = OFF_V + D_ATTN
OFF_IQ = OFF_POOL + D_POOL
OFF_IK = OFF_IQ + IDX_HEADS * IDX_DIM
OFF_IW = OFF_IK + IDX_DIM
D_IN_PROJ = OFF_IW + IDX_HEADS
PEER_HEADS = 8
N_KEYS = 128
N_EXPERTS = N_KEYS * N_KEYS
PEER_QDIM = 256
PEER_HALF = PEER_QDIM // 2
PEER_TOPK = 16
TOK_BLOCK = 256

kernel_name = 'hymba_dsa_pool_peer_layer'

def rms_norm(x, g):
    xf = x.astype(jnp.float32)
    y = xf * lax.rsqrt(jnp.mean(xf * xf, axis=-1, keepdims=True) + RMS_EPS)
    return (y * g.astype(jnp.float32)).astype(x.dtype)

def rope_tables(T, dim):
    inv = ROPE_THETA ** (-jnp.arange(0, dim, 2, dtype=jnp.float32) / dim)
    ang = jnp.arange(T, dtype=jnp.float32)[:, None] * inv[None, :]
    return jnp.cos(ang), jnp.sin(ang)

def apply_rope(x, cos, sin):
    xf = x.astype(jnp.float32)
    x1, x2 = jnp.split(xf, 2, axis=-1)
    c = cos[None, :, None, :]
    s = sin[None, :, None, :]
    return jnp.concatenate([x1 * c - x2 * s, x2 * c + x1 * s], axis=-1).astype(x.dtype)

def chunk_ids(T):
    pos = jnp.arange(T, dtype=jnp.int32)
    return jnp.where(pos < N_META, 0, 1 + (pos - N_META) // CHUNK)

def dsa_attention(q, k, v, qi, ki, wi, k_sel):
    B, T = q.shape[0], q.shape[1]
    nb = -(-T // Q_BLOCK)
    Tp = nb * Q_BLOCK
    pad = Tp - T
    cid = chunk_ids(T)
    cq_all = chunk_ids(Tp).reshape(nb, Q_BLOCK)

    def blocks(a):
        a = jnp.pad(a, [(0, 0), (0, pad)] + [(0, 0)] * (a.ndim - 2))
        return a.reshape((B, nb, Q_BLOCK) + a.shape[2:]).swapaxes(0, 1)

    gather = jax.vmap(lambda a, i: a[i])

    def one_block(args):
        qb, qib, wb, cqb = args
        rel = jax.nn.relu(jnp.einsum('bqhd,bsd->bqhs', qib, ki, preferred_element_type=jnp.float32))
        score = jnp.einsum('bqhs,bqh->bqs', rel, wb.astype(jnp.float32))
        vis = cid[None, :] <= cqb[:, None]
        score = jnp.where(vis[None], score, -jnp.inf)
        _, idx = lax.top_k(score, k_sel)
        ks = gather(k, idx)
        vs = gather(v, idx)
        ok = cid[idx] <= cqb[None, :, None]
        logits = jnp.einsum('bqhd,bqkhd->bhqk', qb, ks,
                            preferred_element_type=jnp.float32) * (HEAD_DIM ** -0.5)
        logits = jnp.where(ok[:, None], logits, -jnp.inf)
        p = jax.nn.softmax(logits, axis=-1).astype(vs.dtype)
        return jnp.einsum('bhqk,bqkhd->bqhd', p, vs)

    out = lax.map(one_block, (blocks(q), blocks(qi), blocks(wi), cq_all))
    out = out.swapaxes(0, 1).reshape(B, Tp, q.shape[2], q.shape[3])[:, :T]
    return out

def pool_mixer(u, pool_w, pool_scale):
    B, T, _ = u.shape
    uf = u.astype(jnp.float32).reshape(B, T, POOL_GROUPS, POOL_CH)
    c = jnp.cumsum(jnp.pad(uf, ((0, 0), (1, 0), (0, 0), (0, 0))), axis=1)
    t = jnp.arange(T, dtype=jnp.int32)
    means = []
    for g, w in enumerate(POOL_WINDOWS):
        lo = jnp.maximum(t + 1 - w, 0)
        cnt = jnp.minimum(t + 1, w).astype(jnp.float32)
        means.append((c[:, 1:, g] - c[:, lo, g]) / cnt[None, :, None])
    y = (jnp.stack(means, axis=2) - uf).astype(u.dtype)
    y = jnp.einsum('btgc,gcd->btgd', y, pool_w).reshape(B, T, D_POOL)
    return y * pool_scale

def peer_ffn(h, peer_wq, sub_keys1, sub_keys2, peer_u, peer_v):
    B, T, D = h.shape
    q = (h @ peer_wq).reshape(B, T, PEER_HEADS, PEER_QDIM)
    q1, q2 = q[..., :PEER_HALF], q[..., PEER_HALF:]
    s1 = jnp.einsum('bthd,nd->bthn', q1, sub_keys1, preferred_element_type=jnp.float32)
    s2 = jnp.einsum('bthd,nd->bthn', q2, sub_keys2, preferred_element_type=jnp.float32)
    v1, i1 = lax.top_k(s1, PEER_TOPK)
    v2, i2 = lax.top_k(s2, PEER_TOPK)
    n_cand = PEER_TOPK * PEER_TOPK
    cand_s = (v1[..., :, None] + v2[..., None, :]).reshape(B, T, PEER_HEADS, n_cand)
    cand_i = (i1[..., :, None] * N_KEYS + i2[..., None, :]).reshape(B, T, PEER_HEADS, n_cand)
    top_s, pos = lax.top_k(cand_s, PEER_TOPK)
    eid = jnp.take_along_axis(cand_i, pos, axis=-1)
    gate = jax.nn.softmax(top_s, axis=-1)
    n = B * T
    npad = -(-n // TOK_BLOCK) * TOK_BLOCK
    kk = PEER_HEADS * PEER_TOPK
    hf = jnp.pad(h.reshape(n, D), ((0, npad - n), (0, 0))).reshape(-1, TOK_BLOCK, D)
    ef = jnp.pad(eid.reshape(n, kk), ((0, npad - n), (0, 0))).reshape(-1, TOK_BLOCK, kk)
    gf = jnp.pad(gate.reshape(n, kk), ((0, npad - n), (0, 0))).reshape(-1, TOK_BLOCK, kk)

    def one_block(args):
        hb, eb, gb = args
        a = jnp.einsum('td,tkd->tk', hb, peer_u[eb], preferred_element_type=jnp.float32)
        a = jax.nn.gelu(a, approximate=False)
        return jnp.einsum('tk,tkd->td', (gb * a).astype(hb.dtype), peer_v[eb])

    out = lax.map(one_block, (hf, ef, gf))
    return out.reshape(npad, D)[:n].reshape(B, T, D)

def setup_inputs(seed: int = 0) -> dict:
    key = jax.random.key(seed)
    ks = jax.random.split(key, 16)
    nrm = jax.random.normal
    f32 = jnp.float32
    return {
        'x': nrm(ks[0], (BATCH, SEQ, D_MODEL), f32),
        'meta_tokens': nrm(ks[1], (N_META, D_MODEL), f32),
        'norm1_g': 1.0 + 0.02 * nrm(ks[2], (DEPTH, D_MODEL), f32),
        'w_in': nrm(ks[3], (DEPTH, D_MODEL, D_IN_PROJ), f32) * D_MODEL ** -0.5,
        'q_norm_g': 1.0 + 0.02 * nrm(ks[4], (DEPTH, HEAD_DIM), f32),
        'k_norm_g': 1.0 + 0.02 * nrm(ks[5], (DEPTH, HEAD_DIM), f32),
        'pool_w': nrm(ks[6], (DEPTH, POOL_GROUPS, POOL_CH, POOL_CH), f32) * POOL_CH ** -0.5,
        'pool_scale': 1.0 + 0.1 * nrm(ks[7], (DEPTH, D_POOL), f32),
        'w_out': nrm(ks[8], (DEPTH, D_MIX, D_MODEL), f32) * D_MIX ** -0.5,
        'norm2_g': 1.0 + 0.02 * nrm(ks[9], (DEPTH, D_MODEL), f32),
        'peer_wq': nrm(ks[10], (DEPTH, D_MODEL, PEER_HEADS * PEER_QDIM), f32) * D_MODEL ** -0.5,
        'sub_keys1': nrm(ks[11], (DEPTH, N_KEYS, PEER_HALF), f32) * PEER_HALF ** -0.5,
        'sub_keys2': nrm(ks[12], (DEPTH, N_KEYS, PEER_HALF), f32) * PEER_HALF ** -0.5,
        'peer_u': nrm(ks[13], (DEPTH, N_EXPERTS, D_MODEL), f32) * D_MODEL ** -0.5,
        'peer_v': nrm(ks[14], (DEPTH, N_EXPERTS, D_MODEL), f32) * PEER_HEADS ** -0.5,
    }

def reference(x, meta_tokens, norm1_g, w_in, q_norm_g, k_norm_g, pool_w, pool_scale,
              w_out, norm2_g, peer_wq, sub_keys1, sub_keys2, peer_u, peer_v):
    B, S, D = x.shape
    k_sel = min(TOPK_MAX, S // 4)
    T = S + N_META
    h = jnp.concatenate([jnp.broadcast_to(meta_tokens.astype(x.dtype)[None], (B, N_META, D)), x], axis=1)
    cos, sin = rope_tables(T, HEAD_DIM)
    for l in range(DEPTH):
        z = rms_norm(h, norm1_g[l]) @ w_in[l]
        q = z[..., OFF_Q:OFF_K].reshape(B, T, ATTN_HEADS, HEAD_DIM)
        k = z[..., OFF_K:OFF_V].reshape(B, T, ATTN_HEADS, HEAD_DIM)
        v = z[..., OFF_V:OFF_POOL].reshape(B, T, ATTN_HEADS, HEAD_DIM)
        q = apply_rope(rms_norm(q, q_norm_g[l]), cos, sin)
        k = apply_rope(rms_norm(k, k_norm_g[l]), cos, sin)
        qi = apply_rope(z[..., OFF_IQ:OFF_IK].reshape(B, T, IDX_HEADS, IDX_DIM), cos, sin)
        ki = apply_rope(z[..., OFF_IK:OFF_IW][:, :, None, :], cos, sin)[:, :, 0, :]
        wi = z[..., OFF_IW:D_IN_PROJ] * (IDX_HEADS ** -0.5 * IDX_DIM ** -0.5)
        a = dsa_attention(q, k, v, qi, ki, wi, k_sel).reshape(B, T, D_ATTN)
        p = pool_mixer(z[..., OFF_POOL:OFF_IQ], pool_w[l], pool_scale[l])
        h = h + jnp.concatenate([a, p], axis=-1) @ w_out[l]
        h = h + peer_ffn(rms_norm(h, norm2_g[l]), peer_wq[l], sub_keys1[l], sub_keys2[l],
                         peer_u[l], peer_v[l])
    return h[:, N_META:]


_drawn_inputs = setup_inputs


def setup_inputs(seed=0):
    import zlib

    import numpy as np

    out = dict(_drawn_inputs(seed))
    spreads = {}
    factors = {'q_norm_g': 6.764, 'k_norm_g': 6.062, 'norm2_g': 2.929}
    for name, (base, spread) in spreads.items():
        noise = np.random.default_rng([zlib.crc32(name.encode()), seed]).standard_normal(out[name].shape)
        drawn = base * np.exp(spread * noise) if base else spread * noise
        out[name] = __import__('jax').numpy.asarray(drawn.astype(out[name].dtype))
    for name, factor in factors.items():
        out[name] = (out[name] * factor).astype(out[name].dtype)
    return out
```

```python
import concourse.bass as bass
from concourse import mybir
from contextlib import ExitStack

F32 = mybir.dt.float32
F32R = mybir.dt.float32r
U32 = mybir.dt.uint32
ALU = mybir.AluOpType
ACT = mybir.ActivationFunctionType
AX = mybir.AxisListType
ds = bass.ds

P = 128
SEQ, META = 256, 16
T = SEQ + META
D = 1024
DK = D // P
HD, NH = 64, 8
PAIRS = NH // 2
KSEL = 64
EPS = 1e-6
NEG = -3.0e38
NK = 128
PH, TOPK = 8, 16
QUAD = 4
CW = 256

KEYS = [META + P, META + 2 * P]
KOFF = [0, KEYS[0]]
KALL = KEYS[0] + KEYS[1]

STAIRS, off = [], 0
for first, rows in ((0, 1), (1, 1), (2, 1), (3, 1), (4, 1), (5, 3), (8, 8)):
    cols = TOPK // (first + 1)
    STAIRS.append((first, rows, cols, off))
    off += rows * cols
NCAND = off

C_Q, C_K, C_V, C_POOL, C_IQ, C_IK = 0, 512, 1024, 1536, 2048, 2560
CI = HD + NH
W_IN = [C_IK, C_IQ, C_IQ + CW, C_Q, C_Q + CW, C_K, C_K + CW, C_V, C_V + CW, C_POOL, C_POOL + CW]
N_IN, N_OUT, N_WQ = len(W_IN), D // CW, PH
N_CHUNK = N_IN + N_OUT + N_WQ
OUT0, WQ0 = N_IN, N_IN + N_OUT
K_ID, K_IOTA, K_COS, K_SIN, K_BAND = 0, 128, 256, 448, 640
N_CONST = K_BAND + 3 * 4 * P


def chunk_tiles(c):
    return (3 if c == 0 or 5 <= c < N_IN else 2) if c < WQ0 else 1


def z_after(c):
    return sum(chunk_tiles(k) for k in range(c + 1))


class Count:

    def __init__(self):
        self.n = 0

    def up(self):
        self.n += 1
        return self.n


def layer(nc, x, meta, g1, w_in, gq, gk, pool_w, pool_s, w_out, g2, wq, sk1, sk2, pu, pv, const, out):
    ctx = ExitStack()
    with ctx:
        def sb(name, shape, dt=F32):
            return ctx.enter_context(nc.sbuf_tensor(name, shape, dt))

        def sem(name):
            return ctx.enter_context(nc.semaphore(name))

        big = sb("big", [P, NK * SEQ])
        gates = big[:, :].rearrange("p (n t) -> p n t", t=SEQ)
        rr = sb("rr", [P, 8448], F32R)
        ht = sb("ht", [P, 2, DK, SEQ], F32R)
        raw = sb("raw", [P, 5120])
        cst = sb("cst", [P, 256])
        picks = sb("picks", [P, 3, SEQ])
        gel = sb("gel", [P, 2, SEQ])
        psum = ctx.enter_context(nc.psum_tensor("psum", [P, 8, 512], F32))
        h_dram = nc.dram_tensor("h_kept", [2, P, D], F32, kind="Internal").ap()

        at = 0

        def take(n):
            nonlocal at
            at += n
            assert at <= NK * SEQ
            return big[:, at - n:at]

        xt = take(2 * D).rearrange("p (t d) -> p t d", t=2)
        xm = take(D)
        xs_at = at
        xs = take(3 * D).rearrange("p (t d) -> p t d", t=3)
        t32 = take(DK * SEQ).rearrange("p (k t) -> p k t", k=DK)
        t32m = take(DK * META).rearrange("p (k t) -> p k t", k=DK)
        wraw = take(3 * DK * CW).rearrange("p (s k n) -> p s k n", s=3, k=DK)
        z_at = at
        zq = take(2 * 512).rearrange("p (t n) -> p t n", t=2)
        ziq = take(2 * 512).rearrange("p (t n) -> p t n", t=2)
        zk = take(3 * 512).rearrange("p (t n) -> p t n", t=3)
        zv = take(3 * 512).rearrange("p (t n) -> p t n", t=3)
        zp = take(3 * 512).rearrange("p (t n) -> p t n", t=3)
        zi = take(3 * CI).rearrange("p (t n) -> p t n", t=3)
        rot_at = at
        qr = take(2 * 512).rearrange("p (t n) -> p t n", t=2)
        kr = take(3 * 512).rearrange("p (t n) -> p t n", t=3)
        tmp = take(3 * 512).rearrange("p (a n) -> p a n", a=3)
        iqr = take(2 * 512).rearrange("p (t n) -> p t n", t=2)
        kir = take(3 * P).rearrange("p (t n) -> p t n", t=3)
        stat = take(256)
        cossin = take(6 * HD)
        cos, sin = (cossin[:, a * 3 * HD:(a + 1) * 3 * HD].rearrange("p (t n) -> p t n", t=3) for a in range(2))
        gqk = take(2 * HD).rearrange("p (a n) -> p a n", a=2)
        score = take(KALL)
        work = take(KALL)
        bias = take(KALL)
        top8 = take(8)
        grow = take(P)
        at = max(at, NK * SEQ - 640)
        ksub = take(2 * P).rearrange("p (a n) -> p a n", a=2)
        kt_sub = take(2 * P).rearrange("p (a n) -> p a n", a=2)
        gains = take(20)
        half = take(1)
        scal = take(64)
        rel = big[:, rot_at:rot_at + NH * KALL]
        at = xs_at
        iqt = take(PAIRS * SEQ).rearrange("p (a t) -> p a t", a=PAIRS)
        kit = take(T)
        qt = take(PAIRS * SEQ).rearrange("p (a t) -> p a t", a=PAIRS)
        kt = take(PAIRS * T).rearrange("p (a t) -> p a t", a=PAIRS)
        yt = take(4 * SEQ).rearrange("p (a t) -> p a t", a=4)
        p32 = iqt
        at = z_at
        qp = take(2 * 2 * SEQ).rearrange("p (s a t) -> p s a t", s=2, a=2)
        sc = take(PH * 4 * NK).rearrange("p (h t a n) -> p h t a n", h=PH, t=2, a=2)
        v16 = take(PH * 64).rearrange("p (h t a k) -> p h t a k", h=PH, t=2, a=2)
        i16 = take(PH * 64).rearrange("p (h t a k) -> p h t a k", h=PH, t=2, a=2).bitcast(U32)
        n16 = take(PH * 64).rearrange("p (h t a k) -> p h t a k", h=PH, t=2, a=2)
        cand = take(PH * 2 * NCAND).rearrange("p (h t c) -> p h t c", h=PH, t=2)
        cide = take(PH * 2 * NCAND).rearrange("p (h t c) -> p h t c", h=PH, t=2)
        vtop = take(PH * 32).rearrange("p (t h k) -> p t h k", h=PH, t=2)
        ptop = take(PH * 32).rearrange("p (t h k) -> p t h k", h=PH, t=2).bitcast(U32)
        ntop = take(PH * 32).rearrange("p (t h k) -> p t h k", h=PH, t=2)
        eid = take(PH * 32).rearrange("p (t h k) -> p t h k", h=PH, t=2)
        eqs = take(2 * 2 * TOPK * NCAND).rearrange("p (s t k c) -> p s t k c", s=2, t=2, k=TOPK)
        pick3 = take(3 * PH * 32).rearrange("p (a t h k) -> p a t h k", a=3, t=2, h=PH)
        eint = take(PH * 32).rearrange("p (t h k) -> p t h k", h=PH, t=2).bitcast(mybir.dt.int32)
        fint = take(PH * 32).rearrange("p (t h k) -> p t h k", h=PH, t=2).bitcast(mybir.dt.int32)
        assert at <= NK * SEQ - 640

        ident, iota = cst[:, 0:P], cst[:, P:2 * P]
        band = raw[:, 0:3 * 512].rearrange("p (a g t) -> p a g t", a=3, g=4)
        poolw = raw[:, 1536:2048].rearrange("p (g d) -> p g d", g=4)
        pt = raw[:, :].rearrange("p (c h q) -> p c h q", c=5, h=NH)
        u_raw = raw[:, 0:2 * D].rearrange("p (s k c) -> p s k c", s=2, k=DK)
        v_raw = raw[:, 2 * D:4 * D].rearrange("p (s d) -> p s d", s=2)
        oh2 = raw[:, 2 * D:3 * D].rearrange("p (s q n) -> p s q n", s=2, q=QUAD)
        oh1 = raw[:, 4 * D:5 * D].rearrange("p (s q n) -> p s q n", s=2, q=QUAD)
        w_sp = rr[:, 0:8192].rearrange("p (s a k n) -> p s a k n", s=2, a=2, k=DK)
        hm = rr[:, 8192:8448].rearrange("p (a k t) -> p a k t", a=2, k=DK)
        ut = rr[:, 0:2 * D].rearrange("p (a k n) -> p a k n", a=2, k=DK)
        v_sp = rr[:, 2 * D:6 * D].rearrange("p (s a d) -> p s a d", s=2, a=2)
        g_sp = rr[:, 6 * D:7 * D].rearrange("p (s a t) -> p s a t", s=2, a=2)

        def f(ap):
            return ap.bitcast(F32)

        rows = [P, P, META]
        trow = [1, 2, 0]

        ld_x = [sem(f"ld_x{t}") for t in range(3)]
        ld_cst, ld_rope, ld_small, ld_g2, ld_band = (sem(n) for n in ("ld_cst", "ld_rope", "ld_small", "ld_g2", "ld_band"))
        ld_w = [sem(f"ld_w{s}") for s in range(3)]
        ld_u = [sem(f"ld_u{s}") for s in range(2)]
        ld_v = [sem(f"ld_v{s}") for s in range(2)]
        ld_h = sem("ld_h")
        st_h, st_out = sem("st_h"), sem("st_out")
        a_sq, a_xs, a_hi, w_hi, z_ev = sem("a_sq"), sem("a_xs"), sem("a_hi"), sem("w_hi"), sem("z_ev")
        ix_tr, a_rel, y_ev, pc_hi, qk_tr = sem("ix_tr"), sem("a_rel"), sem("y_ev"), sem("pc_hi"), sem("qk_tr")
        a_exp, pt_ev, cat_hi, qp_ev, s_ev = sem("a_exp"), sem("pt_ev"), sem("cat_hi"), sem("qp_ev"), sem("s_ev")
        a_soft, b_ev, ut_hi, v_hi, a_gel = sem("a_soft"), sem("b_ev"), sem("ut_hi"), sem("v_hi"), sem("a_gel")
        ks_ev, pk_ev = sem("ks_ev"), sem("pk_ev")
        d_ms, d_t32, d_lo, w_lo_e, d_seq = sem("d_ms"), sem("d_t32"), sem("d_lo"), sem("w_lo_e"), sem("d_seq")
        d_ki, d_iq, d_qst, d_kst, d_qk = sem("d_ki"), sem("d_iq"), sem("d_qst"), sem("d_kst"), sem("d_qk")
        d_p32, pc_lo, d_log, d_max, d_prob = sem("d_p32"), sem("pc_lo"), sem("d_log"), sem("d_max"), sem("d_prob")
        cat_lo, h_ev, d_top, d_match, d_sub = sem("cat_lo"), sem("h_ev"), sem("d_top"), sem("d_match"), sem("d_sub")
        d_pick, oh1_up, ut_lo, v_lo, g_lo = sem("d_pick"), sem("oh1_up"), sem("ut_lo"), sem("v_lo"), sem("g_lo")
        d_g32, d_out = sem("d_g32"), sem("d_out")
        p_half, p_rs, w_lo_o, p_seq, p_eq, oh2_up = (sem(n) for n in ("p_half", "p_rs", "w_lo_o", "p_seq", "p_eq", "oh2_up"))
        pe_x, z_done, pe_ix, pe_sc, pe_y = sem("pe_x"), sem("z_done"), sem("pe_ix"), sem("pe_sc"), sem("pe_y")
        pe_qk, pe_log, pe_pt, pe_cat, pe_ks = sem("pe_qk"), sem("pe_log"), sem("pe_pt"), sem("pe_cat"), sem("pe_ks")
        pe_gain = sem("pe_gain")
        pe_s, pe_pk, b_done, t_done, a_done, c_done = (sem(n) for n in ("pe_s", "pe_pk", "b_done", "t_done", "a_done", "c_done"))

        pu_v = pu[0].rearrange("(n m) d -> n m d", m=NK)
        pv_v = pv[0].rearrange("(n m) d -> n m d", m=NK)

        def w_src(c):
            w, first = (w_in, W_IN[c]) if c < OUT0 else (w_out, (c - OUT0) * CW) if c < WQ0 else (wq, (c - WQ0) * CW)
            n = CI if c == 0 else CW
            return w[0, :, first:first + n].rearrange("(k p) n -> p k n", p=P), n

        def w_cols(c):
            return CI if c == 0 else CW

        def lo_ready(eng, c):
            eng.wait_ge(w_lo_o if c % 2 else w_lo_e, c // 2 + 1)

        block = ctx.enter_context(nc.Block())

        @block.sync
        def _(sp):
            def load_w(c):
                if c >= 3:
                    sp.wait_ge(w_hi, c - 2)
                    lo_ready(sp, c - 3)
                src, n = w_src(c)
                sp.dma_start(wraw[:, c % 3, :, 0:n], src).then_inc(ld_w[c % 3], 16)

            sp.dma_start(xt[:, 0, :], x[0, 0:P, :]).then_inc(ld_x[0], 16)
            sp.dma_start(xt[:, 1, :], x[0, P:2 * P, :]).then_inc(ld_x[1], 16)
            sp.dma_start(xm[0:META, :], meta[:, :]).then_inc(ld_x[2], 16)
            load_w(0)
            sp.dma_start(cst[:, :], const[:, 0:K_COS]).then_inc(ld_cst, 16)
            load_w(1)
            load_w(2)
            sp.dma_start(cossin, const[:, K_COS:K_BAND]).then_inc(ld_rope, 16)
            for c in range(3, 6):
                load_w(c)
            sp.dma_start(band, const[:, K_BAND:N_CONST].rearrange("p (a g t) -> p a g t", a=3, g=4)).then_inc(ld_band, 16)
            sp.dma_start(poolw, pool_w[0].rearrange("g c d -> c g d")).then_inc(ld_band, 16)
            sp.dma_start(ksub[:, 0, :], sk1[0]).then_inc(ld_g2, 16)
            sp.dma_start(ksub[:, 1, :], sk2[0]).then_inc(ld_g2, 16)
            for c in range(6, OUT0 + 4):
                load_w(c)
            for c in range(OUT0 + 4, WQ0 + 4):
                load_w(c)
            sp.wait_ge(h_ev, 2 * N_OUT)
            for t in range(2):
                sp.dma_start(h_dram[t], xt[:, t, :]).then_inc(st_h, 16)
            for c in range(WQ0 + 4, N_CHUNK):
                load_w(c)
            sp.wait_ge(pe_cat, 2)
            for s in range(2):
                sp.dma_start(u_raw[:, s], pu_v[:, s, :].rearrange("p (k c) -> p k c", k=DK)).then_inc(ld_u[s], 16)
            sp.wait_ge(b_done, SEQ // QUAD)
            for s in range(2):
                sp.dma_start(v_raw[:, s, :], pv_v[:, s, :]).then_inc(ld_v[s], 16)
            with sp.Fori(0, NK // 2 - 1) as i:
                for s in range(2):
                    sp.wait_ge(t_done, 2 * i + (s + 1))
                    sp.dma_start(u_raw[:, s], pu_v[:, ds(2 * i + (s + 2), 1), :].rearrange("p o (k c) -> p (o k) c", k=DK))\
                      .then_inc(ld_u[s], 16)
                    sp.wait_ge(v_hi, 2 * i + (s + 1))
                    sp.wait_ge(v_lo, 2 * i + (s + 1))
                    sp.dma_start(v_raw[:, s, :], pv_v[:, ds(2 * i + (s + 2), 1), :].rearrange("p o d -> p (o d)"))\
                      .then_inc(ld_v[s], 16)
            sp.wait_ge(st_h, 32)
            sp.wait_ge(t_done, NK)
            for t in range(2):
                sp.dma_start(raw[:, t * D:(t + 1) * D], h_dram[t]).then_inc(ld_h, 16)
            for t in range(2):
                sp.wait_ge(d_out, 2 * t + 2)
                sp.dma_start(out[0, t * P:(t + 1) * P, :], big[:, t * D:(t + 1) * D]).then_inc(st_out, 16)
            sp.wait_ge(st_out, 32)

        @block.scalar
        def _(act):
            act.dma_start(grow[0:8, :], g1[0].rearrange("(k p) -> k p", p=P)).then_inc(ld_small, 16)
            act.dma_start(grow[8:16, :], g2[0].rearrange("(k p) -> k p", p=P)).then_inc(ld_small, 16)
            act.dma_start(grow[16:20, :], pool_s[0].rearrange("(k p) -> k p", p=P)).then_inc(ld_small, 16)
            act.dma_start(gqk[:, 0, :], gq[0:1, :].to_broadcast([P, HD])).then_inc(ld_small, 16)
            act.dma_start(gqk[:, 1, :], gk[0:1, :].to_broadcast([P, HD])).then_inc(ld_small, 16)

            def split_w(c):
                act.wait_ge(ld_w[c % 3], 16 * (c // 3 + 1))
                if c >= 2:
                    act.wait_ge(z_done, z_after(c - 2))
                n = w_cols(c)
                act.activation(w_sp[:, c % 2, 0, :, 0:n], wraw[:, c % 3, :, 0:n], ACT.Copy).then_inc(w_hi, 1)

            srcs = [xt[:, 0, :], xt[:, 1, :], xm[0:META, :]]
            for t, r in enumerate(rows):
                act.wait_ge(ld_x[t], 16)
                act.activation(xs[0:r, t, :], srcs[t], ACT.Square, accum_out=stat[0:r, t:t + 1]).then_inc(a_sq, 1)
            split_w(0)
            split_w(1)
            for t, r in enumerate(rows):
                act.wait_ge(p_rs, t + 1)
                act.wait_ge(a_sq, t + 1)
                act.activation(xs[0:r, t, :], srcs[t], ACT.Copy, scale=scal[0:r, 8 + t:9 + t]).then_inc(a_xs, 1)
            for t in range(3):
                act.wait_ge(d_t32, t + 1)
                dst, src = (ht[:, 0, :, t * P:(t + 1) * P], t32[:, :, t * P:(t + 1) * P]) if t < 2 else (hm[:, 0], t32m)
                act.activation(dst, src, ACT.Copy).then_inc(a_hi, 1)

            def keep_z(c):
                sec, first = {0: (zi, 0), 1: (ziq, 0), 2: (ziq, CW), 3: (zq, 0), 4: (zq, CW), 5: (zk, 0), 6: (zk, CW),
                              7: (zv, 0), 8: (zv, CW), 9: (zp, 0), 10: (zp, CW)}[c]
                n = w_cols(c)
                for t in range(chunk_tiles(c)):
                    act.wait_ge(z_done, z_after(c) - chunk_tiles(c) + t + 1)
                    r = rows[t]
                    act.activation(sec[0:r, t, first:first + n], psum[0:r, 3 * (c % 2) + t, 0:n], ACT.Copy)\
                       .then_inc(z_ev, 1)

            for c in range(5):
                keep_z(c)
                split_w(c + 2)
            for t in range(2):
                act.wait_ge(pe_ix, t + 1)
                act.activation(iqt[:, :, t * P:(t + 1) * P], psum[:, t, :].rearrange("p (a q) -> p a q", a=PAIRS),
                               ACT.Copy).then_inc(ix_tr, 1)
            act.wait_ge(pe_ix, 3)
            act.activation(kit, psum[:, 2, 0:T], ACT.Copy).then_inc(ix_tr, 1)
            for t in range(2):
                act.wait_ge(pe_sc, 2)
                act.wait_ge(d_iq, 2)
                act.activation(rel[:, NH * KOFF[t]:NH * (KOFF[t] + KEYS[t])].rearrange("p (h k) -> p h k", h=NH),
                               psum[:, :, KOFF[t]:KOFF[t] + KEYS[t]], ACT.Relu).then_inc(a_rel, 1)
            for c in range(5, N_IN):
                keep_z(c)
                split_w(c + 2)
            act.wait_ge(pe_y, 1)
            act.activation(yt, psum[:, 6:8, :].rearrange("p t (g q) -> p g t q", g=4), ACT.Copy).then_inc(y_ev, 1)
            act.wait_ge(d_p32, 1)
            act.activation(ht[:, 0, 4:8, :], p32, ACT.Copy).then_inc(pc_hi, 1)
            for t in range(2):
                act.wait_ge(pe_qk, t + 1)
                act.activation(qt[:, :, t * P:(t + 1) * P], psum[:, t, :].rearrange("p (a q) -> p a q", a=PAIRS),
                               ACT.Copy).then_inc(qk_tr, 1)
            for n, (t, first) in enumerate(((2, 0), (0, META), (1, META + P))):
                act.wait_ge(pe_qk, n + 3)
                r = rows[t]
                act.activation(kt[:, :, first:first + r], psum[:, 2 + n, 0:PAIRS * r].rearrange("p (a q) -> p a q", a=PAIRS),
                               ACT.Copy).then_inc(qk_tr, 1)
            for t in range(2):
                act.wait_ge(d_max, t + 1)
                for h in range(NH):
                    a = NH * KOFF[t] + h * KEYS[t]
                    act.activation(rel[:, a:a + KEYS[t]], rel[:, a:a + KEYS[t]], ACT.Exp,
                                   bias=stat[:, 128 + 8 * t + h:129 + 8 * t + h],
                                   accum_out=stat[:, 144 + 8 * t + h:145 + 8 * t + h]).then_inc(a_exp, 1)
            for n, (c, b, r) in enumerate(((0, 0, META), (1, 2, P), (2, 4, META), (3, 6, P), (4, 0, P))):
                act.wait_ge(pe_pt, n + 1)
                act.activation(pt[0:r, c].rearrange("p (b h) q -> p b (h q)", b=2), psum[0:r, b:b + 2, :],
                               ACT.Copy).then_inc(pt_ev, 1)
            for t in range(2):
                act.wait_ge(pe_cat, t + 1)
                act.activation(ht[:, 0, 0:4, t * P:(t + 1) * P], psum[:, 2 + t, :].rearrange("p (a q) -> p a q", a=PAIRS),
                               ACT.Copy).then_inc(cat_hi, 1)
            for c in range(OUT0 + 2, OUT0 + 6):
                split_w(c)
            for t in range(2):
                act.wait_ge(h_ev, 2 * N_OUT)
                act.activation(xs[:, t, :], xt[:, t, :], ACT.Square, accum_out=stat[:, 200 + t:201 + t]).then_inc(a_sq, 1)
            for t in range(2):
                act.wait_ge(p_rs, 5 + t + 1)
                act.wait_ge(a_sq, 3 + t + 1)
                act.activation(xs[:, t, :], xt[:, t, :], ACT.Copy, scale=scal[:, 48 + t:49 + t]).then_inc(a_xs, 1)
            act.wait_ge(pe_ks, 1)
            act.activation(kt_sub, psum[:, 5, 0:2 * P].rearrange("p (a n) -> p a n", a=2), ACT.Copy).then_inc(ks_ev, 1)
            for t in range(2):
                act.wait_ge(d_t32, 3 + t + 1)
                act.activation(ht[:, 0, :, t * P:(t + 1) * P], t32[:, :, t * P:(t + 1) * P], ACT.Copy).then_inc(a_hi, 1)

            def keep_s(h):
                act.wait_ge(pe_s, h + 1)
                act.activation(sc[:, h].rearrange("p t a n -> p (t a n)"), psum[:, 3 * ((WQ0 + h) % 2) + 1, :], ACT.Copy)\
                   .then_inc(s_ev, 1)

            for h in range(PH):
                act.wait_ge(z_done, z_after(WQ0 + h))
                if h >= 2:
                    act.wait_ge(pe_s, h - 1)
                act.activation(qp[:, h % 2].rearrange("p a t -> p (a t)"), psum[:, 3 * ((WQ0 + h) % 2), :], ACT.Copy)\
                   .then_inc(qp_ev, 1)
                if WQ0 + h + 2 < N_CHUNK:
                    split_w(WQ0 + h + 2)
                if h:
                    keep_s(h - 1)
            keep_s(PH - 1)
            act.wait_ge(d_sub, 1)
            act.activation(pick3[:, 2], pick3[:, 2], ACT.Exp).then_inc(a_soft, 1)
            act.wait_ge(pe_pk, 1)
            act.activation(picks[:, 0:2, :].rearrange("p a t -> p (a t)"), psum[:, 6, :], ACT.Copy).then_inc(pk_ev, 1)
            act.wait_ge(pe_pk, 2)
            act.activation(picks[:, 2, :], psum[:, 7, 0:SEQ], ACT.Copy).then_inc(pk_ev, 1)
            with act.Fori(0, SEQ // QUAD // 2) as i:
                for s in range(2):
                    act.wait_ge(b_done, 2 * i + (s + 1))
                    act.activation(gates[:, :, ds(8 * i + QUAD * s, QUAD)],
                                   psum[:, 2 + s, :].rearrange("p (q n) -> p n q", q=QUAD), ACT.Copy).then_inc(b_ev, 1)

            def block_u(s, b, first):
                act.wait_ge(t_done, b + 1)
                act.activation(ut[:, 0], psum[:, 0:2, :].rearrange("p b (k n) -> p (b k) n", n=P), ACT.Copy).then_inc(ut_hi, 1)

            def block_v(s, b, first):
                if not first:
                    act.wait_ge(c_done, b - 1)
                act.wait_ge(ld_v[s], v_turn(b, s))
                act.activation(v_sp[:, s, 0, :], v_raw[:, s, :], ACT.Copy).then_inc(v_hi, 1)

            def block_g(s, b, first):
                act.wait_ge(a_done, b + 1)
                if not first:
                    act.wait_ge(d_g32, b - 1)
                act.activation(gel[:, s, :], psum[:, 2 + s, 0:SEQ], ACT.Gelu).then_inc(a_gel, 1)

            def v_turn(b, s):
                return 8 * b + (16 - 8 * s)

            for b in range(2):
                block_u(b, b, True)
                block_v(b, b, True)
                block_g(b, b, True)
            with act.Fori(1, NK // 2) as i:
                for s in range(2):
                    block_u(s, 2 * i + s, False)
                    block_v(s, 2 * i + s, False)
                    block_g(s, 2 * i + s, False)

        @block.vector
        def _(dve):
            seq = Count()

            def split_lo(c):
                dve.wait_ge(w_hi, c + 1)
                n = w_cols(c)
                dve.tensor_tensor(w_sp[:, c % 2, 1, :, 0:n], wraw[:, c % 3, :, 0:n], f(w_sp[:, c % 2, 0, :, 0:n]), ALU.subtract)\
                   .then_inc(w_lo_e, 1)

            for t, r in enumerate(rows):
                dve.wait_ge(a_sq, t + 1)
                dve.tensor_scalar(scal[0:r, t:t + 1], stat[0:r, t:t + 1], 1.0 / D, EPS, ALU.mult, ALU.add).then_inc(d_ms, 1)
            split_lo(0)
            dve.wait_ge(pe_gain, 1)
            dve.tensor_copy(gains, psum[:, 5, 0:20]).then_inc(d_seq, 1)
            dve.wait_ge(d_seq, seq.up())
            gain = [gains[:, 0:8], gains[:, 8:16]]
            for t, r in enumerate(rows):
                dve.wait_ge(pe_x, t + 1)
                dst = t32[:, :, t * P:(t + 1) * P] if t < 2 else t32m
                src = (psum[:, 2 * t:2 * t + 2, :].rearrange("p b (k n) -> p (b k) n", n=P) if t < 2
                       else psum[:, 4, 0:DK * META].rearrange("p (k n) -> p k n", n=META))
                dve.tensor_tensor(dst, src, gain[0].unsqueeze(2).to_broadcast([P, DK, r]), ALU.mult).then_inc(d_t32, 1)
            for t in range(3):
                dve.wait_ge(d_t32, t + 1)
                dve.wait_ge(a_hi, t + 1)
                hi, lo, src = ((ht[:, 0, :, t * P:(t + 1) * P], ht[:, 1, :, t * P:(t + 1) * P], t32[:, :, t * P:(t + 1) * P])
                               if t < 2 else (hm[:, 0], hm[:, 1], t32m))
                dve.tensor_tensor(lo, src, f(hi), ALU.subtract).then_inc(d_lo, 1)
            split_lo(2)

            def rope(r, t, src, nh, dsts, done):
                s3 = src.rearrange("p (h d) -> p h d", h=nh)
                c3 = cos[0:r, trow[t], :].unsqueeze(1).to_broadcast([r, nh, HD])
                n3 = sin[0:r, trow[t], :].unsqueeze(1).to_broadcast([r, nh, HD])
                a3 = tmp[0:r, 0, 0:nh * HD].rearrange("p (h d) -> p h d", h=nh)
                b3 = tmp[0:r, 1, 0:nh * HD].rearrange("p (h d) -> p h d", h=nh)
                hh = HD // 2
                dve.tensor_tensor(a3, s3, c3, ALU.mult).then_inc(d_seq, 1)
                seq.up()
                dve.tensor_tensor(b3[:, :, 0:hh], s3[:, :, hh:HD], n3[:, :, 0:hh], ALU.mult).then_inc(d_seq, 1)
                seq.up()
                dve.tensor_tensor(b3[:, :, hh:HD], s3[:, :, 0:hh], n3[:, :, hh:HD], ALU.mult).then_inc(d_seq, 1)
                dve.wait_ge(d_seq, seq.up())
                for d in dsts:
                    dve.tensor_tensor(d.rearrange("p (h d) -> p h d", h=nh), a3, b3, ALU.add).then_inc(done, 1)

            dve.wait_ge(ld_rope, 16)
            dve.wait_ge(z_ev, 3)
            for n, t in enumerate((0, 1, 2)):
                r = rows[t]
                rope(r, t, zi[0:r, t, 0:HD], 1, [kir[0:r, t, 0:HD], kir[0:r, t, HD:P]], d_ki)
                dve.wait_ge(d_ki, 2 * n + 2)
            dve.tensor_scalar(scal[:, 16:32].rearrange("p (t h) -> p t h", t=2), zi[:, 0:2, HD:CI],
                              NH ** -0.5 * HD ** -0.5, None, ALU.mult).then_inc(d_seq, 1)
            seq.up()
            split_lo(4)
            dve.wait_ge(z_ev, z_after(2))
            for t in range(2):
                rope(P, t, ziq[:, t, :], NH, [iqr[:, t, :]], d_iq)
                dve.wait_ge(d_iq, t + 1)

            def head_means(t, src, at0, done):
                r = rows[t]
                dve.tensor_tensor(tmp[0:r, 2, :], src, src, ALU.mult).then_inc(d_seq, 1)
                dve.wait_ge(d_seq, seq.up())
                dve.tensor_reduce(stat[0:r, at0:at0 + 8], tmp[0:r, 2, :].rearrange("p (h d) -> p h d", h=NH), AX.X, ALU.add)\
                   .then_inc(d_seq, 1)
                dve.wait_ge(d_seq, seq.up())
                dve.tensor_scalar(stat[0:r, at0:at0 + 8], stat[0:r, at0:at0 + 8], 1.0 / HD, EPS, ALU.mult, ALU.add)\
                   .then_inc(done, 1)

            dve.wait_ge(z_ev, z_after(4))
            for t in range(2):
                head_means(t, zq[:, t, :], 32 + 8 * t, d_qst)
            split_lo(6)
            for t in range(2):
                dve.wait_ge(a_rel, t + 1)
                k = KEYS[t]
                acc = score[:, KOFF[t]:KOFF[t] + k]
                for h in range(NH):
                    part = rel[:, NH * KOFF[t] + h * k:NH * KOFF[t] + (h + 1) * k]
                    w = scal[:, 16 + 8 * t + h:17 + 8 * t + h]
                    if h == 0:
                        dve.tensor_scalar(acc, part, w, None, ALU.mult).then_inc(d_seq, 1)
                    else:
                        dve.scalar_tensor_tensor(acc, part, w, acc, ALU.mult, ALU.add).then_inc(d_seq, 1)
                    dve.wait_ge(d_seq, seq.up())
                dve.memset(acc[0:KSEL, k - 64:k], NEG).then_inc(d_seq, 1)
                dve.wait_ge(d_seq, seq.up())

            def keep_top(t):
                k = KEYS[t]
                a, w, b = (m[:, KOFF[t]:KOFF[t] + k] for m in (score, work, bias))
                for n in range(KSEL // 8):
                    src = a if n == 0 else w
                    dve.max(top8, src).then_inc(d_seq, 1)
                    dve.wait_ge(d_seq, seq.up())
                    dve.match_replace(w, top8, src, NEG).then_inc(d_seq, 1)
                    dve.wait_ge(d_seq, seq.up())
                dve.tensor_tensor(b, w, a, ALU.is_equal).then_inc(d_seq, 1)
                dve.wait_ge(d_seq, seq.up())
                dve.tensor_scalar(b, b, -1.0e30, None, ALU.mult).then_inc(d_seq, 1)
                dve.wait_ge(d_seq, seq.up())

            keep_top(0)
            split_lo(8)
            dve.wait_ge(z_ev, z_after(6))
            for t in range(3):
                head_means(t, zk[0:rows[t], t, :], 48 + 8 * t, d_kst)
            keep_top(1)

            def norm_rope(t, src, gi, at0, dst):
                r = rows[t]
                m = tmp[0:r, 2, :]
                m3 = m.rearrange("p (h d) -> p h d", h=NH)
                dve.tensor_tensor(m3, src.rearrange("p (h d) -> p h d", h=NH),
                                  stat[0:r, at0:at0 + 8].unsqueeze(2).to_broadcast([r, NH, HD]), ALU.mult).then_inc(d_seq, 1)
                dve.wait_ge(d_seq, seq.up())
                dve.tensor_tensor(m3, m3, gqk[0:r, gi, :].unsqueeze(1).to_broadcast([r, NH, HD]), ALU.mult).then_inc(d_seq, 1)
                dve.wait_ge(d_seq, seq.up())
                rope(r, t, m, NH, [dst], d_qk)

            dve.wait_ge(p_rs, 4)
            for t in range(2):
                norm_rope(t, zq[:, t, :], 0, 80 + 8 * t, qr[:, t, :])
                dve.wait_ge(d_qk, t + 1)
            split_lo(10)
            dve.wait_ge(p_rs, 5)
            for n, t in enumerate((2, 0, 1)):
                r = rows[t]
                norm_rope(t, zk[0:r, t, :], 1, 96 + 8 * t, kr[0:r, t, :])
                dve.wait_ge(d_qk, 3 + n)
            split_lo(12)
            dve.wait_ge(pe_y, 2)
            dve.tensor_tensor(p32, psum[:, 6:8, :].rearrange("p b (g t) -> p (b g) t", t=SEQ),
                              gains[:, 16:20].unsqueeze(2).to_broadcast([P, 4, SEQ]), ALU.mult).then_inc(d_p32, 1)
            dve.wait_ge(pc_hi, 1)
            dve.tensor_tensor(ht[:, 1, 4:8, :], p32, f(ht[:, 0, 4:8, :]), ALU.subtract).then_inc(pc_lo, 1)
            for t in range(2):
                k = KEYS[t]
                lg = rel[:, NH * KOFF[t]:NH * (KOFF[t] + k)].rearrange("p (h k) -> p h k", h=NH)
                dve.wait_ge(pe_log, 2)
                dve.scalar_tensor_tensor(lg, psum[:, :, KOFF[t]:KOFF[t] + k], HD ** -0.5,
                                         bias[:, KOFF[t]:KOFF[t] + k].unsqueeze(1).to_broadcast([P, NH, k]),
                                         ALU.mult, ALU.add).then_inc(d_log, 1)
                dve.wait_ge(d_log, t + 1)
                dve.tensor_reduce(stat[:, 128 + 8 * t:136 + 8 * t], lg, AX.X, ALU.max, negate=True).then_inc(d_max, 1)
            for t in range(2):
                k = KEYS[t]
                lg = rel[:, NH * KOFF[t]:NH * (KOFF[t] + k)].rearrange("p (h k) -> p h k", h=NH)
                dve.wait_ge(a_exp, NH * (t + 1))
                dve.reciprocal(stat[:, 160 + 8 * t:168 + 8 * t], stat[:, 144 + 8 * t:152 + 8 * t]).then_inc(d_seq, 1)
                dve.wait_ge(d_seq, seq.up())
                dve.tensor_tensor(lg, lg, stat[:, 160 + 8 * t:168 + 8 * t].unsqueeze(2).to_broadcast([P, NH, k]), ALU.mult)\
                   .then_inc(d_prob, 1)
            for t in range(2):
                dve.wait_ge(cat_hi, t + 1)
                dve.tensor_tensor(ht[:, 1, 0:4, t * P:(t + 1) * P], psum[:, 2 + t, :].rearrange("p (a q) -> p a q", a=PAIRS),
                                  f(ht[:, 0, 0:4, t * P:(t + 1) * P]), ALU.subtract).then_inc(cat_lo, 1)
            for c in range(OUT0, WQ0):
                for t in range(2):
                    dve.wait_ge(z_done, z_after(c) - 1 + t)
                    n = (c - OUT0) * CW
                    dve.tensor_tensor(xt[:, t, n:n + CW], xt[:, t, n:n + CW], psum[:, 3 * (c % 2) + t, 0:CW], ALU.add)\
                       .then_inc(h_ev, 1)
                if c % 2 == 0:
                    split_lo(c + 2)
            for t in range(2):
                dve.wait_ge(a_sq, 3 + t + 1)
                dve.tensor_scalar(scal[:, 3 + t:4 + t], stat[:, 200 + t:201 + t], 1.0 / D, EPS, ALU.mult, ALU.add)\
                   .then_inc(d_ms, 1)
            for t, b in enumerate((6, 0)):
                dve.wait_ge(pe_x, 3 + t + 1)
                dve.tensor_tensor(t32[:, :, t * P:(t + 1) * P], psum[:, b:b + 2, :].rearrange("p b (k n) -> p (b k) n", n=P),
                                  gain[1].unsqueeze(2).to_broadcast([P, DK, P]), ALU.mult).then_inc(d_t32, 1)
            for t in range(2):
                dve.wait_ge(a_hi, 3 + t + 1)
                dve.tensor_tensor(ht[:, 1, :, t * P:(t + 1) * P], t32[:, :, t * P:(t + 1) * P],
                                  f(ht[:, 0, :, t * P:(t + 1) * P]), ALU.subtract).then_inc(d_lo, 1)

            def top16(parts):
                for n in range(2):
                    at = slice(8 * n, 8 * n + 8)
                    n0 = seq.n
                    for k, (vals, idx, src) in enumerate(parts):
                        if n:
                            dve.wait_ge(d_seq, n0 - len(parts) + k + 1)
                        dve.max(vals[:, at], src).then_inc(d_seq, 1)
                        seq.up()
                    for k, (vals, idx, src) in enumerate(parts):
                        dve.wait_ge(d_seq, n0 + k + 1)
                        dve.max_index(idx[:, at], vals[:, at], src).then_inc(d_seq, 1)
                        seq.up()
                    for k, (vals, idx, src) in enumerate(parts if n == 0 else []):
                        dve.wait_ge(d_seq, n0 + len(parts) + k + 1)
                        dve.match_replace(src, vals[:, at], src, NEG).then_inc(d_seq, 1)
                        seq.up()

            def pick(h):
                dve.wait_ge(s_ev, h + 1)
                top16([(v16[:, h, t, a, :], i16[:, h, t, a, :], sc[:, h, t, a, :]) for t in range(2) for a in range(2)])
                dve.wait_ge(d_seq, seq.n)
                dve.tensor_copy(n16[:, h], i16[:, h]).then_inc(d_top, 1)
                for first, nr, ncol, o in STAIRS:
                    dve.tensor_tensor(cand[:, h, :, o:o + nr * ncol].rearrange("p t (i j) -> p t i j", i=nr),
                                      v16[:, h, :, 0, first:first + nr].unsqueeze(3).to_broadcast([P, 2, nr, ncol]),
                                      v16[:, h, :, 1, 0:ncol].unsqueeze(2).to_broadcast([P, 2, nr, ncol]), ALU.add)\
                       .then_inc(d_seq, 1)
                    seq.up()
                dve.wait_ge(d_seq, seq.n)
                top16([(vtop[:, t, h, :], ptop[:, t, h, :], cand[:, h, t, :]) for t in range(2)])
                dve.wait_ge(d_seq, seq.n)
                dve.tensor_copy(ntop[:, :, h, :], ptop[:, :, h, :]).then_inc(d_seq, 1)
                dve.wait_ge(d_seq, seq.up())
                if h >= 2:
                    dve.wait_ge(d_pick, h - 1)
                for t in range(2):
                    i = dve.tensor_tensor(eqs[:, h % 2, t], iota[:, 0:NCAND].unsqueeze(1).to_broadcast([P, TOPK, NCAND]),
                                          ntop[:, t, h, :].unsqueeze(2).to_broadcast([P, TOPK, NCAND]), ALU.is_equal)
                i.then_inc(d_match, 1)

            def look_up(h):
                dve.wait_ge(p_eq, h + 1)
                dve.tensor_reduce(eid[:, :, h, :], eqs[:, h % 2], AX.X, ALU.add).then_inc(d_pick, 1)

            for h in range(PH):
                if h in (0, 2, 4):
                    split_lo(WQ0 + 3 + h)
                pick(h)
                if h:
                    look_up(h - 1)
            dve.tensor_tensor(pick3[:, 2], vtop, vtop[:, :, :, 0:1].to_broadcast([P, 2, PH, TOPK]), ALU.subtract).then_inc(d_sub, 1)
            look_up(PH - 1)
            dve.wait_ge(d_pick, PH)
            dve.tensor_copy(eint, eid).then_inc(d_seq, 1)
            dve.wait_ge(d_seq, seq.up())
            dve.tensor_scalar(fint, eint, 7, None, ALU.logical_shift_right).then_inc(d_seq, 1)
            dve.wait_ge(d_seq, seq.up())
            dve.tensor_copy(pick3[:, 0], fint).then_inc(d_seq, 1)
            dve.wait_ge(d_seq, seq.up())
            dve.tensor_scalar(fint, eint, NK - 1, None, ALU.bitwise_and).then_inc(d_seq, 1)
            dve.wait_ge(d_seq, seq.up())
            dve.tensor_copy(pick3[:, 1], fint).then_inc(d_seq, 1)
            dve.wait_ge(a_soft, 1)
            seq.up()
            dve.tensor_reduce(scal[:, 0:16].rearrange("p (t h) -> p t h", t=2), pick3[:, 2], AX.X, ALU.add).then_inc(d_seq, 1)
            dve.wait_ge(d_seq, seq.up())
            dve.reciprocal(scal[:, 0:16], scal[:, 0:16]).then_inc(d_seq, 1)
            dve.wait_ge(d_seq, seq.up())
            dve.tensor_tensor(pick3[:, 2], pick3[:, 2],
                              scal[:, 0:16].rearrange("p (t h) -> p t h", t=2).unsqueeze(3).to_broadcast([P, 2, PH, TOPK]),
                              ALU.mult).then_inc(d_pick, 1)

            def ones(s, tok):
                for j in range(QUAD):
                    i = dve.tensor_scalar(oh1[:, s, j, :], iota, picks[:, 0, ds(tok + j, 1)], None, ALU.is_equal)
                i.then_inc(oh1_up, 1)
                for j in range(QUAD):
                    i = dve.tensor_scalar(oh2[:, s, j, :], iota, picks[:, 1, ds(tok + j, 1)], picks[:, 2, ds(tok + j, 1)],
                                          ALU.is_equal, ALU.mult)
                i.then_inc(oh2_up, 1)

            dve.wait_ge(pk_ev, 2)
            for s in range(2):
                ones(s, QUAD * s)
            with dve.Fori(0, SEQ // QUAD // 2 - 1) as i:
                for s in range(2):
                    dve.wait_ge(b_done, 2 * i + (s + 1))
                    ones(s, 8 * i + (8 + QUAD * s))

            def block_u(s, b):
                dve.wait_ge(ut_hi, b + 1)
                dve.tensor_tensor(ut[:, 1], psum[:, 0:2, :].rearrange("p b (k n) -> p (b k) n", n=P), f(ut[:, 0]), ALU.subtract)\
                   .then_inc(ut_lo, 1)

            def block_v(s, b):
                dve.wait_ge(v_hi, b + 1)
                dve.tensor_tensor(v_sp[:, s, 1, :], v_raw[:, s, :], f(v_sp[:, s, 0, :]), ALU.subtract).then_inc(v_lo, 1)

            def block_g(s, b, first):
                dve.wait_ge(a_gel, b + 1)
                act_in = gel[:, s, :]
                dve.tensor_tensor(gates_at(b), gates_at(b), act_in, ALU.mult).then_inc(d_g32, 1)
                dve.wait_ge(d_g32, b + 1)
                if not first:
                    dve.wait_ge(c_done, b - 1)
                dve.tensor_scalar(g_sp[:, s, 0, :], gates_at(b), 1.0, None, ALU.mult).then_inc(d_seq, 1)
                dve.wait_ge(d_seq, b + (seq.n + 1))
                dve.tensor_tensor(g_sp[:, s, 1, :], gates_at(b), f(g_sp[:, s, 0, :]), ALU.subtract).then_inc(g_lo, 1)

            def gates_at(b):
                return big[:, ds(b * SEQ, SEQ)]

            dve.wait_ge(b_ev, SEQ // QUAD)
            for b in range(2):
                block_u(b, b)
                block_v(b, b)
                block_g(b, b, True)
            with dve.Fori(1, NK // 2) as i:
                for s in range(2):
                    block_u(s, 2 * i + s)
                    block_v(s, 2 * i + s)
                    block_g(s, 2 * i + s, False)
            dve.wait_ge(c_done, NK)
            dve.wait_ge(ld_h, 32)
            dve.wait_ge(g_lo, NK)
            for t in range(2):
                for n in range(2):
                    a = t * D + n * 512
                    dve.tensor_tensor(big[:, a:a + 512], raw[:, a:a + 512], psum[:, 4 + 2 * t + n, :], ALU.add).then_inc(d_out, 1)

        @block.gpsimd
        def _(pool):
            seq = Count()
            pool.memset(half, -0.5).then_inc(p_half, 1)
            pool.wait_ge(p_half, 1)

            def rsqrt(dst, src, r, n):
                pool.tensor_tensor(dst, src, half[0:r, :].to_broadcast([r, n]), ALU.pow).then_inc(p_rs, 1)

            def split_lo(c):
                pool.wait_ge(w_hi, c + 1)
                pool.tensor_tensor(w_sp[:, c % 2, 1], wraw[:, c % 3], f(w_sp[:, c % 2, 0]), ALU.subtract).then_inc(w_lo_o, 1)

            for t, r in enumerate(rows):
                pool.wait_ge(d_ms, t + 1)
                rsqrt(scal[0:r, 8 + t:9 + t], scal[0:r, t:t + 1], r, 1)
            split_lo(1)
            split_lo(3)
            split_lo(5)
            pool.wait_ge(d_qst, 2)
            rsqrt(stat[:, 80:96], stat[:, 32:48], P, 16)
            split_lo(7)
            pool.wait_ge(d_kst, 3)
            pool.tensor_tensor(stat[0:META, 112:120], stat[0:META, 64:72], half[0:META, :].to_broadcast([META, 8]), ALU.pow)\
                .then_inc(p_seq, 1)
            pool.wait_ge(p_seq, seq.up())
            rsqrt(stat[:, 96:112], stat[:, 48:64], P, 16)
            split_lo(9)
            split_lo(11)
            split_lo(13)
            split_lo(15)
            for t in range(2):
                pool.wait_ge(d_ms, 3 + t + 1)
                rsqrt(scal[:, 48 + t:49 + t], scal[:, 3 + t:4 + t], P, 1)

            def candidates(h):
                pool.wait_ge(d_top, h + 1)
                pool.tensor_scalar(n16[:, h, :, 0, :], n16[:, h, :, 0, :], float(NK), None, ALU.mult).then_inc(p_seq, 1)
                pool.wait_ge(p_seq, seq.up())
                for first, nr, ncol, o in STAIRS:
                    for t in range(2):
                        pool.tensor_tensor(cide[:, h, t, o:o + nr * ncol].rearrange("p (i j) -> p i j", i=nr),
                                           n16[:, h, t, 0, first:first + nr].unsqueeze(2).to_broadcast([P, nr, ncol]),
                                           n16[:, h, t, 1, 0:ncol].unsqueeze(1).to_broadcast([P, nr, ncol]), ALU.add)\
                            .then_inc(p_seq, 1)
                        seq.up()
                pool.wait_ge(p_seq, seq.n)
                pool.wait_ge(d_match, h + 1)
                for t in range(2):
                    i = pool.tensor_tensor(eqs[:, h % 2, t], eqs[:, h % 2, t],
                                           cide[:, h, t, :].unsqueeze(1).to_broadcast([P, TOPK, NCAND]), ALU.mult)
                i.then_inc(p_eq, 1)

            for h in range(PH):
                if h % 2 == 0 and WQ0 + 2 + h < N_CHUNK:
                    split_lo(WQ0 + 2 + h)
                candidates(h)

        @block.tensor
        def _(pe):
            def transpose8(t, banks, r):
                flat = psum[:, banks[0]:banks[-1] + 1, :].rearrange("p b n -> p (b n)")
                for k in range(DK):
                    i = pe.transpose(flat[:, k * r:(k + 1) * r], xs[0:r, t, k * P:(k + 1) * P], ident[0:r, 0:r])
                i.then_inc(pe_x, 1)

            def product(dst, lhs, rhs, sem_):
                n = 0
                for k in range(DK):
                    for a, b in ((0, 0), (0, 1), (1, 0)):
                        i = pe.matmul(dst, lhs(a, k), rhs(b, k), start=(n == 0), stop=(n == 3 * DK - 1))
                        n += 1
                i.then_inc(sem_, 1)

            def tokens(a, k, t):
                return ht[:, a, k, t * P:(t + 1) * P] if t < 2 else hm[:, a, k, :]

            def project(s, nt, n):
                for t in range(nt):
                    product(psum[0:rows[t], 3 * s + t, 0:n], lambda a, k: tokens(a, k, t), lambda b, k: w_sp[:, s, b, k, 0:n], z_done)

            pe.wait_ge(ld_cst, 16)
            pe.wait_ge(ld_small, 80)
            pe.transpose(psum[:, 5, 0:20], grow[0:20, :], ident[0:20, 0:20]).then_inc(pe_gain, 1)
            for t, b in enumerate(([0, 1], [2, 3], [4])):
                pe.wait_ge(a_xs, t + 1)
                transpose8(t, b, rows[t])
            pe.wait_ge(d_lo, 3)
            lo_ready(pe, 0)
            project(0, 3, CI)
            with pe.Fori(0, 2) as i:
                pe.wait_ge(w_lo_o, i + 1)
                pe.wait_ge(z_ev, 4 * i + 1)
                project(1, 2, CW)
                pe.wait_ge(w_lo_e, i + 2)
                pe.wait_ge(z_ev, 4 * i + 3)
                project(0, 2, CW)
            pe.wait_ge(z_ev, z_after(4))
            for t in range(2):
                pe.wait_ge(d_iq, t + 1)
                for a in range(PAIRS):
                    i = pe.transpose(psum[:, t, a * P:(a + 1) * P], iqr[:, t, a * P:(a + 1) * P], ident)
                i.then_inc(pe_ix, 1)
            pe.wait_ge(d_ki, 6)
            for t, first in ((2, 0), (0, META), (1, META + P)):
                r = rows[t]
                i = pe.transpose(psum[:, 2, first:first + r], kir[0:r, t, :], ident[0:r, 0:r])
            i.then_inc(pe_ix, 1)
            pe.wait_ge(ix_tr, 3)
            for t in range(2):
                for h in range(NH):
                    lo = HD * (h % 2)
                    i = pe.matmul(psum[:, h, KOFF[t]:KOFF[t] + KEYS[t]], iqt[lo:lo + HD, h // 2, t * P:(t + 1) * P],
                                  kit[lo:lo + HD, 0:KEYS[t]], start=True, stop=True)
                i.then_inc(pe_sc, 1)
            pe.wait_ge(a_rel, 2)
            with pe.Fori(0, 3) as i:
                pe.wait_ge(w_lo_o, i + 3)
                pe.wait_ge(z_ev, 6 * i + z_after(3))
                project(1, 3, CW)
                pe.wait_ge(w_lo_e, i + 4)
                pe.wait_ge(z_ev, 6 * i + z_after(4))
                project(0, 3, CW)
            pe.wait_ge(z_ev, z_after(N_IN - 1))
            pe.wait_ge(ld_band, 32)
            for t in range(2):
                for g in range(4):
                    dst = psum[:, 6 + t, g * P:(g + 1) * P]
                    gs = slice(g * P, (g + 1) * P)
                    pe.matmul(dst, zp[:, t, gs], band[:, 0, g, :], start=True, stop=False)
                    i = (pe.matmul(dst, zp[0:META, 2, gs], band[0:META, 2, g, :], start=False, stop=True) if t == 0
                         else pe.matmul(dst, zp[:, 0, gs], band[:, 1, g, :], start=False, stop=True))
            i.then_inc(pe_y, 1)
            pe.wait_ge(y_ev, 1)
            for g in range(4):
                i = pe.matmul(psum[:, 6 + g // 2, (g % 2) * SEQ:(g % 2 + 1) * SEQ], poolw[:, g, :], yt[:, g, :], start=True, stop=True)
            i.then_inc(pe_y, 1)
            for t in range(2):
                pe.wait_ge(d_qk, t + 1)
                for a in range(PAIRS):
                    i = pe.transpose(psum[:, t, a * P:(a + 1) * P], qr[:, t, a * P:(a + 1) * P], ident)
                i.then_inc(pe_qk, 1)
            for n, t in enumerate((2, 0, 1)):
                pe.wait_ge(d_qk, 3 + n)
                r = rows[t]
                for a in range(PAIRS):
                    i = pe.transpose(psum[:, 2 + n, a * r:(a + 1) * r], kr[0:r, t, a * P:(a + 1) * P], ident[0:r, 0:r])
                i.then_inc(pe_qk, 1)
            pe.wait_ge(qk_tr, 5)
            pe.wait_ge(d_p32, 1)
            for t in range(2):
                for h in range(NH):
                    lo = HD * (h % 2)
                    i = pe.matmul(psum[:, h, KOFF[t]:KOFF[t] + KEYS[t]], qt[lo:lo + HD, h // 2, t * P:(t + 1) * P],
                                  kt[lo:lo + HD, h // 2, 0:KEYS[t]], start=True, stop=True)
                i.then_inc(pe_log, 1)
            pe.wait_ge(d_log, 2)
            for n, (t, r, first, b) in enumerate(((0, META, 0, 0), (0, P, META, 2), (1, META, 0, 4), (1, P, META, 6),
                                                  (1, P, META + P, 0))):
                pe.wait_ge(d_prob, t + 1)
                if n == 4:
                    pe.wait_ge(pt_ev, 1)
                for h in range(NH):
                    a = NH * KOFF[t] + h * KEYS[t] + first
                    i = pe.transpose(psum[0:r, b + h // 4, (h % 4) * P:(h % 4 + 1) * P], rel[:, a:a + r], ident)
                i.then_inc(pe_pt, 1)
            for t in range(2):
                chunks = ((0, 2, META), (1, 0, P)) if t == 0 else ((2, 2, META), (3, 0, P), (4, 1, P))
                pe.wait_ge(pt_ev, 2 if t == 0 else 5)
                for h in range(NH):
                    lo = HD * (h % 2)
                    for n, (c, vt, r) in enumerate(chunks):
                        i = pe.matmul(psum[lo:lo + HD, 2 + t, (h // 2) * P:(h // 2 + 1) * P], zv[0:r, vt, h * HD:(h + 1) * HD],
                                      pt[0:r, c, h, :], start=(n == 0), stop=(n == len(chunks) - 1))
                i.then_inc(pe_cat, 1)
            pe.wait_ge(cat_lo, 2)
            pe.wait_ge(pc_lo, 1)
            for c in range(OUT0, WQ0):
                lo_ready(pe, c)
                if c >= OUT0 + 2:
                    pe.wait_ge(h_ev, 2 * (c - OUT0 - 1))
                project(c % 2, 2, CW)
            pe.wait_ge(ld_g2, 32)
            for a in range(2):
                i = pe.transpose(psum[:, 5, a * P:(a + 1) * P], ksub[:, a, :], ident)
            i.then_inc(pe_ks, 1)
            pe.wait_ge(h_ev, 2 * N_OUT)
            for t, b in enumerate(([6, 7], [0, 1])):
                pe.wait_ge(a_xs, 3 + t + 1)
                transpose8(t, b, P)
            pe.wait_ge(d_lo, 5)
            pe.wait_ge(ks_ev, 1)

            def queries(s):
                for a in range(2):
                    n = 0
                    for k in range(DK):
                        for u, w in ((0, 0), (0, 1), (1, 0)):
                            i = pe.matmul(psum[:, 3 * s, a * SEQ:(a + 1) * SEQ], w_sp[:, s, u, k, a * P:(a + 1) * P],
                                          ht[:, w, k, :], start=(n == 0), stop=(n == 3 * DK - 1))
                            n += 1
                i.then_inc(z_done, 1)

            def sub_scores(s, q):
                for t in range(2):
                    for a in range(2):
                        i = pe.matmul(psum[:, 3 * s + 1, (2 * t + a) * P:(2 * t + a + 1) * P], qp[:, q, a, t * P:(t + 1) * P],
                                      kt_sub[:, a, :], start=True, stop=True)
                i.then_inc(pe_s, 1)

            for h in range(PH + 1):
                c = WQ0 + h
                if h < PH:
                    lo_ready(pe, c)
                    if h >= 2:
                        pe.wait_ge(qp_ev, h - 1)
                    queries(c % 2)
                if h:
                    pe.wait_ge(qp_ev, h)
                    if h >= 3:
                        pe.wait_ge(s_ev, h - 2)
                    sub_scores((c - 1) % 2, (h - 1) % 2)
            pe.wait_ge(d_pick, PH + 1)
            for a in range(3):
                for t in range(2):
                    i = pe.transpose(psum[:, 6 + a // 2, (a % 2) * SEQ + t * P:(a % 2) * SEQ + (t + 1) * P],
                                     pick3[:, a, t].rearrange("p h k -> p (h k)"), ident)
                if a:
                    i.then_inc(pe_pk, 1)

            def gate4(s):
                for j in range(QUAD):
                    i = pe.matmul(psum[:, 2 + s, j * P:(j + 1) * P], oh1[:, s, j, :], oh2[:, s, j, :], start=True, stop=True)
                i.then_inc(b_done, 1)

            for s in range(2):
                pe.wait_ge(oh1_up, s + 1)
                pe.wait_ge(oh2_up, s + 1)
                gate4(s)
            with pe.Fori(0, SEQ // QUAD // 2 - 1) as i:
                for s in range(2):
                    pe.wait_ge(oh1_up, 2 * i + (s + 3))
                    pe.wait_ge(oh2_up, 2 * i + (s + 3))
                    pe.wait_ge(b_ev, 2 * i + (s + 1))
                    gate4(s)

            def turn_u(s, landed):
                pe.wait_ge(ld_u[s], landed)
                for k in range(DK):
                    i = pe.transpose(psum[:, k // 4, (k % 4) * P:(k % 4 + 1) * P], u_raw[:, s, k, :], ident)
                i.then_inc(t_done, 1)

            def up(s):
                product(psum[:, 2 + s, 0:SEQ], lambda a, k: ut[:, a, k, :], lambda b, k: ht[:, b, k, :], a_done)

            def down(s, first, last):
                for t in range(2):
                    for n in range(2):
                        for m, (a, b) in enumerate(((0, 0), (0, 1), (1, 0))):
                            i = pe.matmul(psum[:, 4 + 2 * t + n, :], g_sp[:, s, a, t * P:(t + 1) * P],
                                          v_sp[:, s, b, n * 512:(n + 1) * 512], start=(first and m == 0), stop=(last and m == 2))
                i.then_inc(c_done, 1)

            def turn(b, s, first, last, more=True):
                if more:
                    pe.wait_ge(ut_lo, b + 1)
                    turn_u(1 - s, 8 * b + 16 + 8 * s)
                pe.wait_ge(g_lo, b)
                pe.wait_ge(v_lo, b)
                down(1 - s, first, last)
                if more:
                    pe.wait_ge(ut_lo, b + 2)
                    pe.wait_ge(a_gel, b)
                    up(1 - s)

            for b in range(2):
                if b:
                    pe.wait_ge(ut_lo, 1)
                turn_u(b, 16)
                pe.wait_ge(ut_lo, b + 1)
                if b == 0:
                    pe.wait_ge(b_ev, SEQ // QUAD)
                up(b)
            turn(1, 1, True, False)
            turn(2, 0, False, False)
            with pe.Fori(1, NK // 2 - 1) as i:
                turn(2 * i + 1, 1, False, False)
                turn(2 * i + 2, 0, False, False)
            turn(NK - 1, 1, False, False, more=False)
            turn(NK, 0, False, True, more=False)


_INS = ['x', 'meta_tokens', 'norm1_g', 'w_in', 'q_norm_g', 'k_norm_g', 'pool_w', 'pool_scale', 'w_out', 'norm2_g',
        'peer_wq', 'sub_keys1', 'sub_keys2', 'peer_u', 'peer_v']


def constants():
    import numpy as np
    c = np.zeros((P, N_CONST), np.float32)
    c[:, K_ID:K_ID + P] = np.eye(P)
    c[:, K_IOTA:K_IOTA + P] = np.arange(P)
    inv = (np.float32(10000.0) ** (-np.arange(0, HD, 2, dtype=np.float32) / np.float32(HD))).astype(np.float32)
    ang = (np.arange(T, dtype=np.float32)[:, None] * inv[None, :]).astype(np.float32)
    cs = np.cos(ang.astype(np.float64)).astype(np.float32)
    sn = np.sin(ang.astype(np.float64)).astype(np.float32)
    for n, (first, r) in enumerate(((0, META), (META, P), (META + P, P))):
        for at, a, b in ((K_COS, cs, cs), (K_SIN, -sn, sn)):
            c[0:r, at + n * HD:at + n * HD + HD // 2] = a[first:first + r]
            c[0:r, at + n * HD + HD // 2:at + (n + 1) * HD] = b[first:first + r]
    band = np.zeros((P, 3, 4, P), np.float32)
    for g, w in enumerate((2, 4, 8, 16)):
        for t in range(P):
            for s in range(t - w + 1, t + 1):
                if s >= 0:
                    band[s, 0, g, t] += 1.0 / w
                else:
                    band[P + s, 1, g, t] += 1.0 / w
                    band[META + s, 2, g, t] += 1.0 / w
            band[t, 0, g, t] -= 1.0
    c[:, K_BAND:] = band.reshape(P, -1)
    return c


def kernel(**inputs):
    import numpy as _np
    import concourse.bacc as _bacc
    from concourse import mybir as _mybir
    from concourse.bass_utils import run_bass_kernel_spmd as _run

    nc = _bacc.Bacc("TRN2", target_bir_lowering=False, num_devices=1)
    arrays, args = {}, []
    for name in _INS + ["const"]:
        a = constants() if name == "const" else _np.ascontiguousarray(inputs[name])
        arrays[f"in_{name}_dram"] = a
        args.append(nc.dram_tensor(f"in_{name}_dram", a.shape, _mybir.dt.from_np(a.dtype), kind="ExternalInput").ap())
    args.append(nc.dram_tensor("out_0_dram", (1, SEQ, D), _mybir.dt.float32, kind="ExternalOutput").ap())
    layer(nc, *args)
    r = _run(nc, [arrays], core_ids=[0])
    return r.results[0]["out_0_dram"]
```

```python
import concourse.bass as bass
from concourse import mybir
from contextlib import ExitStack

F32 = mybir.dt.float32
F32R = mybir.dt.float32r
U32 = mybir.dt.uint32
ALU = mybir.AluOpType
ACT = mybir.ActivationFunctionType
AX = mybir.AxisListType
ds = bass.ds

P = 128
SEQ, META = 256, 16
T = SEQ + META
D = 1024
DK = D // P
HD, NH = 64, 8
PAIRS = NH // 2
KSEL = 64
EPS = 1e-6
NEG = -3.0e38
NK = 128
PH, TOPK = 8, 16
GRP = 8
NQ, OHS = SEQ // GRP, 3
Q_LAST = NQ // OHS * OHS
ACT_T = 4
CW = 256

KEYS = [META + P, META + 2 * P]
KOFF = [0, KEYS[0]]
KALL = KEYS[0] + KEYS[1]

STAIRS, off = [], 0
for first, rows in ((0, 1), (1, 1), (2, 1), (3, 1), (4, 1), (5, 3), (8, 8)):
    cols = TOPK // (first + 1)
    STAIRS.append((first, rows, cols, off))
    off += rows * cols
NCAND = off

C_Q, C_K, C_V, C_POOL, C_IQ, C_IK = 0, 512, 1024, 1536, 2048, 2560
CI = HD + NH
W_IN = [C_IK, C_IQ, C_IQ + CW, C_Q, C_Q + CW, C_K, C_K + CW, C_V, C_V + CW, C_POOL, C_POOL + CW]
N_IN, N_OUT, N_WQ = len(W_IN), D // CW, PH
N_CHUNK = N_IN + N_OUT + N_WQ
OUT0, WQ0 = N_IN, N_IN + N_OUT
LO_ALL = WQ0 + 4
K_ID, K_IOTA, K_COS, K_SIN, K_BAND = 0, 128, 256, 448, 640
N_CONST = K_BAND + 3 * 4 * P


def by_vector(c):
    return c in (9, 13) or c % 2 == 0 and c < LO_ALL


def chunk_tiles(c):
    return (3 if c == 0 or 5 <= c < N_IN else 2) if c < WQ0 else 1


def z_after(c):
    return sum(chunk_tiles(k) for k in range(c + 1))


class Count:

    def __init__(self):
        self.n = 0

    def up(self):
        self.n += 1
        return self.n


def layer(nc, x, meta, g1, w_in, gq, gk, pool_w, pool_s, w_out, g2, wq, sk1, sk2, pu, pv, const, out):
    ctx = ExitStack()
    with ctx:
        def sb(name, shape, dt=F32):
            return ctx.enter_context(nc.sbuf_tensor(name, shape, dt))

        def sem(name):
            return ctx.enter_context(nc.semaphore(name))

        big = sb("big", [P, NK * SEQ])
        gates = big[:, :].rearrange("p (n t) -> p n t", t=SEQ)
        rr = sb("rr", [P, 8448], F32R)
        ht = sb("ht", [P, 2, DK, SEQ], F32R)
        raw = sb("raw", [P, 5120])
        cst = sb("cst", [P, 256])
        picks = sb("picks", [P, 3, SEQ])
        gel = sb("gel", [P, 2, SEQ])
        psum = ctx.enter_context(nc.psum_tensor("psum", [P, 8, 512], F32))
        h_dram = nc.dram_tensor("h_kept", [2, P, D], F32, kind="Internal").ap()

        at = 0

        def take(n):
            nonlocal at
            at += n
            assert at <= NK * SEQ
            return big[:, at - n:at]

        xt = take(2 * D).rearrange("p (t d) -> p t d", t=2)
        xm = take(D)
        xs_at = at
        xs = take(3 * D).rearrange("p (t d) -> p t d", t=3)
        t32 = take(DK * SEQ).rearrange("p (k t) -> p k t", k=DK)
        t32m = take(DK * META).rearrange("p (k t) -> p k t", k=DK)
        wraw = take(3 * DK * CW).rearrange("p (s k n) -> p s k n", s=3, k=DK)
        z_at = at
        zq = take(2 * 512).rearrange("p (t n) -> p t n", t=2)
        ziq = take(2 * 512).rearrange("p (t n) -> p t n", t=2)
        zk = take(3 * 512).rearrange("p (t n) -> p t n", t=3)
        zv = take(3 * 512).rearrange("p (t n) -> p t n", t=3)
        zp = take(3 * 512).rearrange("p (t n) -> p t n", t=3)
        zi = take(3 * CI).rearrange("p (t n) -> p t n", t=3)
        rot_at = at
        qr = take(2 * 512).rearrange("p (t n) -> p t n", t=2)
        kr = take(3 * 512).rearrange("p (t n) -> p t n", t=3)
        tmp = take(3 * 512).rearrange("p (a n) -> p a n", a=3)
        iqr = take(2 * 512).rearrange("p (t n) -> p t n", t=2)
        kir = take(3 * P).rearrange("p (t n) -> p t n", t=3)
        stat = take(256)
        cossin = take(6 * HD)
        cos, sin = (cossin[:, a * 3 * HD:(a + 1) * 3 * HD].rearrange("p (t n) -> p t n", t=3) for a in range(2))
        gqk = take(2 * HD).rearrange("p (a n) -> p a n", a=2)
        score = take(KALL)
        work = take(KALL)
        bias = take(KALL)
        tops = take(16).rearrange("p (t n) -> p t n", t=2)
        grow = take(P)
        zt = take(T)
        at = max(at, NK * SEQ - 640)
        ksub = take(2 * P).rearrange("p (a n) -> p a n", a=2)
        kt_sub = take(2 * P).rearrange("p (a n) -> p a n", a=2)
        gains = take(20)
        half = take(1)
        scal = take(64)
        rel = big[:, rot_at:rot_at + NH * KALL]
        at = xs_at
        iqt = take(PAIRS * SEQ).rearrange("p (a t) -> p a t", a=PAIRS)
        kit = take(T)
        qt = take(PAIRS * SEQ).rearrange("p (a t) -> p a t", a=PAIRS)
        kt = take(PAIRS * T).rearrange("p (a t) -> p a t", a=PAIRS)
        yt = take(4 * SEQ).rearrange("p (a t) -> p a t", a=4)
        p32 = iqt
        at = z_at
        qp = take(2 * 2 * SEQ).rearrange("p (s a t) -> p s a t", s=2, a=2)
        sc = take(PH * 4 * NK).rearrange("p (h t a n) -> p h t a n", h=PH, t=2, a=2)
        v16 = take(PH * 64).rearrange("p (h t a k) -> p h t a k", h=PH, t=2, a=2)
        i16 = take(PH * 64).rearrange("p (h t a k) -> p h t a k", h=PH, t=2, a=2).bitcast(U32)
        n16 = take(PH * 64).rearrange("p (h t a k) -> p h t a k", h=PH, t=2, a=2)
        cand = take(PH * 2 * NCAND).rearrange("p (h t c) -> p h t c", h=PH, t=2)
        cide = take(PH * 2 * NCAND).rearrange("p (h t c) -> p h t c", h=PH, t=2)
        vtop = take(PH * 32).rearrange("p (t h k) -> p t h k", h=PH, t=2)
        ptop = take(PH * 32).rearrange("p (t h k) -> p t h k", h=PH, t=2).bitcast(U32)
        eid = take(PH * 32).rearrange("p (t h k) -> p t h k", h=PH, t=2)
        eqs = take(2 * 2 * TOPK * NCAND).rearrange("p (s t k c) -> p s t k c", s=2, t=2, k=TOPK)
        pick3 = take(3 * PH * 32).rearrange("p (a t h k) -> p a t h k", a=3, t=2, h=PH)
        eint = take(PH * 32).rearrange("p (t h k) -> p t h k", h=PH, t=2).bitcast(mybir.dt.int32)
        fint = take(PH * 32).rearrange("p (t h k) -> p t h k", h=PH, t=2).bitcast(mybir.dt.int32)
        assert at <= NK * SEQ - 640

        ident, iota = cst[:, 0:P], cst[:, P:2 * P]
        ixrel = raw[:, 0:NH * KALL]
        tmp_p = raw[:, 5120 - 3 * 512:5120].rearrange("p (a n) -> p a n", a=3)
        band = raw[:, 0:3 * 512].rearrange("p (a g t) -> p a g t", a=3, g=4)
        poolw = raw[:, 3072:3584].rearrange("p (g d) -> p g d", g=4)
        pt = raw[:, :].rearrange("p (c h q) -> p c h q", c=5, h=NH)
        u_raw = raw[:, 0:2 * D].rearrange("p (s k c) -> p s k c", s=2, k=DK)
        v_raw = raw[:, 2 * D:4 * D].rearrange("p (s d) -> p s d", s=2)
        oh_g = raw[:, 2 * D:5 * D].rearrange("p (s q n) -> p s q n", s=OHS, q=GRP)
        w_sp = rr[:, 0:8192].rearrange("p (s a k n) -> p s a k n", s=2, a=2, k=DK)
        hm = rr[:, 8192:8448].rearrange("p (a k t) -> p a k t", a=2, k=DK)
        ut = rr[:, 0:2 * D].rearrange("p (a k n) -> p a k n", a=2, k=DK)
        v_sp = rr[:, 2 * D:6 * D].rearrange("p (s a d) -> p s a d", s=2, a=2)
        oh = rr[:, 0:6 * D].rearrange("p (s a q n) -> p s a q n", s=OHS, a=2, q=GRP)
        g_sp = rr[:, 6 * D:7 * D].rearrange("p (s a t) -> p s a t", s=2, a=2)

        def f(ap):
            return ap.bitcast(F32)

        rows = [P, P, META]
        trow = [1, 2, 0]

        ld_x = [sem(f"ld_x{t}") for t in range(3)]
        ld_cst, ld_rope, ld_small, ld_g2, ld_band = (sem(n) for n in ("ld_cst", "ld_rope", "ld_small", "ld_g2", "ld_band"))
        ld_w = [sem(f"ld_w{s}") for s in range(3)]
        ld_u = [sem(f"ld_u{s}") for s in range(2)]
        ld_v = [sem(f"ld_v{s}") for s in range(2)]
        ld_h = sem("ld_h")
        st_h, st_out = sem("st_h"), sem("st_out")
        a_sq, a_xs, a_hi, w_hi, z_ev = sem("a_sq"), sem("a_xs"), sem("a_hi"), sem("w_hi"), sem("z_ev")
        ix_tr, a_rel, y_ev, pc_hi, qk_tr = sem("ix_tr"), sem("a_rel"), sem("y_ev"), sem("pc_hi"), sem("qk_tr")
        a_exp, pt_ev, cat_hi, qp_ev, s_ev = sem("a_exp"), sem("pt_ev"), sem("cat_hi"), sem("qp_ev"), sem("s_ev")
        a_soft, b_ev, ut_hi, v_hi, a_gel = sem("a_soft"), sem("b_ev"), sem("ut_hi"), sem("v_hi"), sem("a_gel")
        ks_ev, pk_ev, ohg_up, zt_ev = sem("ks_ev"), sem("pk_ev"), sem("ohg_up"), sem("zt_ev")
        d_ms, d_t32, d_lo, w_lo_e, d_seq = sem("d_ms"), sem("d_t32"), sem("d_lo"), sem("w_lo_e"), sem("d_seq")
        d_ki, d_iq, d_qst, d_kst, d_qk = sem("d_ki"), sem("d_iq"), sem("d_qst"), sem("d_kst"), sem("d_qk")
        d_p32, pc_lo, d_log, d_max, d_prob = sem("d_p32"), sem("pc_lo"), sem("d_log"), sem("d_max"), sem("d_prob")
        cat_lo, h_ev, d_top, d_match, d_sub = sem("cat_lo"), sem("h_ev"), sem("d_top"), sem("d_match"), sem("d_sub")
        d_pick, oh_up, ut_lo, v_lo, g_lo = sem("d_pick"), sem("oh_up"), sem("ut_lo"), sem("v_lo"), sem("g_lo")
        d_g32, d_out = sem("d_g32"), sem("d_out")
        d_xs = sem("d_xs")
        d_place, n_ev = sem("d_place"), sem("n_ev")
        d_rel, p_qk = sem("d_rel"), sem("p_qk")
        p_half, p_rs, w_lo_o, p_seq, p_eq, ohp_up = (sem(n) for n in ("p_half", "p_rs", "w_lo_o", "p_seq", "p_eq", "ohp_up"))
        pe_x, z_done, pe_ix, pe_sc, pe_y = sem("pe_x"), sem("z_done"), sem("pe_ix"), sem("pe_sc"), sem("pe_y")
        pe_qk, pe_log, pe_pt, pe_cat, pe_ks = sem("pe_qk"), sem("pe_log"), sem("pe_pt"), sem("pe_cat"), sem("pe_ks")
        pe_gain, pe_zt = sem("pe_gain"), sem("pe_zt")
        pe_s, pe_pk, b_done, t_done, a_done, c_done = (sem(n) for n in ("pe_s", "pe_pk", "b_done", "t_done", "a_done", "c_done"))

        pu_v = pu[0].rearrange("(n m) d -> n m d", m=NK)
        pv_v = pv[0].rearrange("(n m) d -> n m d", m=NK)

        def w_src(c):
            w, first = (w_in, W_IN[c]) if c < OUT0 else (w_out, (c - OUT0) * CW) if c < WQ0 else (wq, (c - WQ0) * CW)
            n = CI if c == 0 else CW
            return w[0, :, first:first + n].rearrange("(k p) n -> p k n", p=P), n

        def w_cols(c):
            return CI if c == 0 else CW

        def lo_ready(eng, c):
            mine = [k for k in range(c + 1) if by_vector(k) == by_vector(c)]
            eng.wait_ge(w_lo_e if by_vector(c) else w_lo_o, len(mine))

        block = ctx.enter_context(nc.Block())

        @block.sync
        def _(sp):
            def load_w(c):
                if c >= 3:
                    sp.wait_ge(w_hi, c - 2)
                    lo_ready(sp, c - 3)
                src, n = w_src(c)
                sp.dma_start(wraw[:, c % 3, :, 0:n], src).then_inc(ld_w[c % 3], 16)

            sp.dma_start(xt[:, 0, :], x[0, 0:P, :]).then_inc(ld_x[0], 16)
            sp.dma_start(xt[:, 1, :], x[0, P:2 * P, :]).then_inc(ld_x[1], 16)
            sp.dma_start(xm[0:META, :], meta[:, :]).then_inc(ld_x[2], 16)
            load_w(0)
            sp.dma_start(cst[:, :], const[:, 0:K_COS]).then_inc(ld_cst, 16)
            load_w(1)
            load_w(2)
            sp.dma_start(cossin, const[:, K_COS:K_BAND]).then_inc(ld_rope, 16)
            for c in range(3, 6):
                load_w(c)
            for c in range(6, 9):
                load_w(c)
            sp.wait_ge(d_rel, 2)
            sp.dma_start(band, const[:, K_BAND:N_CONST].rearrange("p (a g t) -> p a g t", a=3, g=4)).then_inc(ld_band, 16)
            sp.dma_start(poolw, pool_w[0].rearrange("g c d -> c g d")).then_inc(ld_band, 16)
            sp.dma_start(ksub[:, 0, :], sk1[0]).then_inc(ld_g2, 16)
            sp.dma_start(ksub[:, 1, :], sk2[0]).then_inc(ld_g2, 16)
            for c in range(9, OUT0 + 4):
                load_w(c)
            for c in range(OUT0 + 4, WQ0 + 4):
                load_w(c)
            sp.wait_ge(h_ev, 2 * N_OUT)
            for t in range(2):
                sp.dma_start(h_dram[t], xt[:, t, :]).then_inc(st_h, 16)
            for c in range(WQ0 + 4, N_CHUNK):
                load_w(c)
            sp.wait_ge(pe_cat, 2)
            for s in range(2):
                sp.dma_start(u_raw[:, s], pu_v[:, s, :].rearrange("p (k c) -> p k c", k=DK)).then_inc(ld_u[s], 16)
            sp.wait_ge(b_done, NQ)
            for s in range(2):
                sp.dma_start(v_raw[:, s, :], pv_v[:, s, :]).then_inc(ld_v[s], 16)
            with sp.Fori(0, NK // 2 - 1) as i:
                for s in range(2):
                    sp.wait_ge(t_done, 2 * i + (s + 1))
                    sp.dma_start(u_raw[:, s], pu_v[:, ds(2 * i + (s + 2), 1), :].rearrange("p o (k c) -> p (o k) c", k=DK))\
                      .then_inc(ld_u[s], 16)
                    sp.wait_ge(v_hi, 2 * i + (s + 1))
                    sp.wait_ge(v_lo, 2 * i + (s + 1))
                    sp.dma_start(v_raw[:, s, :], pv_v[:, ds(2 * i + (s + 2), 1), :].rearrange("p o d -> p (o d)"))\
                      .then_inc(ld_v[s], 16)
            sp.wait_ge(st_h, 32)
            sp.wait_ge(t_done, NK)
            for t in range(2):
                sp.dma_start(raw[:, t * D:(t + 1) * D], h_dram[t]).then_inc(ld_h, 16)
            for t in range(2):
                sp.wait_ge(d_out, 2 * t + 2)
                sp.dma_start(out[0, t * P:(t + 1) * P, :], big[:, t * D:(t + 1) * D]).then_inc(st_out, 16)
            sp.wait_ge(st_out, 32)

        @block.scalar
        def _(act):
            act.dma_start(grow[0:8, :], g1[0].rearrange("(k p) -> k p", p=P)).then_inc(ld_small, 16)
            act.dma_start(grow[8:16, :], g2[0].rearrange("(k p) -> k p", p=P)).then_inc(ld_small, 16)
            act.dma_start(grow[16:20, :], pool_s[0].rearrange("(k p) -> k p", p=P)).then_inc(ld_small, 16)
            act.dma_start(gqk[:, 0, :], gq[0:1, :].to_broadcast([P, HD])).then_inc(ld_small, 16)
            act.dma_start(gqk[:, 1, :], gk[0:1, :].to_broadcast([P, HD])).then_inc(ld_small, 16)

            def split_w(c):
                act.wait_ge(ld_w[c % 3], 16 * (c // 3 + 1))
                if c >= 2:
                    act.wait_ge(z_done, z_after(c - 2))
                n = w_cols(c)
                act.activation(w_sp[:, c % 2, 0, :, 0:n], wraw[:, c % 3, :, 0:n], ACT.Copy).then_inc(w_hi, 1)

            srcs = [xt[:, 0, :], xt[:, 1, :], xm[0:META, :]]
            for t, r in enumerate(rows):
                act.wait_ge(ld_x[t], 16)
                act.activation(xs[0:r, t, :], srcs[t], ACT.Square, accum_out=stat[0:r, t:t + 1]).then_inc(a_sq, 1)
            split_w(0)
            for t, r in enumerate(rows):
                act.wait_ge(p_rs, t + 1)
                act.wait_ge(a_sq, t + 1)
                act.activation(xs[0:r, t, :], srcs[t], ACT.Copy, scale=scal[0:r, 8 + t:9 + t]).then_inc(a_xs, 1)
            split_w(1)
            for t in range(3):
                act.wait_ge(d_t32, t + 1)
                dst, src = (ht[:, 0, :, t * P:(t + 1) * P], t32[:, :, t * P:(t + 1) * P]) if t < 2 else (hm[:, 0], t32m)
                act.activation(dst, src, ACT.Copy).then_inc(a_hi, 1)

            def keep_z(c):
                sec, first = {0: (zi, 0), 1: (ziq, 0), 2: (ziq, CW), 3: (zq, 0), 4: (zq, CW), 5: (zk, 0), 6: (zk, CW),
                              7: (zv, 0), 8: (zv, CW), 9: (zp, 0), 10: (zp, CW)}[c]
                n = w_cols(c)
                for t in range(chunk_tiles(c)):
                    act.wait_ge(z_done, z_after(c) - chunk_tiles(c) + t + 1)
                    r = rows[t]
                    act.activation(sec[0:r, t, first:first + n], psum[0:r, 3 * (c % 2) + t, 0:n], ACT.Copy)\
                       .then_inc(z_ev, 1)

            act.wait_ge(pe_zt, 2)
            act.activation(zt[0:CI, :], psum[0:CI, 5, 0:T], ACT.Copy).then_inc(zt_ev, 1)
            for c in range(5):
                keep_z(c)
                split_w(c + 2)
            for t in range(2):
                act.wait_ge(pe_ix, t + 1)
                act.activation(iqt[:, :, t * P:(t + 1) * P], psum[:, t, :].rearrange("p (a q) -> p a q", a=PAIRS),
                               ACT.Copy).then_inc(ix_tr, 1)
            act.wait_ge(pe_ix, 3)
            act.activation(kit, psum[:, 2, 0:T], ACT.Copy).then_inc(ix_tr, 1)
            for t in range(2):
                act.wait_ge(pe_sc, 2)
                act.activation(ixrel[:, NH * KOFF[t]:NH * (KOFF[t] + KEYS[t])].rearrange("p (h k) -> p h k", h=NH),
                               psum[:, :, KOFF[t]:KOFF[t] + KEYS[t]], ACT.Relu).then_inc(a_rel, 1)
            for c in range(5, N_IN - 1):
                keep_z(c)
                split_w(c + 2)
            for t in range(2):
                act.wait_ge(pe_qk, t + 1)
                act.activation(qt[:, :, t * P:(t + 1) * P], psum[:, t, :].rearrange("p (a q) -> p a q", a=PAIRS),
                               ACT.Copy).then_inc(qk_tr, 1)
            for n, (t, first) in enumerate(((2, 0), (0, META), (1, META + P))):
                act.wait_ge(pe_qk, n + 3)
                r = rows[t]
                act.activation(kt[:, :, first:first + r], psum[:, 2 + n, 0:PAIRS * r].rearrange("p (a q) -> p a q", a=PAIRS),
                               ACT.Copy).then_inc(qk_tr, 1)
            for t in range(2):
                act.wait_ge(d_max, t + 1)
                for h in range(NH):
                    a = NH * KOFF[t] + h * KEYS[t]
                    act.activation(rel[:, a:a + KEYS[t]], rel[:, a:a + KEYS[t]], ACT.Exp,
                                   bias=stat[:, 128 + 8 * t + h:129 + 8 * t + h],
                                   accum_out=stat[:, 144 + 8 * t + h:145 + 8 * t + h]).then_inc(a_exp, 1)
            keep_z(N_IN - 1)
            split_w(N_IN + 1)
            act.wait_ge(pe_y, 1)
            act.activation(yt, psum[:, 6:8, :].rearrange("p t (g q) -> p g t q", g=4), ACT.Copy).then_inc(y_ev, 1)
            for n, (c, b, r) in enumerate(((0, 0, META), (1, 2, P), (2, 4, META), (3, 6, P), (4, 0, P))):
                if n == 2:
                    act.wait_ge(d_p32, 1)
                    act.activation(ht[:, 0, 4:8, :], p32, ACT.Copy).then_inc(pc_hi, 1)
                act.wait_ge(pe_pt, n + 1)
                act.activation(pt[0:r, c].rearrange("p (b h) q -> p b (h q)", b=2), psum[0:r, b:b + 2, :],
                               ACT.Copy).then_inc(pt_ev, 1)
            for t in range(2):
                act.wait_ge(pe_cat, t + 1)
                act.activation(ht[:, 0, 0:4, t * P:(t + 1) * P], psum[:, 2 + t, :].rearrange("p (a q) -> p a q", a=PAIRS),
                               ACT.Copy).then_inc(cat_hi, 1)
            split_w(OUT0 + 2)
            for n in range(N_OUT):
                for t in range(2):
                    act.wait_ge(h_ev, 2 * n + t + 1)
                    at0 = 200 + N_OUT * t + n
                    act.activation(xs[:, t, n * CW:(n + 1) * CW], xt[:, t, n * CW:(n + 1) * CW], ACT.Square,
                                   accum_out=stat[:, at0:at0 + 1]).then_inc(a_sq, 1)
                if n < N_OUT - 1:
                    split_w(OUT0 + 3 + n)
            act.wait_ge(p_rs, 6)
            act.wait_ge(a_sq, 3 + 2 * N_OUT)
            act.activation(xs[:, 0, :], xt[:, 0, :], ACT.Copy, scale=scal[:, 48:49]).then_inc(a_xs, 1)
            act.wait_ge(pe_ks, 1)
            act.activation(kt_sub, psum[:, 5, 0:2 * P].rearrange("p (a n) -> p a n", a=2), ACT.Copy).then_inc(ks_ev, 1)
            for t in range(2):
                act.wait_ge(d_t32, 3 + t + 1)
                act.activation(ht[:, 0, :, t * P:(t + 1) * P], t32[:, :, t * P:(t + 1) * P], ACT.Copy).then_inc(a_hi, 1)

            def numbers(h):
                act.wait_ge(d_top, h + 1)
                act.activation(n16[:, h, :, 0, :], i16[:, h, :, 0, :], ACT.Copy, scale=float(NK)).then_inc(n_ev, 1)
                act.activation(n16[:, h, :, 1, :], i16[:, h, :, 1, :], ACT.Copy).then_inc(n_ev, 1)

            def keep_s(h):
                act.wait_ge(pe_s, h + 1)
                act.activation(sc[:, h].rearrange("p t a n -> p (t a n)"), psum[:, 3 * ((WQ0 + h) % 2) + 1, :], ACT.Copy)\
                   .then_inc(s_ev, 1)

            for h in range(PH):
                act.wait_ge(z_done, z_after(WQ0 + h))
                if h >= 2:
                    act.wait_ge(pe_s, h - 1)
                act.activation(qp[:, h % 2].rearrange("p a t -> p (a t)"), psum[:, 3 * ((WQ0 + h) % 2), :], ACT.Copy)\
                   .then_inc(qp_ev, 1)
                keep_s(h)
                if h >= 2:
                    numbers(h - 2)
                if WQ0 + h + 2 < N_CHUNK:
                    split_w(WQ0 + h + 2)
            numbers(PH - 2)
            numbers(PH - 1)
            act.wait_ge(d_sub, 1)
            act.activation(pick3[:, 2], pick3[:, 2], ACT.Exp).then_inc(a_soft, 1)
            act.wait_ge(pe_pk, 1)
            act.activation(picks[:, 0:2, :].rearrange("p a t -> p (a t)"), psum[:, 6, :], ACT.Copy).then_inc(pk_ev, 1)
            act.wait_ge(pe_pk, 2)
            act.activation(picks[:, 2, :], psum[:, 7, 0:SEQ], ACT.Copy).then_inc(pk_ev, 1)
            def gated(s, tok):
                for j in range(ACT_T):
                    i = act.activation(oh_g[:, s, j, :], f(oh[:, s, 1, j, :]), ACT.Copy, scale=picks[:, 2, ds(tok + j, 1)])
                i.then_inc(ohg_up, 1)

            def keep_gates(s, tok):
                act.activation(gates[:, :, ds(tok, GRP)], psum[:, 2 + 2 * s:4 + 2 * s, :].rearrange("p b (q n) -> p n (b q)", n=NK), ACT.Copy)\
                   .then_inc(b_ev, 1)

            act.wait_ge(pk_ev, 2)

            def gate_group(q, s, first=False):
                act.wait_ge(oh_up, q + 1)
                gated(s, GRP * q)
                if not first:
                    act.wait_ge(b_done, q)
                    keep_gates((s - 1) % OHS, GRP * q - GRP)

            for q in range(OHS):
                gate_group(q, q, q == 0)
            with act.Fori(1, NQ // OHS) as i:
                for s in range(OHS):
                    gate_group(OHS * i + s, s)
            for q in range(Q_LAST, NQ):
                gate_group(q, q % OHS)
            act.wait_ge(b_done, NQ)
            keep_gates((NQ - 1) % OHS, GRP * (NQ - 1))

            def block_u(s, b, first):
                act.wait_ge(t_done, b + 1)
                act.activation(ut[:, 0], psum[:, 0:2, :].rearrange("p b (k n) -> p (b k) n", n=P), ACT.Copy).then_inc(ut_hi, 1)

            def block_v(s, b, first):
                if not first:
                    act.wait_ge(c_done, b - 1)
                act.wait_ge(ld_v[s], v_turn(b, s))
                act.activation(v_sp[:, s, 0, :], v_raw[:, s, :], ACT.Copy).then_inc(v_hi, 1)

            def block_g(s, b, first):
                act.wait_ge(a_done, b + 1)
                if not first:
                    act.wait_ge(d_g32, b - 1)
                act.activation(gel[:, s, :], psum[:, 2 + s, 0:SEQ], ACT.Gelu).then_inc(a_gel, 1)

            def v_turn(b, s):
                return 8 * b + (16 - 8 * s)

            for b in range(2):
                block_u(b, b, True)
                block_v(b, b, True)
                block_g(b, b, True)
            with act.Fori(1, NK // 2) as i:
                for s in range(2):
                    block_u(s, 2 * i + s, False)
                    block_v(s, 2 * i + s, False)
                    block_g(s, 2 * i + s, False)

        @block.vector
        def _(dve):
            seq = Count()

            def split_lo(c):
                dve.wait_ge(w_hi, c + 1)
                n = w_cols(c)
                dve.tensor_tensor(w_sp[:, c % 2, 1, :, 0:n], wraw[:, c % 3, :, 0:n], f(w_sp[:, c % 2, 0, :, 0:n]), ALU.subtract)\
                   .then_inc(w_lo_e, 1)

            for t, r in enumerate(rows):
                dve.wait_ge(a_sq, t + 1)
                dve.tensor_scalar(scal[0:r, t:t + 1], stat[0:r, t:t + 1], 1.0 / D, EPS, ALU.mult, ALU.add).then_inc(d_ms, 1)
            split_lo(0)
            dve.wait_ge(pe_gain, 1)
            dve.tensor_copy(gains, psum[:, 5, 0:20]).then_inc(d_seq, 1)
            dve.wait_ge(d_seq, seq.up())
            gain = [gains[:, 0:8], gains[:, 8:16]]
            for t, r in enumerate(rows):
                dve.wait_ge(pe_x, t + 1)
                dst = t32[:, :, t * P:(t + 1) * P] if t < 2 else t32m
                src = (psum[:, 2 * t:2 * t + 2, :].rearrange("p b (k n) -> p (b k) n", n=P) if t < 2
                       else psum[:, 4, 0:DK * META].rearrange("p (k n) -> p k n", n=META))
                dve.tensor_tensor(dst, src, gain[0].unsqueeze(2).to_broadcast([P, DK, r]), ALU.mult).then_inc(d_t32, 1)
            for t in range(3):
                dve.wait_ge(d_t32, t + 1)
                dve.wait_ge(a_hi, t + 1)
                hi, lo, src = ((ht[:, 0, :, t * P:(t + 1) * P], ht[:, 1, :, t * P:(t + 1) * P], t32[:, :, t * P:(t + 1) * P])
                               if t < 2 else (hm[:, 0], hm[:, 1], t32m))
                dve.tensor_tensor(lo, src, f(hi), ALU.subtract).then_inc(d_lo, 1)
            split_lo(2)

            def rope(r, t, src, nh, dsts, done):
                s3 = src.rearrange("p (h d) -> p h d", h=nh)
                c3 = cos[0:r, trow[t], :].unsqueeze(1).to_broadcast([r, nh, HD])
                n3 = sin[0:r, trow[t], :].unsqueeze(1).to_broadcast([r, nh, HD])
                a3 = tmp[0:r, 0, 0:nh * HD].rearrange("p (h d) -> p h d", h=nh)
                b3 = tmp[0:r, 1, 0:nh * HD].rearrange("p (h d) -> p h d", h=nh)
                hh = HD // 2
                dve.tensor_tensor(a3, s3, c3, ALU.mult).then_inc(d_seq, 1)
                seq.up()
                dve.tensor_tensor(b3[:, :, 0:hh], s3[:, :, hh:HD], n3[:, :, 0:hh], ALU.mult).then_inc(d_seq, 1)
                seq.up()
                dve.tensor_tensor(b3[:, :, hh:HD], s3[:, :, 0:hh], n3[:, :, hh:HD], ALU.mult).then_inc(d_seq, 1)
                dve.wait_ge(d_seq, seq.up())
                for d in dsts:
                    dve.tensor_tensor(d.rearrange("p (h d) -> p h d", h=nh), a3, b3, ALU.add).then_inc(done, 1)

            dve.wait_ge(ld_rope, 16)
            dve.wait_ge(z_ev, 3)
            for n, t in enumerate((0, 1, 2)):
                r = rows[t]
                rope(r, t, zi[0:r, t, 0:HD], 1, [kir[0:r, t, 0:HD], kir[0:r, t, HD:P]], d_ki)
                dve.wait_ge(d_ki, 2 * n + 2)
            dve.tensor_scalar(scal[:, 16:32].rearrange("p (t h) -> p t h", t=2), zi[:, 0:2, HD:CI],
                              NH ** -0.5 * HD ** -0.5, None, ALU.mult).then_inc(d_seq, 1)
            seq.up()
            split_lo(4)
            dve.wait_ge(z_ev, z_after(2))
            for t in range(2):
                rope(P, t, ziq[:, t, :], NH, [iqr[:, t, :]], d_iq)
                dve.wait_ge(d_iq, t + 1)

            def head_means(t, src, at0, done):
                r = rows[t]
                dve.tensor_tensor(tmp[0:r, 2, :], src, src, ALU.mult).then_inc(d_seq, 1)
                dve.wait_ge(d_seq, seq.up())
                dve.tensor_reduce(stat[0:r, at0:at0 + 8], tmp[0:r, 2, :].rearrange("p (h d) -> p h d", h=NH), AX.X, ALU.add)\
                   .then_inc(d_seq, 1)
                dve.wait_ge(d_seq, seq.up())
                dve.tensor_scalar(stat[0:r, at0:at0 + 8], stat[0:r, at0:at0 + 8], 1.0 / HD, EPS, ALU.mult, ALU.add)\
                   .then_inc(done, 1)

            dve.wait_ge(z_ev, z_after(4))
            for t in range(2):
                head_means(t, zq[:, t, :], 32 + 8 * t, d_qst)
            split_lo(6)
            for t in range(2):
                dve.wait_ge(a_rel, t + 1)
                k = KEYS[t]
                acc = score[:, KOFF[t]:KOFF[t] + k]
                for h in range(NH):
                    part = ixrel[:, NH * KOFF[t] + h * k:NH * KOFF[t] + (h + 1) * k]
                    w = scal[:, 16 + 8 * t + h:17 + 8 * t + h]
                    if h == 0:
                        dve.tensor_scalar(acc, part, w, None, ALU.mult).then_inc(d_seq, 1)
                    else:
                        i = dve.scalar_tensor_tensor(acc, part, w, acc, ALU.mult, ALU.add)
                        if h == NH - 1:
                            i.then_inc(d_rel, 1)
                            dve.wait_ge(d_rel, t + 1)
                            break
                        i.then_inc(d_seq, 1)
                    dve.wait_ge(d_seq, seq.up())
                dve.memset(acc[0:KSEL, k - 64:k], NEG).then_inc(d_seq, 1)
                dve.wait_ge(d_seq, seq.up())

            parts = [[m[:, KOFF[t]:KOFF[t] + KEYS[t]] for m in (score, work, bias)] for t in range(2)]
            for n in range(KSEL // 8):
                for t, (a, w, b) in enumerate(parts):
                    if n:
                        dve.wait_ge(d_seq, seq.n - 1)
                    dve.max(tops[:, t, :], a if n == 0 else w).then_inc(d_seq, 1)
                    seq.up()
                for t, (a, w, b) in enumerate(parts):
                    dve.wait_ge(d_seq, seq.n - 1)
                    dve.match_replace(w, tops[:, t, :], a if n == 0 else w, NEG).then_inc(d_seq, 1)
                    seq.up()
                if n == KSEL // 8 - 2:
                    split_lo(8)
            for t, (a, w, b) in enumerate(parts):
                dve.wait_ge(d_seq, seq.n - 1)
                dve.tensor_tensor(b, w, a, ALU.is_equal).then_inc(d_seq, 1)
                seq.up()
            for t, (a, w, b) in enumerate(parts):
                dve.wait_ge(d_seq, seq.n - 1)
                dve.tensor_scalar(b, b, -1.0e30, None, ALU.mult).then_inc(d_seq, 1)
                seq.up()
            dve.wait_ge(z_ev, z_after(6))
            for t in range(3):
                head_means(t, zk[0:rows[t], t, :], 48 + 8 * t, d_kst)
            split_lo(9)

            def norm_rope(t, src, gi, at0, dst):
                r = rows[t]
                m = tmp[0:r, 2, :]
                m3 = m.rearrange("p (h d) -> p h d", h=NH)
                dve.tensor_tensor(m3, src.rearrange("p (h d) -> p h d", h=NH),
                                  stat[0:r, at0:at0 + 8].unsqueeze(2).to_broadcast([r, NH, HD]), ALU.mult).then_inc(d_seq, 1)
                dve.wait_ge(d_seq, seq.up())
                dve.tensor_tensor(m3, m3, gqk[0:r, gi, :].unsqueeze(1).to_broadcast([r, NH, HD]), ALU.mult).then_inc(d_seq, 1)
                dve.wait_ge(d_seq, seq.up())
                rope(r, t, m, NH, [dst], d_qk)

            split_lo(10)
            dve.wait_ge(p_rs, 5)
            for n, t in enumerate((2, 1)):
                r = rows[t]
                norm_rope(t, zk[0:r, t, :], 1, 96 + 8 * t, kr[0:r, t, :])
                dve.wait_ge(d_qk, 1 + n)
            for t in range(2):
                k = KEYS[t]
                lg = rel[:, NH * KOFF[t]:NH * (KOFF[t] + k)].rearrange("p (h k) -> p h k", h=NH)
                dve.wait_ge(pe_log, 2)
                dve.scalar_tensor_tensor(lg, psum[:, :, KOFF[t]:KOFF[t] + k], HD ** -0.5,
                                         bias[:, KOFF[t]:KOFF[t] + k].unsqueeze(1).to_broadcast([P, NH, k]),
                                         ALU.mult, ALU.add).then_inc(d_log, 1)
            for t in range(2):
                k = KEYS[t]
                lg = rel[:, NH * KOFF[t]:NH * (KOFF[t] + k)].rearrange("p (h k) -> p h k", h=NH)
                dve.wait_ge(d_log, t + 1)
                dve.tensor_reduce(stat[:, 128 + 8 * t:136 + 8 * t], lg, AX.X, ALU.max, negate=True).then_inc(d_max, 1)
            for t in range(2):
                k = KEYS[t]
                lg = rel[:, NH * KOFF[t]:NH * (KOFF[t] + k)].rearrange("p (h k) -> p h k", h=NH)
                dve.wait_ge(a_exp, NH * (t + 1))
                dve.reciprocal(stat[:, 160 + 8 * t:168 + 8 * t], stat[:, 144 + 8 * t:152 + 8 * t]).then_inc(d_seq, 1)
                dve.wait_ge(d_seq, seq.up())
                dve.tensor_tensor(lg, lg, stat[:, 160 + 8 * t:168 + 8 * t].unsqueeze(2).to_broadcast([P, NH, k]), ALU.mult)\
                   .then_inc(d_prob, 1)
            dve.wait_ge(pe_y, 2)
            dve.tensor_tensor(p32, psum[:, 6:8, :].rearrange("p b (g t) -> p (b g) t", t=SEQ),
                              gains[:, 16:20].unsqueeze(2).to_broadcast([P, 4, SEQ]), ALU.mult).then_inc(d_p32, 1)
            dve.wait_ge(pc_hi, 1)
            dve.tensor_tensor(ht[:, 1, 4:8, :], p32, f(ht[:, 0, 4:8, :]), ALU.subtract).then_inc(pc_lo, 1)
            split_lo(12)
            for t in range(2):
                dve.wait_ge(cat_hi, t + 1)
                dve.tensor_tensor(ht[:, 1, 0:4, t * P:(t + 1) * P], psum[:, 2 + t, :].rearrange("p (a q) -> p a q", a=PAIRS),
                                  f(ht[:, 0, 0:4, t * P:(t + 1) * P]), ALU.subtract).then_inc(cat_lo, 1)
            for c in range(OUT0, WQ0):
                for t in range(2):
                    dve.wait_ge(z_done, z_after(c) - 1 + t)
                    n = (c - OUT0) * CW
                    dve.tensor_tensor(xt[:, t, n:n + CW], xt[:, t, n:n + CW], psum[:, 3 * (c % 2) + t, 0:CW], ALU.add)\
                       .then_inc(h_ev, 1)
                if c in (OUT0, OUT0 + 1):
                    split_lo(c + 2)
            dve.wait_ge(a_sq, 3 + 2 * N_OUT)
            dve.tensor_reduce(scal[:, 3:5], stat[:, 200:200 + 2 * N_OUT].rearrange("p (t n) -> p t n", t=2), AX.X, ALU.add)\
               .then_inc(d_seq, 1)
            dve.wait_ge(d_seq, seq.up())
            dve.tensor_scalar(scal[:, 3:5], scal[:, 3:5], 1.0 / D, EPS, ALU.mult, ALU.add).then_inc(d_ms, 1)
            dve.wait_ge(p_rs, 6)
            dve.tensor_scalar(xs[:, 1, :], xt[:, 1, :], scal[:, 49:50], None, ALU.mult).then_inc(d_xs, 1)
            for t, b in enumerate((6, 0)):
                dve.wait_ge(pe_x, 3 + t + 1)
                dve.tensor_tensor(t32[:, :, t * P:(t + 1) * P], psum[:, b:b + 2, :].rearrange("p b (k n) -> p (b k) n", n=P),
                                  gain[1].unsqueeze(2).to_broadcast([P, DK, P]), ALU.mult).then_inc(d_t32, 1)
            for t in range(2):
                dve.wait_ge(a_hi, 3 + t + 1)
                dve.tensor_tensor(ht[:, 1, :, t * P:(t + 1) * P], t32[:, :, t * P:(t + 1) * P],
                                  f(ht[:, 0, :, t * P:(t + 1) * P]), ALU.subtract).then_inc(d_lo, 1)

            split_lo(WQ0 + 1)

            def top16(parts, done):
                for n in range(2):
                    at = slice(8 * n, 8 * n + 8)
                    n0 = seq.n
                    for k, (vals, idx, src) in enumerate(parts):
                        if n:
                            dve.wait_ge(d_seq, n0 - len(parts) + k + 1)
                        dve.max(vals[:, at], src).then_inc(d_seq, 1)
                        seq.up()
                    for k, (vals, idx, src) in enumerate(parts):
                        dve.wait_ge(d_seq, n0 + k + 1)
                        i = dve.max_index(idx[:, at], vals[:, at], src)
                        if n and k == len(parts) - 1:
                            i.then_inc(done, 1)
                        else:
                            i.then_inc(d_seq, 1)
                            seq.up()
                    for k, (vals, idx, src) in enumerate(parts if n == 0 else []):
                        dve.wait_ge(d_seq, n0 + len(parts) + k + 1)
                        dve.match_replace(src, vals[:, at], src, NEG).then_inc(d_seq, 1)
                        seq.up()

            def pick(h):
                dve.wait_ge(s_ev, h + 1)
                top16([(v16[:, h, t, a, :], i16[:, h, t, a, :], sc[:, h, t, a, :]) for t in range(2) for a in range(2)], d_top)
                dve.wait_ge(d_seq, seq.n)
                for first, nr, ncol, o in STAIRS:
                    dve.tensor_tensor(cand[:, h, :, o:o + nr * ncol].rearrange("p t (i j) -> p t i j", i=nr),
                                      v16[:, h, :, 0, first:first + nr].unsqueeze(3).to_broadcast([P, 2, nr, ncol]),
                                      v16[:, h, :, 1, 0:ncol].unsqueeze(2).to_broadcast([P, 2, nr, ncol]), ALU.add)\
                       .then_inc(d_seq, 1)
                    seq.up()
                dve.wait_ge(d_seq, seq.n)
                top16([(vtop[:, t, h, :], ptop[:, t, h, :], cand[:, h, t, :]) for t in range(2)], d_place)
                dve.wait_ge(d_seq, seq.n)
                dve.wait_ge(d_place, h + 1)
                if h >= 2:
                    dve.wait_ge(d_pick, h - 1)
                for t in range(2):
                    i = dve.tensor_tensor(eqs[:, h % 2, t], iota[:, 0:NCAND].unsqueeze(1).to_broadcast([P, TOPK, NCAND]),
                                          ptop[:, t, h, :].unsqueeze(2).to_broadcast([P, TOPK, NCAND]), ALU.is_equal)
                i.then_inc(d_match, 1)

            def look_up(h):
                dve.wait_ge(p_eq, h + 1)
                dve.tensor_reduce(eid[:, :, h, :], eqs[:, h % 2], AX.X, ALU.add).then_inc(d_pick, 1)

            for h in range(PH):
                pick(h)
                if h == 0:
                    split_lo(WQ0 + 3)
                if h:
                    look_up(h - 1)
            dve.tensor_tensor(pick3[:, 2], vtop, vtop[:, :, :, 0:1].to_broadcast([P, 2, PH, TOPK]), ALU.subtract).then_inc(d_sub, 1)
            look_up(PH - 1)
            dve.wait_ge(d_pick, PH)
            dve.tensor_copy(eint, eid).then_inc(d_seq, 1)
            dve.wait_ge(d_seq, seq.up())
            dve.tensor_scalar(fint, eint, 7, None, ALU.logical_shift_right).then_inc(d_seq, 1)
            dve.wait_ge(d_seq, seq.up())
            dve.tensor_copy(pick3[:, 0], fint).then_inc(d_seq, 1)
            dve.wait_ge(d_seq, seq.up())
            dve.tensor_scalar(fint, eint, NK - 1, None, ALU.bitwise_and).then_inc(d_seq, 1)
            dve.wait_ge(d_seq, seq.up())
            dve.tensor_copy(pick3[:, 1], fint).then_inc(d_seq, 1)
            dve.wait_ge(a_soft, 1)
            seq.up()
            dve.tensor_reduce(scal[:, 0:16].rearrange("p (t h) -> p t h", t=2), pick3[:, 2], AX.X, ALU.add).then_inc(d_seq, 1)
            dve.wait_ge(d_seq, seq.up())
            dve.reciprocal(scal[:, 0:16], scal[:, 0:16]).then_inc(d_seq, 1)
            dve.wait_ge(d_seq, seq.up())
            dve.tensor_tensor(pick3[:, 2], pick3[:, 2],
                              scal[:, 0:16].rearrange("p (t h) -> p t h", t=2).unsqueeze(3).to_broadcast([P, 2, PH, TOPK]),
                              ALU.mult).then_inc(d_pick, 1)

            def ones(s, tok):
                dve.tensor_tensor(oh[:, s], iota.unsqueeze(1).unsqueeze(1).to_broadcast([P, 2, GRP, NK]),
                                  picks[:, 0:2, ds(tok, GRP)].unsqueeze(3).to_broadcast([P, 2, GRP, NK]), ALU.is_equal)\
                   .then_inc(oh_up, 1)

            dve.wait_ge(pk_ev, 2)
            for q in range(OHS):
                ones(q, GRP * q)
            with dve.Fori(1, NQ // OHS) as i:
                for s in range(OHS):
                    dve.wait_ge(b_done, OHS * i + (s + 1 - OHS))
                    ones(s, GRP * OHS * i + GRP * s)
            for q in range(Q_LAST, NQ):
                dve.wait_ge(b_done, q - OHS + 1)
                ones(q % OHS, GRP * q)

            def block_u(s, b):
                dve.wait_ge(ut_hi, b + 1)
                dve.tensor_tensor(ut[:, 1], psum[:, 0:2, :].rearrange("p b (k n) -> p (b k) n", n=P), f(ut[:, 0]), ALU.subtract)\
                   .then_inc(ut_lo, 1)

            def block_v(s, b):
                dve.wait_ge(v_hi, b + 1)
                dve.tensor_tensor(v_sp[:, s, 1, :], v_raw[:, s, :], f(v_sp[:, s, 0, :]), ALU.subtract).then_inc(v_lo, 1)

            def block_g(s, b, first):
                dve.wait_ge(a_gel, b + 1)
                act_in = gel[:, s, :]
                dve.tensor_tensor(gates_at(b), gates_at(b), act_in, ALU.mult).then_inc(d_g32, 1)
                dve.wait_ge(d_g32, b + 1)
                if not first:
                    dve.wait_ge(c_done, b - 1)
                dve.tensor_scalar(g_sp[:, s, 0, :], gates_at(b), 1.0, None, ALU.mult).then_inc(d_seq, 1)
                dve.wait_ge(d_seq, b + (seq.n + 1))
                dve.tensor_tensor(g_sp[:, s, 1, :], gates_at(b), f(g_sp[:, s, 0, :]), ALU.subtract).then_inc(g_lo, 1)

            def gates_at(b):
                return big[:, ds(b * SEQ, SEQ)]

            dve.wait_ge(b_ev, NQ)
            for b in range(2):
                block_u(b, b)
                block_v(b, b)
                block_g(b, b, True)
            with dve.Fori(1, NK // 2) as i:
                for s in range(2):
                    block_u(s, 2 * i + s)
                    block_v(s, 2 * i + s)
                    block_g(s, 2 * i + s, False)
            dve.wait_ge(c_done, NK)
            dve.wait_ge(ld_h, 32)
            dve.wait_ge(g_lo, NK)
            for t in range(2):
                for n in range(2):
                    a = t * D + n * 512
                    dve.tensor_tensor(big[:, a:a + 512], raw[:, a:a + 512], psum[:, 4 + 2 * t + n, :], ALU.add).then_inc(d_out, 1)

        @block.gpsimd
        def _(pool):
            seq = Count()
            pool.memset(half, -0.5).then_inc(p_half, 1)
            pool.wait_ge(p_half, 1)

            def rsqrt(dst, src, r, n):
                pool.tensor_tensor(dst, src, half[0:r, :].to_broadcast([r, n]), ALU.pow).then_inc(p_rs, 1)

            def split_lo(c):
                pool.wait_ge(w_hi, c + 1)
                pool.tensor_tensor(w_sp[:, c % 2, 1], wraw[:, c % 3], f(w_sp[:, c % 2, 0]), ALU.subtract).then_inc(w_lo_o, 1)

            for t, r in enumerate(rows):
                pool.wait_ge(d_ms, t + 1)
                rsqrt(scal[0:r, 8 + t:9 + t], scal[0:r, t:t + 1], r, 1)
            split_lo(1)
            split_lo(3)
            split_lo(5)
            pool.wait_ge(d_qst, 2)
            rsqrt(stat[:, 80:96], stat[:, 32:48], P, 16)

            def norm_rope(t, src, gi, at0, dst):
                hh = HD // 2
                m3, a3, b3 = (tmp_p[:, n, :].rearrange("p (h d) -> p h d", h=NH) for n in range(3))
                c3, n3 = (a[:, trow[t], :].unsqueeze(1).to_broadcast([P, NH, HD]) for a in (cos, sin))
                pool.tensor_tensor(m3, src.rearrange("p (h d) -> p h d", h=NH),
                                   stat[:, at0:at0 + 8].unsqueeze(2).to_broadcast([P, NH, HD]), ALU.mult).then_inc(p_seq, 1)
                pool.wait_ge(p_seq, seq.up())
                pool.tensor_tensor(m3, m3, gqk[:, gi, :].unsqueeze(1).to_broadcast([P, NH, HD]), ALU.mult).then_inc(p_seq, 1)
                pool.wait_ge(p_seq, seq.up())
                pool.tensor_tensor(a3, m3, c3, ALU.mult).then_inc(p_seq, 1)
                seq.up()
                pool.tensor_tensor(b3[:, :, 0:hh], m3[:, :, hh:HD], n3[:, :, 0:hh], ALU.mult).then_inc(p_seq, 1)
                seq.up()
                pool.tensor_tensor(b3[:, :, hh:HD], m3[:, :, 0:hh], n3[:, :, hh:HD], ALU.mult).then_inc(p_seq, 1)
                pool.wait_ge(p_seq, seq.up())
                pool.tensor_tensor(dst.rearrange("p (h d) -> p h d", h=NH), a3, b3, ALU.add).then_inc(p_qk, 1)

            pool.wait_ge(ld_rope, 16)
            pool.wait_ge(ld_small, 80)
            pool.wait_ge(z_ev, z_after(4))
            pool.wait_ge(p_rs, 4)
            for t in range(2):
                norm_rope(t, zq[:, t, :], 0, 80 + 8 * t, qr[:, t, :])
                pool.wait_ge(p_qk, t + 1)
            split_lo(7)
            pool.wait_ge(d_kst, 3)
            pool.tensor_tensor(stat[0:META, 112:120], stat[0:META, 64:72], half[0:META, :].to_broadcast([META, 8]), ALU.pow)\
                .then_inc(p_seq, 1)
            pool.wait_ge(p_seq, seq.up())
            rsqrt(stat[:, 96:112], stat[:, 48:64], P, 16)
            pool.wait_ge(p_rs, 5)
            norm_rope(0, zk[:, 0, :], 1, 96, kr[:, 0, :])
            split_lo(11)
            split_lo(15)
            pool.wait_ge(d_ms, 4)
            rsqrt(scal[:, 48:50], scal[:, 3:5], P, 2)

            def candidates(h):
                pool.wait_ge(n_ev, 2 * h + 2)
                for first, nr, ncol, o in STAIRS:
                    pool.tensor_tensor(cide[:, h, :, o:o + nr * ncol].rearrange("p t (i j) -> p t i j", i=nr),
                                       n16[:, h, :, 0, first:first + nr].unsqueeze(3).to_broadcast([P, 2, nr, ncol]),
                                       n16[:, h, :, 1, 0:ncol].unsqueeze(2).to_broadcast([P, 2, nr, ncol]), ALU.add)\
                        .then_inc(p_seq, 1)
                    seq.up()
                pool.wait_ge(p_seq, seq.n)
                pool.wait_ge(d_match, h + 1)
                for t in range(2):
                    i = pool.tensor_tensor(eqs[:, h % 2, t], eqs[:, h % 2, t],
                                           cide[:, h, t, :].unsqueeze(1).to_broadcast([P, TOPK, NCAND]), ALU.mult)
                i.then_inc(p_eq, 1)

            split_lo(WQ0 + 2)
            for h in range(PH):
                candidates(h)
                if WQ0 + 4 + h < N_CHUNK:
                    split_lo(WQ0 + 4 + h)

            def gated(s, tok):
                n = GRP - ACT_T
                pool.tensor_tensor(oh_g[:, s, ACT_T:, :], f(oh[:, s, 1, ACT_T:, :]),
                                   picks[:, 2, ds(tok + ACT_T, n)].unsqueeze(2).to_broadcast([P, n, NK]), ALU.mult)\
                    .then_inc(ohp_up, 1)

            pool.wait_ge(pk_ev, 2)
            for q in range(OHS):
                pool.wait_ge(oh_up, q + 1)
                gated(q, GRP * q)
            with pool.Fori(1, NQ // OHS) as i:
                for s in range(OHS):
                    pool.wait_ge(oh_up, OHS * i + (s + 1))
                    gated(s, GRP * OHS * i + GRP * s)
            for q in range(Q_LAST, NQ):
                pool.wait_ge(oh_up, q + 1)
                gated(q % OHS, GRP * q)

        @block.tensor
        def _(pe):
            def transpose8(t, banks, r):
                flat = psum[:, banks[0]:banks[-1] + 1, :].rearrange("p b n -> p (b n)")
                for k in range(DK):
                    i = pe.transpose(flat[:, k * r:(k + 1) * r], xs[0:r, t, k * P:(k + 1) * P], ident[0:r, 0:r])
                i.then_inc(pe_x, 1)

            def product(dst, lhs, rhs, sem_):
                n = 0
                for k in range(DK):
                    for a, b in ((0, 0), (0, 1), (1, 0)):
                        i = pe.matmul(dst, lhs(a, k), rhs(b, k), start=(n == 0), stop=(n == 3 * DK - 1))
                        n += 1
                i.then_inc(sem_, 1)

            def tokens(a, k, t):
                return ht[:, a, k, t * P:(t + 1) * P] if t < 2 else hm[:, a, k, :]

            def project(s, nt, n):
                for t in range(nt):
                    product(psum[0:rows[t], 3 * s + t, 0:n], lambda a, k: tokens(a, k, t), lambda b, k: w_sp[:, s, b, k, 0:n], z_done)

            pe.wait_ge(ld_cst, 16)
            pe.wait_ge(ld_small, 80)
            pe.transpose(psum[:, 5, 0:20], grow[0:20, :], ident[0:20, 0:20]).then_inc(pe_gain, 1)
            for t, b in enumerate(([0, 1], [2, 3], [4])):
                pe.wait_ge(a_xs, t + 1)
                transpose8(t, b, rows[t])
            pe.wait_ge(d_lo, 3)
            lo_ready(pe, 0)
            for toks, n, at0 in ((lambda b, k: ht[:, b, k, :], SEQ, 0), (lambda b, k: hm[:, b, k, :], META, SEQ)):
                product(psum[0:CI, 5, at0:at0 + n], lambda a, k: w_sp[:, 0, a, k, 0:CI], toks, pe_zt)
            pe.wait_ge(zt_ev, 1)
            for t, r in enumerate(rows):
                pe.transpose(psum[0:r, t, 0:CI], zt[0:CI, t * P:t * P + r], ident[0:CI, 0:CI]).then_inc(z_done, 1)
            with pe.Fori(0, 2) as i:
                pe.wait_ge(w_lo_o, i + 1)
                pe.wait_ge(z_ev, 4 * i + 1)
                project(1, 2, CW)
                pe.wait_ge(w_lo_e, i + 2)
                pe.wait_ge(z_ev, 4 * i + 3)
                project(0, 2, CW)
            pe.wait_ge(z_ev, z_after(4))
            for t in range(2):
                pe.wait_ge(d_iq, t + 1)
                for a in range(PAIRS):
                    i = pe.transpose(psum[:, t, a * P:(a + 1) * P], iqr[:, t, a * P:(a + 1) * P], ident)
                i.then_inc(pe_ix, 1)
            pe.wait_ge(d_ki, 6)
            for t, first in ((2, 0), (0, META), (1, META + P)):
                r = rows[t]
                i = pe.transpose(psum[:, 2, first:first + r], kir[0:r, t, :], ident[0:r, 0:r])
            i.then_inc(pe_ix, 1)
            pe.wait_ge(ix_tr, 3)
            for t in range(2):
                for h in range(NH):
                    lo = HD * (h % 2)
                    i = pe.matmul(psum[:, h, KOFF[t]:KOFF[t] + KEYS[t]], iqt[lo:lo + HD, h // 2, t * P:(t + 1) * P],
                                  kit[lo:lo + HD, 0:KEYS[t]], start=True, stop=True)
                i.then_inc(pe_sc, 1)
            pe.wait_ge(a_rel, 2)
            with pe.Fori(0, 2) as i:
                pe.wait_ge(w_lo_o, i + 3)
                pe.wait_ge(z_ev, 6 * i + z_after(3))
                project(1, 3, CW)
                pe.wait_ge(w_lo_e, i + 4)
                pe.wait_ge(z_ev, 6 * i + z_after(4))
                project(0, 3, CW)
            lo_ready(pe, 9)
            pe.wait_ge(z_ev, z_after(7))
            project(1, 3, CW)
            pe.wait_ge(z_ev, z_after(9))
            for t in range(2):
                pe.wait_ge(p_qk, t + 1)
                for a in range(PAIRS):
                    i = pe.transpose(psum[:, t, a * P:(a + 1) * P], qr[:, t, a * P:(a + 1) * P], ident)
                i.then_inc(pe_qk, 1)
            for n, t in enumerate((2, 0, 1)):
                if t == 0:
                    pe.wait_ge(p_qk, 3)
                else:
                    pe.wait_ge(d_qk, 1 if t == 2 else 2)
                r = rows[t]
                for a in range(PAIRS):
                    i = pe.transpose(psum[:, 2 + n, a * r:(a + 1) * r], kr[0:r, t, a * P:(a + 1) * P], ident[0:r, 0:r])
                i.then_inc(pe_qk, 1)
            pe.wait_ge(qk_tr, 5)
            for t in range(2):
                for h in range(NH):
                    lo = HD * (h % 2)
                    i = pe.matmul(psum[:, h, KOFF[t]:KOFF[t] + KEYS[t]], qt[lo:lo + HD, h // 2, t * P:(t + 1) * P],
                                  kt[lo:lo + HD, h // 2, 0:KEYS[t]], start=True, stop=True)
                i.then_inc(pe_log, 1)
            pe.wait_ge(d_log, 2)
            lo_ready(pe, N_IN - 1)
            project(0, 3, CW)
            pe.wait_ge(z_ev, z_after(N_IN - 1))
            pe.wait_ge(ld_band, 32)
            for t in range(2):
                for g in range(4):
                    dst = psum[:, 6 + t, g * P:(g + 1) * P]
                    gs = slice(g * P, (g + 1) * P)
                    pe.matmul(dst, zp[:, t, gs], band[:, 0, g, :], start=True, stop=False)
                    i = (pe.matmul(dst, zp[0:META, 2, gs], band[0:META, 2, g, :], start=False, stop=True) if t == 0
                         else pe.matmul(dst, zp[:, 0, gs], band[:, 1, g, :], start=False, stop=True))
            i.then_inc(pe_y, 1)

            for n, (t, r, first, b) in enumerate(((0, META, 0, 0), (0, P, META, 2), (1, META, 0, 4), (1, P, META, 6),
                                                  (1, P, META + P, 0))):
                if n == 2:
                    pe.wait_ge(y_ev, 1)
                    for g in range(4):
                        i = pe.matmul(psum[:, 6 + g // 2, (g % 2) * SEQ:(g % 2 + 1) * SEQ], poolw[:, g, :], yt[:, g, :],
                                      start=True, stop=True)
                    i.then_inc(pe_y, 1)
                pe.wait_ge(d_prob, t + 1)
                if n == 3:
                    pe.wait_ge(d_p32, 1)
                if n == 4:
                    pe.wait_ge(pt_ev, 1)
                for h in range(NH):
                    a = NH * KOFF[t] + h * KEYS[t] + first
                    i = pe.transpose(psum[0:r, b + h // 4, (h % 4) * P:(h % 4 + 1) * P], rel[:, a:a + r], ident)
                i.then_inc(pe_pt, 1)
            for t in range(2):
                chunks = ((0, 2, META), (1, 0, P)) if t == 0 else ((2, 2, META), (3, 0, P), (4, 1, P))
                pe.wait_ge(pt_ev, 2 if t == 0 else 5)
                for h in range(NH):
                    lo = HD * (h % 2)
                    for n, (c, vt, r) in enumerate(chunks):
                        i = pe.matmul(psum[lo:lo + HD, 2 + t, (h // 2) * P:(h // 2 + 1) * P], zv[0:r, vt, h * HD:(h + 1) * HD],
                                      pt[0:r, c, h, :], start=(n == 0), stop=(n == len(chunks) - 1))
                i.then_inc(pe_cat, 1)
            pe.wait_ge(cat_lo, 2)
            pe.wait_ge(pc_lo, 1)
            for c in range(OUT0, WQ0):
                lo_ready(pe, c)
                if c >= OUT0 + 2:
                    pe.wait_ge(h_ev, 2 * (c - OUT0 - 1))
                project(c % 2, 2, CW)
            pe.wait_ge(ld_g2, 32)
            for a in range(2):
                i = pe.transpose(psum[:, 5, a * P:(a + 1) * P], ksub[:, a, :], ident)
            i.then_inc(pe_ks, 1)
            pe.wait_ge(h_ev, 2 * N_OUT)
            for t, b in enumerate(([6, 7], [0, 1])):
                if t == 0:
                    pe.wait_ge(a_xs, 4)
                else:
                    pe.wait_ge(d_xs, 1)
                transpose8(t, b, P)
            pe.wait_ge(d_lo, 5)
            pe.wait_ge(ks_ev, 1)

            def queries(s):
                for a in range(2):
                    n = 0
                    for k in range(DK):
                        for u, w in ((0, 0), (0, 1), (1, 0)):
                            i = pe.matmul(psum[:, 3 * s, a * SEQ:(a + 1) * SEQ], w_sp[:, s, u, k, a * P:(a + 1) * P],
                                          ht[:, w, k, :], start=(n == 0), stop=(n == 3 * DK - 1))
                            n += 1
                i.then_inc(z_done, 1)

            def sub_scores(s, q):
                for t in range(2):
                    for a in range(2):
                        i = pe.matmul(psum[:, 3 * s + 1, (2 * t + a) * P:(2 * t + a + 1) * P], qp[:, q, a, t * P:(t + 1) * P],
                                      kt_sub[:, a, :], start=True, stop=True)
                i.then_inc(pe_s, 1)

            for h in range(PH):
                c = WQ0 + h
                lo_ready(pe, c)
                queries(c % 2)
                pe.wait_ge(qp_ev, h + 1)
                if h >= 2:
                    pe.wait_ge(s_ev, h - 1)
                sub_scores(c % 2, h % 2)
            pe.wait_ge(d_pick, PH + 1)
            for a in range(3):
                for t in range(2):
                    i = pe.transpose(psum[:, 6 + a // 2, (a % 2) * SEQ + t * P:(a % 2) * SEQ + (t + 1) * P],
                                     pick3[:, a, t].rearrange("p h k -> p (h k)"), ident)
                if a:
                    i.then_inc(pe_pk, 1)

            def gate_group(q, s, first=False):
                pe.wait_ge(ohg_up, q + 1)
                pe.wait_ge(ohp_up, q + 1)
                if not first:
                    pe.wait_ge(b_ev, q - OHS + 1)
                for j in range(GRP):
                    i = pe.matmul(psum[:, 2 + 2 * s + j // 4, (j % 4) * P:(j % 4 + 1) * P], f(oh[:, s, 0, j, :]), oh_g[:, s, j, :],
                                  start=True, stop=True)
                i.then_inc(b_done, 1)

            for q in range(OHS):
                gate_group(q, q, True)
            with pe.Fori(1, NQ // OHS) as i:
                for s in range(OHS):
                    gate_group(OHS * i + s, s)
            for q in range(Q_LAST, NQ):
                gate_group(q, q % OHS)

            def turn_u(s, landed):
                pe.wait_ge(ld_u[s], landed)
                for k in range(DK):
                    i = pe.transpose(psum[:, k // 4, (k % 4) * P:(k % 4 + 1) * P], u_raw[:, s, k, :], ident)
                i.then_inc(t_done, 1)

            def up(s):
                product(psum[:, 2 + s, 0:SEQ], lambda a, k: ut[:, a, k, :], lambda b, k: ht[:, b, k, :], a_done)

            def down(s, first, last):
                for t in range(2):
                    for n in range(2):
                        for m, (a, b) in enumerate(((0, 0), (0, 1), (1, 0))):
                            i = pe.matmul(psum[:, 4 + 2 * t + n, :], g_sp[:, s, a, t * P:(t + 1) * P],
                                          v_sp[:, s, b, n * 512:(n + 1) * 512], start=(first and m == 0), stop=(last and m == 2))
                i.then_inc(c_done, 1)

            def turn(b, s, first, last, more=True):
                if more:
                    pe.wait_ge(ut_lo, b + 1)
                    turn_u(1 - s, 8 * b + 16 + 8 * s)
                pe.wait_ge(g_lo, b)
                pe.wait_ge(v_lo, b)
                down(1 - s, first, last)
                if more:
                    pe.wait_ge(ut_lo, b + 2)
                    pe.wait_ge(a_gel, b)
                    up(1 - s)

            for b in range(2):
                if b:
                    pe.wait_ge(ut_lo, 1)
                turn_u(b, 16)
                pe.wait_ge(ut_lo, b + 1)
                if b == 0:
                    pe.wait_ge(b_ev, NQ)
                up(b)
            turn(1, 1, True, False)
            turn(2, 0, False, False)
            with pe.Fori(1, NK // 2 - 1) as i:
                turn(2 * i + 1, 1, False, False)
                turn(2 * i + 2, 0, False, False)
            turn(NK - 1, 1, False, False, more=False)
            turn(NK, 0, False, True, more=False)


_INS = ['x', 'meta_tokens', 'norm1_g', 'w_in', 'q_norm_g', 'k_norm_g', 'pool_w', 'pool_scale', 'w_out', 'norm2_g',
        'peer_wq', 'sub_keys1', 'sub_keys2', 'peer_u', 'peer_v']


def constants():
    import numpy as np
    c = np.zeros((P, N_CONST), np.float32)
    c[:, K_ID:K_ID + P] = np.eye(P)
    c[:, K_IOTA:K_IOTA + P] = np.arange(P)
    inv = (np.float32(10000.0) ** (-np.arange(0, HD, 2, dtype=np.float32) / np.float32(HD))).astype(np.float32)
    ang = (np.arange(T, dtype=np.float32)[:, None] * inv[None, :]).astype(np.float32)
    cs = np.cos(ang.astype(np.float64)).astype(np.float32)
    sn = np.sin(ang.astype(np.float64)).astype(np.float32)
    for n, (first, r) in enumerate(((0, META), (META, P), (META + P, P))):
        for at, a, b in ((K_COS, cs, cs), (K_SIN, -sn, sn)):
            c[0:r, at + n * HD:at + n * HD + HD // 2] = a[first:first + r]
            c[0:r, at + n * HD + HD // 2:at + (n + 1) * HD] = b[first:first + r]
    band = np.zeros((P, 3, 4, P), np.float32)
    for g, w in enumerate((2, 4, 8, 16)):
        for t in range(P):
            for s in range(t - w + 1, t + 1):
                if s >= 0:
                    band[s, 0, g, t] += 1.0 / w
                else:
                    band[P + s, 1, g, t] += 1.0 / w
                    band[META + s, 2, g, t] += 1.0 / w
            band[t, 0, g, t] -= 1.0
    c[:, K_BAND:] = band.reshape(P, -1)
    return c


def kernel(**inputs):
    import numpy as _np
    import concourse.bacc as _bacc
    from concourse import mybir as _mybir
    from concourse.bass_utils import run_bass_kernel_spmd as _run

    nc = _bacc.Bacc("TRN2", target_bir_lowering=False, num_devices=1)
    arrays, args = {}, []
    for name in _INS + ["const"]:
        a = constants() if name == "const" else _np.ascontiguousarray(inputs[name])
        arrays[f"in_{name}_dram"] = a
        args.append(nc.dram_tensor(f"in_{name}_dram", a.shape, _mybir.dt.from_np(a.dtype), kind="ExternalInput").ap())
    args.append(nc.dram_tensor("out_0_dram", (1, SEQ, D), _mybir.dt.float32, kind="ExternalOutput").ap())
    layer(nc, *args)
    r = _run(nc, [arrays], core_ids=[0])
    return r.results[0]["out_0_dram"]
```

```python
import concourse.bass as bass
from concourse import mybir
from contextlib import ExitStack

F32 = mybir.dt.float32
F32R = mybir.dt.float32r
U32 = mybir.dt.uint32
BF16 = mybir.dt.bfloat16
ALU = mybir.AluOpType
ACT = mybir.ActivationFunctionType
AX = mybir.AxisListType
ds = bass.ds

P = 128
SEQ, META = 256, 16
T = SEQ + META
D = 1024
DK = D // P
HD, NH = 64, 8
PAIRS = NH // 2
KSEL = 64
EPS = 1e-6
NEG = -3.0e38
NK = 128
PH, TOPK = 8, 16
GRP = 8
NQ, OHS = SEQ // GRP, 3
Q_LAST = NQ // OHS * OHS
ACT_T = 4
CW = 256

KEYS = [META + P, META + 2 * P]
KOFF = [0, KEYS[0]]
KALL = KEYS[0] + KEYS[1]

STAIRS, off = [], 0
for first, rows in ((0, 1), (1, 1), (2, 1), (3, 1), (4, 1), (5, 3), (8, 8)):
    cols = TOPK // (first + 1)
    STAIRS.append((first, rows, cols, off))
    off += rows * cols
NCAND = off

FOLDED = PH - 2
CAT_BANK = [2, 7]
C_Q, C_K, C_V, C_POOL, C_IQ, C_IK = 0, 512, 1024, 1536, 2048, 2560
CI = HD + NH
W_IN = [C_IK, C_IQ, C_IQ + CW, C_Q, C_Q + CW, C_K, C_K + CW, C_V, C_V + CW, C_POOL, C_POOL + CW]
N_IN, N_OUT, N_WQ = len(W_IN), D // CW, PH
N_CHUNK = N_IN + N_OUT + N_WQ
OUT0, WQ0 = N_IN, N_IN + N_OUT
K_ID, K_IOTA, K_COS, K_SIN, K_BAND = 0, 128, 256, 448, 640
N_CONST = K_BAND + 3 * 4 * P


def by_vector(c):
    return c in (3, 9, 13) or c % 2 == 0 and c < WQ0


def chunk_tiles(c):
    return (3 if c == 0 or 5 <= c < N_IN else 2) if c < WQ0 else 1


def z_after(c):
    return sum(chunk_tiles(k) for k in range(c + 1))


class Count:

    def __init__(self):
        self.n = 0

    def up(self):
        self.n += 1
        return self.n


def layer(nc, x, meta, g1, w_in, gq, gk, pool_w, pool_s, w_out, g2, wq, sk1, sk2, pu, pv, const, out):
    ctx = ExitStack()
    with ctx:
        def sb(name, shape, dt=F32):
            return ctx.enter_context(nc.sbuf_tensor(name, shape, dt))

        def sem(name):
            return ctx.enter_context(nc.semaphore(name))

        big = sb("big", [P, NK * SEQ])
        gates = big[:, :].rearrange("p (n t) -> p n t", t=SEQ)
        rr = sb("rr", [P, 8448], F32R)
        ht = sb("ht", [P, 2, DK, SEQ], F32R)
        raw = sb("raw", [P, 5120])
        cst = sb("cst", [P, 256])
        picks = sb("picks", [P, 3, SEQ])
        gel = sb("gel", [P, 2, SEQ])
        psum = ctx.enter_context(nc.psum_tensor("psum", [P, 8, 512], F32))
        h_dram = nc.dram_tensor("h_kept", [2, P, D], F32, kind="Internal").ap()

        at = 0

        def take(n):
            nonlocal at
            at += n
            assert at <= NK * SEQ
            return big[:, at - n:at]

        xt = take(2 * D).rearrange("p (t d) -> p t d", t=2)
        xm = take(D)
        xs_at = at
        xs = take(3 * D).rearrange("p (t d) -> p t d", t=3)
        t32 = take(DK * SEQ).rearrange("p (k t) -> p k t", k=DK)
        t32m = take(DK * META).rearrange("p (k t) -> p k t", k=DK)
        wraw = take(3 * DK * CW).rearrange("p (s k n) -> p s k n", s=3, k=DK)
        z_at = at
        zq = take(2 * 512).rearrange("p (t n) -> p t n", t=2)
        ziq = take(2 * 512).rearrange("p (t n) -> p t n", t=2)
        zk = take(3 * 512).rearrange("p (t n) -> p t n", t=3)
        zv = take(3 * 512).rearrange("p (t n) -> p t n", t=3)
        zp = take(3 * 512).rearrange("p (t n) -> p t n", t=3)
        zi = take(3 * CI).rearrange("p (t n) -> p t n", t=3)
        rot_at = at
        qr = take(2 * 512).rearrange("p (t n) -> p t n", t=2)
        kr = take(3 * 512).rearrange("p (t n) -> p t n", t=3)
        tmp = take(3 * 512).rearrange("p (a n) -> p a n", a=3)
        iqr = take(2 * 512).rearrange("p (t n) -> p t n", t=2)
        kir = take(3 * P).rearrange("p (t n) -> p t n", t=3)
        stat = take(256)
        cossin = take(6 * HD)
        cos, sin = (cossin[:, a * 3 * HD:(a + 1) * 3 * HD].rearrange("p (t n) -> p t n", t=3) for a in range(2))
        gqk = take(2 * HD).rearrange("p (a n) -> p a n", a=2)
        score = take(KALL)
        work = take(KALL)
        bias = take(KALL)
        tops = take(16).rearrange("p (t n) -> p t n", t=2)
        grow = take(P)
        zt = take(T)
        at = max(at, NK * SEQ - 640)
        ksub = take(2 * P).rearrange("p (a n) -> p a n", a=2)
        kt_sub = take(2 * P).rearrange("p (a n) -> p a n", a=2)
        gains = take(20)
        half = take(1)
        scal = take(64)
        rel = big[:, rot_at:rot_at + NH * KALL]
        at = xs_at
        iqt = take(PAIRS * SEQ).rearrange("p (a t) -> p a t", a=PAIRS)
        kit = take(T)
        qt = take(PAIRS * SEQ).rearrange("p (a t) -> p a t", a=PAIRS)
        kt = take(PAIRS * T).rearrange("p (a t) -> p a t", a=PAIRS)
        yt = take(4 * SEQ).rearrange("p (a t) -> p a t", a=4)
        p32 = iqt
        at = z_at
        qp = take(2 * 2 * SEQ).rearrange("p (s a t) -> p s a t", s=2, a=2)
        sc = take(PH * 4 * NK).rearrange("p (h t a n) -> p h t a n", h=PH, t=2, a=2)
        v16 = take(PH * 64).rearrange("p (h t a k) -> p h t a k", h=PH, t=2, a=2)
        i16 = take(PH * 64).rearrange("p (h t a k) -> p h t a k", h=PH, t=2, a=2).bitcast(U32)
        n16 = take(PH * 64).rearrange("p (h t a k) -> p h t a k", h=PH, t=2, a=2)
        cand = take(PH * 2 * NCAND).rearrange("p (h t c) -> p h t c", h=PH, t=2)
        cide = take(PH * 2 * NCAND).rearrange("p (h t c) -> p h t c", h=PH, t=2)
        vtop = take(PH * 32).rearrange("p (t h k) -> p t h k", h=PH, t=2)
        ptop = take(PH * 32).rearrange("p (t h k) -> p t h k", h=PH, t=2).bitcast(U32)
        eid = take(PH * 32).rearrange("p (t h k) -> p t h k", h=PH, t=2)
        eqs = take(2 * 2 * TOPK * NCAND).rearrange("p (s t c k) -> p s t c k", s=2, t=2, k=TOPK)
        eq16 = take(2 * TOPK * NCAND).bitcast(BF16).rearrange("p (s t c k) -> p s t c k", s=2, t=2, k=TOPK)
        tab16 = take(TOPK * NCAND // 2).bitcast(BF16).rearrange("p (c k) -> p c k", k=TOPK)
        p16 = take(PH * 16).bitcast(BF16).rearrange("p (t h k) -> p t h k", h=PH, t=2)
        pick3 = take(3 * PH * 32).rearrange("p (a t h k) -> p a t h k", a=3, t=2, h=PH)
        eint = take(PH * 32).rearrange("p (t h k) -> p t h k", h=PH, t=2).bitcast(mybir.dt.int32)
        fint = take(PH * 32).rearrange("p (t h k) -> p t h k", h=PH, t=2).bitcast(mybir.dt.int32)
        assert at <= NK * SEQ - 640

        ident, iota = cst[:, 0:P], cst[:, P:2 * P]
        ixrel = raw[:, 0:NH * KALL]
        tmp_p = raw[:, 5120 - 3 * 512:5120].rearrange("p (a n) -> p a n", a=3)
        band = raw[:, 0:3 * 512].rearrange("p (a g t) -> p a g t", a=3, g=4)
        poolw = raw[:, 3072:3584].rearrange("p (g d) -> p g d", g=4)
        pt = raw[:, :].rearrange("p (c h q) -> p c h q", c=5, h=NH)
        u_raw = raw[:, 0:2 * D].rearrange("p (s k c) -> p s k c", s=2, k=DK)
        v_raw = raw[:, 2 * D:4 * D].rearrange("p (s d) -> p s d", s=2)
        oh_g = raw[:, 2 * D:5 * D].rearrange("p (s q n) -> p s q n", s=OHS, q=GRP)
        w_sp = rr[:, 0:8192].rearrange("p (s a k n) -> p s a k n", s=2, a=2, k=DK)
        hm = rr[:, 8192:8448].rearrange("p (a k t) -> p a k t", a=2, k=DK)
        ut = rr[:, 0:2 * D].rearrange("p (a k n) -> p a k n", a=2, k=DK)
        v_sp = rr[:, 2 * D:6 * D].rearrange("p (s a d) -> p s a d", s=2, a=2)
        oh = rr[:, 2 * D:8 * D].rearrange("p (s a q n) -> p s a q n", s=OHS, a=2, q=GRP)
        g_sp = rr[:, 6 * D:7 * D].rearrange("p (s a t) -> p s a t", s=2, a=2)

        def f(ap):
            return ap.bitcast(F32)

        rows = [P, P, META]
        trow = [1, 2, 0]

        ld_x = [sem(f"ld_x{t}") for t in range(3)]
        ld_cst, ld_rope, ld_small, ld_g2, ld_band = (sem(n) for n in ("ld_cst", "ld_rope", "ld_small", "ld_g2", "ld_band"))
        ld_w = [sem(f"ld_w{s}") for s in range(3)]
        ld_u = [sem(f"ld_u{s}") for s in range(2)]
        ld_v = [sem(f"ld_v{s}") for s in range(2)]
        ld_h = sem("ld_h")
        st_h, st_out = sem("st_h"), sem("st_out")
        a_sq, a_xs, a_hi, w_hi, z_ev = sem("a_sq"), sem("a_xs"), sem("a_hi"), sem("w_hi"), sem("z_ev")
        ix_tr, a_rel, y_ev, pc_hi, qk_tr = sem("ix_tr"), sem("a_rel"), sem("y_ev"), sem("pc_hi"), sem("qk_tr")
        a_exp, pt_ev, cat_hi, qp_ev, s_ev = sem("a_exp"), sem("pt_ev"), sem("cat_hi"), sem("qp_ev"), sem("s_ev")
        a_soft, b_ev, ut_hi, v_hi, a_gel = sem("a_soft"), sem("b_ev"), sem("ut_hi"), sem("v_hi"), sem("a_gel")
        ks_ev, pk_ev, ohg_up, zt_ev = sem("ks_ev"), sem("pk_ev"), sem("ohg_up"), sem("zt_ev")
        d_ms, d_t32, d_lo, w_lo_e, d_seq = sem("d_ms"), sem("d_t32"), sem("d_lo"), sem("w_lo_e"), sem("d_seq")
        d_ki, d_iq, d_qst, a_kst, d_qk = sem("d_ki"), sem("d_iq"), sem("d_qst"), sem("a_kst"), sem("d_qk")
        d_p32, pc_lo, d_log, d_max, d_prob = sem("d_p32"), sem("pc_lo"), sem("d_log"), sem("d_max"), sem("d_prob")
        cat_lo, h_ev, d_top, d_match, d_sub = sem("cat_lo"), sem("h_ev"), sem("d_top"), sem("d_match"), sem("d_sub")
        d_pick, oh_up, ut_lo, v_lo, g_lo = sem("d_pick"), sem("oh_up"), sem("ut_lo"), sem("v_lo"), sem("g_lo")
        d_g32, d_out = sem("d_g32"), sem("d_out")
        d_xs = sem("d_xs")
        d_place, n_ev = sem("d_place"), sem("n_ev")
        d_rel, p_qk = sem("d_rel"), sem("p_qk")
        p_cand, p_cide = sem("p_cand"), sem("p_cide")
        p_half, p_rs, w_lo_o, p_seq, p_eq, ohp_up = (sem(n) for n in ("p_half", "p_rs", "w_lo_o", "p_seq", "p_eq", "ohp_up"))
        pe_x, z_done, pe_ix, pe_sc, pe_y = sem("pe_x"), sem("z_done"), sem("pe_ix"), sem("pe_sc"), sem("pe_y")
        pe_qk, pe_log, pe_pt, pe_cat, pe_ks = sem("pe_qk"), sem("pe_log"), sem("pe_pt"), sem("pe_cat"), sem("pe_ks")
        pe_gain, pe_zt = sem("pe_gain"), sem("pe_zt")
        pe_s, pe_pk, b_done, t_done, a_done, c_done = (sem(n) for n in ("pe_s", "pe_pk", "b_done", "t_done", "a_done", "c_done"))

        pu_v = pu[0].rearrange("(n m) d -> n m d", m=NK)
        pv_v = pv[0].rearrange("(n m) d -> n m d", m=NK)

        def w_src(c):
            w, first = (w_in, W_IN[c]) if c < OUT0 else (w_out, (c - OUT0) * CW) if c < WQ0 else (wq, (c - WQ0) * CW)
            n = CI if c == 0 else CW
            return w[0, :, first:first + n].rearrange("(k p) n -> p k n", p=P), n

        def w_cols(c):
            return CI if c == 0 else CW

        def lo_ready(eng, c):
            mine = [k for k in range(1, c + 1) if k != WQ0 and by_vector(k) == by_vector(c)]
            eng.wait_ge(w_lo_e if by_vector(c) else w_lo_o, len(mine))

        block = ctx.enter_context(nc.Block())

        @block.sync
        def _(sp):
            def load_w(c):
                if c == 3 or c >= WQ0 + 3:
                    sp.wait_ge(z_done, z_after(c - 3))
                elif c > 3:
                    sp.wait_ge(w_hi, c - 3)
                    lo_ready(sp, c - 3)
                src, n = w_src(c)
                sp.dma_start(wraw[:, c % 3, :, 0:n], src).then_inc(ld_w[c % 3], 16)

            sp.dma_start(xt[:, 0, :], x[0, 0:P, :]).then_inc(ld_x[0], 16)
            sp.dma_start(xt[:, 1, :], x[0, P:2 * P, :]).then_inc(ld_x[1], 16)
            sp.dma_start(xm[0:META, :], meta[:, :]).then_inc(ld_x[2], 16)
            load_w(0)
            sp.dma_start(cst[:, :], const[:, 0:K_COS]).then_inc(ld_cst, 16)
            load_w(1)
            load_w(2)
            sp.dma_start(cossin, const[:, K_COS:K_BAND]).then_inc(ld_rope, 16)
            for c in range(3, 6):
                load_w(c)
            for c in range(6, 9):
                load_w(c)
            sp.wait_ge(d_rel, 2)
            sp.dma_start(band, const[:, K_BAND:N_CONST].rearrange("p (a g t) -> p a g t", a=3, g=4)).then_inc(ld_band, 16)
            sp.dma_start(poolw, pool_w[0].rearrange("g c d -> c g d")).then_inc(ld_band, 16)
            sp.dma_start(ksub[:, 0, :], sk1[0]).then_inc(ld_g2, 16)
            sp.dma_start(ksub[:, 1, :], sk2[0]).then_inc(ld_g2, 16)
            for c in range(9, OUT0 + 4):
                load_w(c)
            for c in range(OUT0 + 4, WQ0 + 4):
                load_w(c)
            sp.wait_ge(h_ev, 2 * N_OUT)
            for t in range(2):
                sp.dma_start(h_dram[t], xt[:, t, :]).then_inc(st_h, 16)
            for c in range(WQ0 + 4, N_CHUNK):
                load_w(c)
            sp.wait_ge(pe_cat, 2)
            for s in range(2):
                sp.dma_start(u_raw[:, s], pu_v[:, s, :].rearrange("p (k c) -> p k c", k=DK)).then_inc(ld_u[s], 16)
            for s in range(2):
                sp.wait_ge(b_done, NQ - 1 + s)
                sp.dma_start(v_raw[:, s, :], pv_v[:, s, :]).then_inc(ld_v[s], 16)
            with sp.Fori(0, NK // 2 - 1) as i:
                for s in range(2):
                    sp.wait_ge(t_done, 2 * i + (s + 1))
                    sp.dma_start(u_raw[:, s], pu_v[:, ds(2 * i + (s + 2), 1), :].rearrange("p o (k c) -> p (o k) c", k=DK))\
                      .then_inc(ld_u[s], 16)
                    sp.wait_ge(v_hi, 2 * i + (s + 1))
                    sp.wait_ge(v_lo, 2 * i + (s + 1))
                    sp.dma_start(v_raw[:, s, :], pv_v[:, ds(2 * i + (s + 2), 1), :].rearrange("p o d -> p (o d)"))\
                      .then_inc(ld_v[s], 16)
            sp.wait_ge(st_h, 32)
            sp.wait_ge(t_done, NK)
            for t in range(2):
                sp.dma_start(raw[:, t * D:(t + 1) * D], h_dram[t]).then_inc(ld_h, 16)
            for t in range(2):
                sp.wait_ge(d_out, 2 * t + 2)
                sp.dma_start(out[0, t * P:(t + 1) * P, :], big[:, t * D:(t + 1) * D]).then_inc(st_out, 16)
            sp.wait_ge(st_out, 32)

        @block.scalar
        def _(act):
            act.dma_start(grow[0:8, :], g1[0].rearrange("(k p) -> k p", p=P)).then_inc(ld_small, 16)
            act.dma_start(grow[8:16, :], g2[0].rearrange("(k p) -> k p", p=P)).then_inc(ld_small, 16)
            act.dma_start(grow[16:20, :], pool_s[0].rearrange("(k p) -> k p", p=P)).then_inc(ld_small, 16)
            act.dma_start(gqk[:, 0, :], gq[0:1, :].to_broadcast([P, HD])).then_inc(ld_small, 16)
            act.dma_start(gqk[:, 1, :], gk[0:1, :].to_broadcast([P, HD])).then_inc(ld_small, 16)

            def split_w(c):
                act.wait_ge(ld_w[c % 3], 16 * (c // 3 + 1))
                if c >= 3:
                    act.wait_ge(z_done, z_after(c - 2 if c - 2 != WQ0 else c - 4))
                n = w_cols(c)
                act.activation(w_sp[:, c % 2, 0, :, 0:n], wraw[:, c % 3, :, 0:n], ACT.Copy).then_inc(w_hi, 1)

            srcs = [xt[:, 0, :], xt[:, 1, :], xm[0:META, :]]
            for t, r in enumerate(rows):
                act.wait_ge(ld_x[t], 16)
                act.activation(xs[0:r, t, :], srcs[t], ACT.Square, accum_out=stat[0:r, t:t + 1]).then_inc(a_sq, 1)
            for t, r in enumerate(rows):
                act.wait_ge(p_rs, t + 1)
                act.wait_ge(a_sq, t + 1)
                act.activation(xs[0:r, t, :], srcs[t], ACT.Copy, scale=scal[0:r, 8 + t:9 + t]).then_inc(a_xs, 1)
            split_w(1)
            for t in range(3):
                act.wait_ge(d_t32, t + 1)
                dst, src = (ht[:, 0, :, t * P:(t + 1) * P], t32[:, :, t * P:(t + 1) * P]) if t < 2 else (hm[:, 0], t32m)
                act.activation(dst, src, ACT.Copy).then_inc(a_hi, 1)
            split_w(2)

            def keep_z(c):
                sec, first = {0: (zi, 0), 1: (ziq, 0), 2: (ziq, CW), 3: (zq, 0), 4: (zq, CW), 5: (zk, 0), 6: (zk, CW),
                              7: (zv, 0), 8: (zv, CW), 9: (zp, 0), 10: (zp, CW)}[c]
                n = w_cols(c)
                for t in range(chunk_tiles(c)):
                    act.wait_ge(z_done, z_after(c) - chunk_tiles(c) + t + 1)
                    r = rows[t]
                    act.activation(sec[0:r, t, first:first + n], psum[0:r, 3 * (c % 2) + t, 0:n], ACT.Copy)\
                       .then_inc(z_ev, 1)

            act.wait_ge(pe_zt, 2)
            act.activation(zt[0:CI, :], psum[0:CI, 5, 0:T], ACT.Copy).then_inc(zt_ev, 1)
            for c in range(5):
                keep_z(c)
                if 0 < c < 4:
                    split_w(c + 2)
            for t in range(2):
                act.wait_ge(pe_ix, t + 1)
                act.activation(iqt[:, :, t * P:(t + 1) * P], psum[:, t, :].rearrange("p (a q) -> p a q", a=PAIRS),
                               ACT.Copy).then_inc(ix_tr, 1)
            act.wait_ge(pe_ix, 3)
            act.activation(kit, psum[:, 2, 0:T], ACT.Copy).then_inc(ix_tr, 1)
            split_w(6)
            act.wait_ge(pe_sc, 2)
            for b0, b1 in ((3, 6), (0, 3), (6, NH)):
                for t in range(2):
                    act.activation(ixrel[:, NH * KOFF[t] + b0 * KEYS[t]:NH * KOFF[t] + b1 * KEYS[t]]
                                   .rearrange("p (h k) -> p h k", h=b1 - b0),
                                   psum[:, b0:b1, KOFF[t]:KOFF[t] + KEYS[t]], ACT.Relu).then_inc(a_rel, 1)
            for c in range(5, N_IN - 1):
                keep_z(c)
                if c < N_IN - 2:
                    split_w(c + 2)
                if c == 6:
                    act.wait_ge(z_ev, z_after(6))
                    for t, r in enumerate(rows):
                        for h in range(NH):
                            at0 = 48 + 8 * t + h
                            act.activation(kr[0:r, t, h * HD:(h + 1) * HD], zk[0:r, t, h * HD:(h + 1) * HD], ACT.Square, scale=HD ** -0.5,
                                           accum_out=stat[0:r, at0:at0 + 1]).then_inc(a_kst, 1)
            for t in range(2):
                act.wait_ge(pe_qk, t + 1)
                act.activation(qt[:, :, t * P:(t + 1) * P], psum[:, t, :].rearrange("p (a q) -> p a q", a=PAIRS),
                               ACT.Copy).then_inc(qk_tr, 1)
            for n, (t, first) in enumerate(((2, 0), (0, META), (1, META + P))):
                act.wait_ge(pe_qk, n + 3)
                r = rows[t]
                act.activation(kt[:, :, first:first + r], psum[:, 2 + n, 0:PAIRS * r].rearrange("p (a q) -> p a q", a=PAIRS),
                               ACT.Copy).then_inc(qk_tr, 1)
            split_w(N_IN)
            for t in range(2):
                act.wait_ge(d_max, t + 1)
                for h in range(NH):
                    a = NH * KOFF[t] + h * KEYS[t]
                    act.activation(rel[:, a:a + KEYS[t]], rel[:, a:a + KEYS[t]], ACT.Exp,
                                   bias=stat[:, 128 + 8 * t + h:129 + 8 * t + h],
                                   accum_out=stat[:, 144 + 8 * t + h:145 + 8 * t + h]).then_inc(a_exp, 1)
                    if t == 1 and h == 4:
                        keep_z(N_IN - 1)
            split_w(N_IN + 1)
            act.wait_ge(pe_y, 1)
            act.activation(yt, psum[:, 6:8, :].rearrange("p t (g q) -> p g t q", g=4), ACT.Copy).then_inc(y_ev, 1)
            for n, (c, b, r) in enumerate(((0, 0, META), (1, 2, P), (2, 4, META), (3, 6, P), (4, 0, P))):
                if n == 2:
                    act.wait_ge(d_p32, 1)
                    act.activation(ht[:, 0, 4:8, :], p32, ACT.Copy).then_inc(pc_hi, 1)
                act.wait_ge(pe_pt, n + 1)
                act.activation(pt[0:r, c].rearrange("p (b h) q -> p b (h q)", b=2), psum[0:r, b:b + 2, :],
                               ACT.Copy).then_inc(pt_ev, 1)
            for t in range(2):
                act.wait_ge(pe_cat, t + 1)
                act.activation(ht[:, 0, 0:4, t * P:(t + 1) * P], psum[:, CAT_BANK[t], :].rearrange("p (a q) -> p a q", a=PAIRS),
                               ACT.Copy).then_inc(cat_hi, 1)
            split_w(OUT0 + 2)
            for n in range(N_OUT):
                for t in range(2):
                    act.wait_ge(h_ev, 2 * n + t + 1)
                    at0 = 200 + N_OUT * t + n
                    act.activation(xs[:, t, n * CW:(n + 1) * CW], xt[:, t, n * CW:(n + 1) * CW], ACT.Square,
                                   accum_out=stat[:, at0:at0 + 1]).then_inc(a_sq, 1)
                if n == 0:
                    split_w(OUT0 + 3)
            act.wait_ge(p_rs, 6)
            act.wait_ge(a_sq, 3 + 2 * N_OUT)
            act.activation(xs[:, 1, :], xt[:, 1, :], ACT.Copy, scale=scal[:, 49:50]).then_inc(a_xs, 1)
            split_w(WQ0 + 1)
            act.wait_ge(pe_ks, 1)
            act.activation(kt_sub, psum[:, 5, 0:2 * P].rearrange("p (a n) -> p a n", a=2), ACT.Copy).then_inc(ks_ev, 1)
            for t in range(2):
                act.wait_ge(d_t32, 3 + t + 1)
                act.activation(ht[:, 0, :, t * P:(t + 1) * P], t32[:, :, t * P:(t + 1) * P], ACT.Copy).then_inc(a_hi, 1)

            split_w(WQ0 + 2)

            def block_u(b):
                act.wait_ge(t_done, b + 1)
                for n in range(2):
                    act.activation(ut[:, 0, 4 * n:4 * n + 4], psum[:, n, :].rearrange("p (k n) -> p k n", n=P), ACT.Copy)\
                       .then_inc(ut_hi, 1)

            def numbers(h):
                act.wait_ge(d_top, h + 1)
                act.activation(n16[:, h, :, 0, :], i16[:, h, :, 0, :], ACT.Copy, scale=float(NK)).then_inc(n_ev, 1)
                act.activation(n16[:, h, :, 1, :], i16[:, h, :, 1, :], ACT.Copy).then_inc(n_ev, 1)

            def keep_s(h):
                act.wait_ge(pe_s, h + 1)
                act.activation(sc[:, h].rearrange("p t a n -> p (t a n)"), psum[:, 3 * ((WQ0 + h) % 2) + 1, :], ACT.Copy)\
                   .then_inc(s_ev, 1)

            for h in range(PH):
                act.wait_ge(z_done, z_after(WQ0 + h))
                if h >= 2:
                    act.wait_ge(pe_s, h - 1)
                act.activation(qp[:, h % 2].rearrange("p a t -> p (a t)"), psum[:, 3 * ((WQ0 + h) % 2), :], ACT.Copy)\
                   .then_inc(qp_ev, 1)
                if h:
                    numbers(h - 1)
                keep_s(h)
            numbers(PH - 1)
            block_u(0)
            act.wait_ge(d_sub, 1)
            act.activation(pick3[:, 2], pick3[:, 2], ACT.Exp).then_inc(a_soft, 1)
            act.wait_ge(pe_pk, 1)
            act.activation(picks[:, 0:2, :].rearrange("p a t -> p (a t)"), psum[:, 6, :], ACT.Copy).then_inc(pk_ev, 1)
            act.wait_ge(pe_pk, 2)
            act.activation(picks[:, 2, :], psum[:, 7, 0:SEQ], ACT.Copy).then_inc(pk_ev, 1)
            def gated(s, tok):
                for j in range(ACT_T):
                    i = act.activation(oh_g[:, s, j, :], f(oh[:, s, 1, j, :]), ACT.Copy, scale=picks[:, 2, ds(tok + j, 1)])
                i.then_inc(ohg_up, 1)

            def keep_gates(s, tok):
                act.activation(gates[:, :, ds(tok, GRP)], psum[:, 2 + 2 * s:4 + 2 * s, :].rearrange("p b (q n) -> p n (b q)", n=NK), ACT.Copy)\
                   .then_inc(b_ev, 1)

            act.wait_ge(pk_ev, 2)

            def gate_group(q, s, first=False):
                act.wait_ge(oh_up, q + 1)
                gated(s, GRP * q)
                if not first:
                    act.wait_ge(b_done, q)
                    keep_gates((s - 1) % OHS, GRP * q - GRP)

            for q in range(OHS):
                gate_group(q, q, q == 0)
            with act.Fori(1, NQ // OHS) as i:
                for s in range(OHS):
                    gate_group(OHS * i + s, s)
            for q in range(Q_LAST, NQ):
                gate_group(q, q % OHS)
            act.wait_ge(b_done, NQ)
            keep_gates((NQ - 1) % OHS, GRP * (NQ - 1))

            def block_v(s, b, first):
                if not first:
                    act.wait_ge(c_done, b - 1)
                act.wait_ge(ld_v[s], v_turn(b, s))
                act.activation(v_sp[:, s, 0, :], v_raw[:, s, :], ACT.Copy).then_inc(v_hi, 1)

            def block_g(s, b, first):
                act.wait_ge(a_done, b + 1)
                if not first:
                    act.wait_ge(d_g32, b - 1)
                act.activation(gel[:, s, :], psum[:, 2 + s, 0:SEQ], ACT.Gelu).then_inc(a_gel, 1)

            def v_turn(b, s):
                return 8 * b + (16 - 8 * s)

            act.wait_ge(a_done, 1)
            block_u(1)
            for b in range(2):
                block_v(b, b, True)
                block_g(b, b, True)
            with act.Fori(1, NK // 2) as i:
                for s in range(2):
                    block_u(2 * i + s)
                    block_v(s, 2 * i + s, False)
                    block_g(s, 2 * i + s, False)

        @block.vector
        def _(dve):
            seq = Count()

            def split_lo(c):
                dve.wait_ge(w_hi, c)
                n = w_cols(c)
                dve.tensor_tensor(w_sp[:, c % 2, 1, :, 0:n], wraw[:, c % 3, :, 0:n], f(w_sp[:, c % 2, 0, :, 0:n]), ALU.subtract)\
                   .then_inc(w_lo_e, 1)

            for t, r in enumerate(rows):
                dve.wait_ge(a_sq, t + 1)
                dve.tensor_scalar(scal[0:r, t:t + 1], stat[0:r, t:t + 1], 1.0 / D, EPS, ALU.mult, ALU.add).then_inc(d_ms, 1)
            dve.wait_ge(pe_gain, 1)
            dve.tensor_copy(gains, psum[:, 5, 0:20]).then_inc(d_seq, 1)
            dve.wait_ge(d_seq, seq.up())
            gain = [gains[:, 0:8], gains[:, 8:16]]
            for t, r in enumerate(rows):
                dve.wait_ge(pe_x, t + 1)
                dst = t32[:, :, t * P:(t + 1) * P] if t < 2 else t32m
                src = (psum[:, 2 * t:2 * t + 2, :].rearrange("p b (k n) -> p (b k) n", n=P) if t < 2
                       else psum[:, 4, 0:DK * META].rearrange("p (k n) -> p k n", n=META))
                dve.tensor_tensor(dst, src, gain[0].unsqueeze(2).to_broadcast([P, DK, r]), ALU.mult).then_inc(d_t32, 1)
            for t in range(3):
                dve.wait_ge(d_t32, t + 1)
                dve.wait_ge(a_hi, t + 1)
                hi, lo, src = ((ht[:, 0, :, t * P:(t + 1) * P], ht[:, 1, :, t * P:(t + 1) * P], t32[:, :, t * P:(t + 1) * P])
                               if t < 2 else (hm[:, 0], hm[:, 1], t32m))
                dve.tensor_tensor(lo, src, f(hi), ALU.subtract).then_inc(d_lo, 1)
            split_lo(2)

            def rope(r, t, src, nh, dsts, done):
                s3 = src.rearrange("p (h d) -> p h d", h=nh)
                c3 = cos[0:r, trow[t], :].unsqueeze(1).to_broadcast([r, nh, HD])
                n3 = sin[0:r, trow[t], :].unsqueeze(1).to_broadcast([r, nh, HD])
                a3 = tmp[0:r, 0, 0:nh * HD].rearrange("p (h d) -> p h d", h=nh)
                b3 = tmp[0:r, 1, 0:nh * HD].rearrange("p (h d) -> p h d", h=nh)
                hh = HD // 2
                dve.tensor_tensor(a3, s3, c3, ALU.mult).then_inc(d_seq, 1)
                seq.up()
                dve.tensor_tensor(b3[:, :, 0:hh], s3[:, :, hh:HD], n3[:, :, 0:hh], ALU.mult).then_inc(d_seq, 1)
                seq.up()
                dve.tensor_tensor(b3[:, :, hh:HD], s3[:, :, 0:hh], n3[:, :, hh:HD], ALU.mult).then_inc(d_seq, 1)
                dve.wait_ge(d_seq, seq.up())
                for d in dsts:
                    dve.tensor_tensor(d.rearrange("p (h d) -> p h d", h=nh), a3, b3, ALU.add).then_inc(done, 1)

            dve.wait_ge(ld_rope, 16)
            dve.wait_ge(z_ev, 3)
            for n, t in enumerate((0, 1, 2)):
                r = rows[t]
                rope(r, t, zi[0:r, t, 0:HD], 1, [kir[0:r, t, 0:HD], kir[0:r, t, HD:P]], d_ki)
                dve.wait_ge(d_ki, 2 * n + 2)
            dve.tensor_scalar(scal[:, 16:32].rearrange("p (t h) -> p t h", t=2), zi[:, 0:2, HD:CI],
                              NH ** -0.5 * HD ** -0.5, None, ALU.mult).then_inc(d_seq, 1)
            seq.up()
            split_lo(3)
            split_lo(4)
            dve.wait_ge(z_ev, z_after(2))
            for t in range(2):
                rope(P, t, ziq[:, t, :], NH, [iqr[:, t, :]], d_iq)
                dve.wait_ge(d_iq, t + 1)

            def head_means(t, src, at0, done):
                r = rows[t]
                dve.tensor_tensor(tmp[0:r, 2, :], src, src, ALU.mult).then_inc(d_seq, 1)
                dve.wait_ge(d_seq, seq.up())
                dve.tensor_reduce(stat[0:r, at0:at0 + 8], tmp[0:r, 2, :].rearrange("p (h d) -> p h d", h=NH), AX.X, ALU.add)\
                   .then_inc(d_seq, 1)
                dve.wait_ge(d_seq, seq.up())
                dve.tensor_scalar(stat[0:r, at0:at0 + 8], stat[0:r, at0:at0 + 8], 1.0 / HD, EPS, ALU.mult, ALU.add)\
                   .then_inc(done, 1)

            dve.wait_ge(z_ev, z_after(4))
            for t in range(2):
                head_means(t, zq[:, t, :], 32 + 8 * t, d_qst)
            split_lo(6)
            for t in range(2):
                dve.wait_ge(a_rel, 5 + t)
                k = KEYS[t]
                acc = score[:, KOFF[t]:KOFF[t] + k]
                for h in range(NH):
                    part = ixrel[:, NH * KOFF[t] + h * k:NH * KOFF[t] + (h + 1) * k]
                    w = scal[:, 16 + 8 * t + h:17 + 8 * t + h]
                    if h == 0:
                        dve.tensor_scalar(acc, part, w, None, ALU.mult).then_inc(d_seq, 1)
                    else:
                        i = dve.scalar_tensor_tensor(acc, part, w, acc, ALU.mult, ALU.add)
                        if h == NH - 1:
                            i.then_inc(d_rel, 1)
                            dve.wait_ge(d_rel, t + 1)
                            break
                        i.then_inc(d_seq, 1)
                    dve.wait_ge(d_seq, seq.up())
                dve.memset(acc[0:KSEL, k - 64:k], NEG).then_inc(d_seq, 1)
                dve.wait_ge(d_seq, seq.up())

            parts = [[m[:, KOFF[t]:KOFF[t] + KEYS[t]] for m in (score, work, bias)] for t in range(2)]
            for n in range(KSEL // 8):
                for t, (a, w, b) in enumerate(parts):
                    if n:
                        dve.wait_ge(d_seq, seq.n - 1)
                    dve.max(tops[:, t, :], a if n == 0 else w).then_inc(d_seq, 1)
                    seq.up()
                for t, (a, w, b) in enumerate(parts):
                    dve.wait_ge(d_seq, seq.n - 1)
                    dve.match_replace(w, tops[:, t, :], a if n == 0 else w, NEG).then_inc(d_seq, 1)
                    seq.up()
                if n == KSEL // 8 - 2:
                    split_lo(8)
            for t, (a, w, b) in enumerate(parts):
                dve.wait_ge(d_seq, seq.n - 1)
                dve.tensor_tensor(b, w, a, ALU.is_equal).then_inc(d_seq, 1)
                seq.up()
            for t, (a, w, b) in enumerate(parts):
                dve.wait_ge(d_seq, seq.n - 1)
                dve.tensor_scalar(b, b, -1.0e30, None, ALU.mult).then_inc(d_seq, 1)
                seq.up()
            split_lo(9)

            def norm_rope(t, src, gi, at0, dst):
                r = rows[t]
                m = tmp[0:r, 2, :]
                m3 = m.rearrange("p (h d) -> p h d", h=NH)
                dve.tensor_tensor(m3, src.rearrange("p (h d) -> p h d", h=NH),
                                  stat[0:r, at0:at0 + 8].unsqueeze(2).to_broadcast([r, NH, HD]), ALU.mult).then_inc(d_seq, 1)
                dve.wait_ge(d_seq, seq.up())
                dve.tensor_tensor(m3, m3, gqk[0:r, gi, :].unsqueeze(1).to_broadcast([r, NH, HD]), ALU.mult).then_inc(d_seq, 1)
                dve.wait_ge(d_seq, seq.up())
                rope(r, t, m, NH, [dst], d_qk)

            dve.wait_ge(p_rs, 5)
            for n, t in enumerate((2, 1)):
                r = rows[t]
                norm_rope(t, zk[0:r, t, :], 1, 96 + 8 * t, kr[0:r, t, :])
                dve.wait_ge(d_qk, 1 + n)
            split_lo(10)
            dve.wait_ge(pe_log, 2)
            for b0, b1 in ((0, 3), (3, NH)):
                for t in range(2):
                    k = KEYS[t]
                    lg = rel[:, NH * KOFF[t]:NH * (KOFF[t] + k)].rearrange("p (h k) -> p h k", h=NH)
                    dve.scalar_tensor_tensor(lg[:, b0:b1], psum[:, b0:b1, KOFF[t]:KOFF[t] + k], HD ** -0.5,
                                             bias[:, KOFF[t]:KOFF[t] + k].unsqueeze(1).to_broadcast([P, b1 - b0, k]),
                                             ALU.mult, ALU.add).then_inc(d_log, 1)
            for t in range(2):
                k = KEYS[t]
                lg = rel[:, NH * KOFF[t]:NH * (KOFF[t] + k)].rearrange("p (h k) -> p h k", h=NH)
                dve.wait_ge(d_log, t + 3)
                dve.tensor_reduce(stat[:, 128 + 8 * t:136 + 8 * t], lg, AX.X, ALU.max, negate=True).then_inc(d_max, 1)
            for t in range(2):
                k = KEYS[t]
                lg = rel[:, NH * KOFF[t]:NH * (KOFF[t] + k)].rearrange("p (h k) -> p h k", h=NH)
                dve.wait_ge(a_exp, NH * (t + 1))
                dve.reciprocal(stat[:, 160 + 8 * t:168 + 8 * t], stat[:, 144 + 8 * t:152 + 8 * t]).then_inc(d_seq, 1)
                dve.wait_ge(d_seq, seq.up())
                dve.tensor_tensor(lg, lg, stat[:, 160 + 8 * t:168 + 8 * t].unsqueeze(2).to_broadcast([P, NH, k]), ALU.mult)\
                   .then_inc(d_prob, 1)
            dve.wait_ge(pe_y, 2)
            dve.tensor_tensor(p32, psum[:, 6:8, :].rearrange("p b (g t) -> p (b g) t", t=SEQ),
                              gains[:, 16:20].unsqueeze(2).to_broadcast([P, 4, SEQ]), ALU.mult).then_inc(d_p32, 1)
            dve.wait_ge(pc_hi, 1)
            dve.tensor_tensor(ht[:, 1, 4:8, :], p32, f(ht[:, 0, 4:8, :]), ALU.subtract).then_inc(pc_lo, 1)
            split_lo(12)
            for t in range(2):
                dve.wait_ge(cat_hi, t + 1)
                dve.tensor_tensor(ht[:, 1, 0:4, t * P:(t + 1) * P], psum[:, CAT_BANK[t], :].rearrange("p (a q) -> p a q", a=PAIRS),
                                  f(ht[:, 0, 0:4, t * P:(t + 1) * P]), ALU.subtract).then_inc(cat_lo, 1)
            for c in range(OUT0, WQ0):
                for t in range(2):
                    dve.wait_ge(z_done, z_after(c) - 1 + t)
                    n = (c - OUT0) * CW
                    dve.tensor_tensor(xt[:, t, n:n + CW], xt[:, t, n:n + CW], psum[:, 3 * (c % 2) + t, 0:CW], ALU.add)\
                       .then_inc(h_ev, 1)
                if c in (OUT0, OUT0 + 1):
                    split_lo(c + 2)
            dve.wait_ge(a_sq, 3 + 2 * N_OUT)
            dve.tensor_reduce(scal[:, 3:5], stat[:, 200:200 + 2 * N_OUT].rearrange("p (t n) -> p t n", t=2), AX.X, ALU.add)\
               .then_inc(d_seq, 1)
            dve.wait_ge(d_seq, seq.up())
            dve.tensor_scalar(scal[:, 3:5], scal[:, 3:5], 1.0 / D, EPS, ALU.mult, ALU.add).then_inc(d_ms, 1)
            dve.wait_ge(p_rs, 6)
            dve.tensor_scalar(xs[:, 0, :], xt[:, 0, :], scal[:, 48:49], None, ALU.mult).then_inc(d_xs, 1)
            for t, b in enumerate((6, 0)):
                dve.wait_ge(pe_x, 3 + t + 1)
                dve.tensor_tensor(t32[:, :, t * P:(t + 1) * P], psum[:, b:b + 2, :].rearrange("p b (k n) -> p (b k) n", n=P),
                                  gain[1].unsqueeze(2).to_broadcast([P, DK, P]), ALU.mult).then_inc(d_t32, 1)
            for t in range(2):
                dve.wait_ge(a_hi, 3 + t + 1)
                dve.tensor_tensor(ht[:, 1, :, t * P:(t + 1) * P], t32[:, :, t * P:(t + 1) * P],
                                  f(ht[:, 0, :, t * P:(t + 1) * P]), ALU.subtract).then_inc(d_lo, 1)

            dve.tensor_copy(tab16, iota[:, 0:NCAND].unsqueeze(2).to_broadcast([P, NCAND, TOPK])).then_inc(d_seq, 1)
            seq.up()

            def top16(parts, done):
                for n in range(2):
                    at = slice(8 * n, 8 * n + 8)
                    n0 = seq.n
                    for k, (vals, idx, src) in enumerate(parts):
                        if n:
                            dve.wait_ge(d_seq, n0 - len(parts) + k + 1)
                        dve.max(vals[:, at], src).then_inc(d_seq, 1)
                        seq.up()
                    for k, (vals, idx, src) in enumerate(parts):
                        dve.wait_ge(d_seq, n0 + k + 1)
                        i = dve.max_index(idx[:, at], vals[:, at], src)
                        if n and k == len(parts) - 1:
                            i.then_inc(done, 1)
                        else:
                            i.then_inc(d_seq, 1)
                            seq.up()
                    for k, (vals, idx, src) in enumerate(parts if n == 0 else []):
                        dve.wait_ge(d_seq, n0 + len(parts) + k + 1)
                        dve.match_replace(src, vals[:, at], src, NEG).then_inc(d_seq, 1)
                        seq.up()

            def best_keys(h):
                dve.wait_ge(s_ev, h + 1)
                top16([(v16[:, h, t, a, :], i16[:, h, t, a, :], sc[:, h, t, a, :]) for t in range(2) for a in range(2)], d_top)

            def best_pairs(h):
                dve.wait_ge(p_cand, h + 1)
                top16([(vtop[:, t, h, :], ptop[:, t, h, :], cand[:, h, t, :]) for t in range(2)], d_place)
                dve.wait_ge(d_seq, seq.n)
                dve.wait_ge(d_place, h + 1)
                if h >= 2:
                    dve.wait_ge(d_pick, h - 1)
                dve.tensor_copy(p16[:, :, h, :], ptop[:, :, h, :]).then_inc(d_seq, 1)
                dve.wait_ge(d_seq, seq.up())
                for t in range(2):
                    i = dve.tensor_tensor(eq16[:, h % 2, t], tab16, p16[:, t, h, :].unsqueeze(1).to_broadcast([P, NCAND, TOPK]),
                                          ALU.is_equal)
                i.then_inc(d_match, 1)

            def look_up(h):
                dve.wait_ge(p_eq, h + 1)
                n = NCAND // 2 if h < FOLDED else NCAND
                dve.tensor_reduce(eid[:, :, h, :], eqs[:, h % 2, :, 0:n, :].rearrange("p t c k -> p t k c"), AX.X, ALU.add).then_inc(d_pick, 1)

            def block_u(b):
                for n in range(2):
                    dve.wait_ge(ut_hi, 2 * b + (n + 1))
                    dve.tensor_tensor(ut[:, 1, 4 * n:4 * n + 4], psum[:, n, :].rearrange("p (k n) -> p k n", n=P),
                                      f(ut[:, 0, 4 * n:4 * n + 4]), ALU.subtract).then_inc(ut_lo, 1)

            def last_matches():
                dve.wait_ge(d_match, PH)
                dve.wait_ge(p_cide, PH)
                dve.tensor_tensor(eqs[:, (PH - 1) % 2, 1], eq16[:, (PH - 1) % 2, 1],
                                  cide[:, PH - 1, 1, :].unsqueeze(2).to_broadcast([P, NCAND, TOPK]), ALU.mult).then_inc(d_seq, 1)
                seq.up()

            for h in range(PH + 1):
                if h < PH:
                    best_keys(h)
                if h < 2:
                    best_pairs(h)
                if h > 2:
                    best_pairs(h - 1)
                if h == PH:
                    block_u(0)
                    last_matches()
                if h >= 2:
                    look_up(h - 2)
            dve.tensor_tensor(pick3[:, 2], vtop, vtop[:, :, :, 0:1].to_broadcast([P, 2, PH, TOPK]), ALU.subtract).then_inc(d_sub, 1)
            dve.wait_ge(d_seq, seq.n)
            look_up(PH - 1)
            dve.wait_ge(d_pick, PH)
            dve.tensor_copy(eint, eid).then_inc(d_seq, 1)
            dve.wait_ge(d_seq, seq.up())
            dve.tensor_scalar(fint, eint, 7, None, ALU.logical_shift_right).then_inc(d_seq, 1)
            dve.wait_ge(d_seq, seq.up())
            dve.tensor_copy(pick3[:, 0], fint).then_inc(d_seq, 1)
            dve.wait_ge(d_seq, seq.up())
            dve.tensor_scalar(fint, eint, NK - 1, None, ALU.bitwise_and).then_inc(d_seq, 1)
            dve.wait_ge(d_seq, seq.up())
            dve.tensor_copy(pick3[:, 1], fint).then_inc(d_seq, 1)
            dve.wait_ge(a_soft, 1)
            seq.up()
            dve.tensor_reduce(scal[:, 0:16].rearrange("p (t h) -> p t h", t=2), pick3[:, 2], AX.X, ALU.add).then_inc(d_seq, 1)
            dve.wait_ge(d_seq, seq.up())
            dve.reciprocal(scal[:, 0:16], scal[:, 0:16]).then_inc(d_seq, 1)
            dve.wait_ge(d_seq, seq.up())
            dve.tensor_tensor(pick3[:, 2], pick3[:, 2],
                              scal[:, 0:16].rearrange("p (t h) -> p t h", t=2).unsqueeze(3).to_broadcast([P, 2, PH, TOPK]),
                              ALU.mult).then_inc(d_pick, 1)

            def ones(s, tok):
                dve.tensor_tensor(oh[:, s], iota.unsqueeze(1).unsqueeze(1).to_broadcast([P, 2, GRP, NK]),
                                  picks[:, 0:2, ds(tok, GRP)].unsqueeze(3).to_broadcast([P, 2, GRP, NK]), ALU.is_equal)\
                   .then_inc(oh_up, 1)

            dve.wait_ge(pk_ev, 2)
            for q in range(OHS):
                ones(q, GRP * q)
            with dve.Fori(1, NQ // OHS) as i:
                for s in range(OHS):
                    dve.wait_ge(b_done, OHS * i + (s + 1 - OHS))
                    ones(s, GRP * OHS * i + GRP * s)
            for q in range(Q_LAST, NQ):
                dve.wait_ge(b_done, q - OHS + 1)
                ones(q % OHS, GRP * q)

            def block_v(s, b):
                dve.wait_ge(v_hi, b + 1)
                dve.tensor_tensor(v_sp[:, s, 1, :], v_raw[:, s, :], f(v_sp[:, s, 0, :]), ALU.subtract).then_inc(v_lo, 1)

            def block_g(s, b, first):
                dve.wait_ge(a_gel, b + 1)
                act_in = gel[:, s, :]
                dve.tensor_tensor(gates_at(b), gates_at(b), act_in, ALU.mult).then_inc(d_g32, 1)
                dve.wait_ge(d_g32, b + 1)
                if not first:
                    dve.wait_ge(c_done, b - 1)
                dve.tensor_scalar(g_sp[:, s, 0, :], gates_at(b), 1.0, None, ALU.mult).then_inc(d_seq, 1)
                dve.wait_ge(d_seq, b + (seq.n + 1))
                dve.tensor_tensor(g_sp[:, s, 1, :], gates_at(b), f(g_sp[:, s, 0, :]), ALU.subtract).then_inc(g_lo, 1)

            def gates_at(b):
                return big[:, ds(b * SEQ, SEQ)]

            def expert_block(s, b, first=False, last=False):
                block_v(s, b)
                if not last:
                    block_u(b + 1)
                block_g(s, b, first)

            block_u(1)
            dve.wait_ge(b_ev, NQ)
            block_v(0, 0)
            block_g(0, 0, True)
            expert_block(1, 1, first=True)
            with dve.Fori(1, NK // 2 - 1) as i:
                for s in range(2):
                    expert_block(s, 2 * i + s)
            expert_block(0, NK - 2)
            expert_block(1, NK - 1, last=True)
            dve.wait_ge(c_done, NK)
            dve.wait_ge(ld_h, 32)
            dve.wait_ge(g_lo, NK)
            for t in range(2):
                for n in range(2):
                    a = t * D + n * 512
                    dve.tensor_tensor(big[:, a:a + 512], raw[:, a:a + 512], psum[:, 4 + 2 * t + n, :], ALU.add).then_inc(d_out, 1)

        @block.gpsimd
        def _(pool):
            seq = Count()
            pool.memset(half, -0.5).then_inc(p_half, 1)
            pool.wait_ge(p_half, 1)

            def rsqrt(dst, src, r, n):
                pool.tensor_tensor(dst, src, half[0:r, :].to_broadcast([r, n]), ALU.pow).then_inc(p_rs, 1)

            def split_lo(c):
                pool.wait_ge(w_hi, c - (c > WQ0))
                pool.tensor_tensor(w_sp[:, c % 2, 1], wraw[:, c % 3], f(w_sp[:, c % 2, 0]), ALU.subtract).then_inc(w_lo_o, 1)

            for t, r in enumerate(rows):
                pool.wait_ge(d_ms, t + 1)
                rsqrt(scal[0:r, 8 + t:9 + t], scal[0:r, t:t + 1], r, 1)
            split_lo(1)
            split_lo(5)
            pool.wait_ge(d_qst, 2)
            rsqrt(stat[:, 80:96], stat[:, 32:48], P, 16)

            def norm_rope(t, src, gi, at0, dst):
                hh = HD // 2
                m3, a3, b3 = (tmp_p[:, n, :].rearrange("p (h d) -> p h d", h=NH) for n in range(3))
                c3, n3 = (a[:, trow[t], :].unsqueeze(1).to_broadcast([P, NH, HD]) for a in (cos, sin))
                pool.tensor_tensor(m3, src.rearrange("p (h d) -> p h d", h=NH),
                                   stat[:, at0:at0 + 8].unsqueeze(2).to_broadcast([P, NH, HD]), ALU.mult).then_inc(p_seq, 1)
                pool.wait_ge(p_seq, seq.up())
                pool.tensor_tensor(m3, m3, gqk[:, gi, :].unsqueeze(1).to_broadcast([P, NH, HD]), ALU.mult).then_inc(p_seq, 1)
                pool.wait_ge(p_seq, seq.up())
                pool.tensor_tensor(a3, m3, c3, ALU.mult).then_inc(p_seq, 1)
                seq.up()
                pool.tensor_tensor(b3[:, :, 0:hh], m3[:, :, hh:HD], n3[:, :, 0:hh], ALU.mult).then_inc(p_seq, 1)
                seq.up()
                pool.tensor_tensor(b3[:, :, hh:HD], m3[:, :, 0:hh], n3[:, :, hh:HD], ALU.mult).then_inc(p_seq, 1)
                pool.wait_ge(p_seq, seq.up())
                pool.tensor_tensor(dst.rearrange("p (h d) -> p h d", h=NH), a3, b3, ALU.add).then_inc(p_qk, 1)

            pool.wait_ge(ld_rope, 16)
            pool.wait_ge(ld_small, 80)
            pool.wait_ge(z_ev, z_after(4))
            pool.wait_ge(p_rs, 4)
            for t in range(2):
                norm_rope(t, zq[:, t, :], 0, 80 + 8 * t, qr[:, t, :])
                pool.wait_ge(p_qk, t + 1)
            split_lo(7)
            pool.wait_ge(a_kst, 3 * NH)
            for n, (r, first, w) in enumerate(((META, 64, 8), (P, 48, 16))):
                pool.tensor_scalar(stat[0:r, first:first + w], stat[0:r, first:first + w], EPS, None, ALU.add).then_inc(p_seq, 1)
                pool.wait_ge(p_seq, seq.up())
            pool.tensor_tensor(stat[0:META, 112:120], stat[0:META, 64:72], half[0:META, :].to_broadcast([META, 8]), ALU.pow)\
                .then_inc(p_seq, 1)
            pool.wait_ge(p_seq, seq.up())
            rsqrt(stat[:, 96:112], stat[:, 48:64], P, 16)
            pool.wait_ge(p_rs, 5)
            norm_rope(0, zk[:, 0, :], 1, 96, kr[:, 0, :])
            split_lo(11)
            pool.wait_ge(d_ms, 4)
            rsqrt(scal[:, 48:50], scal[:, 3:5], P, 2)
            split_lo(WQ0 + 1)
            split_lo(WQ0 + 2)

            def staircase(dst, first_, second, done):
                for n, (first, nr, ncol, o) in enumerate(STAIRS):
                    i = pool.tensor_tensor(dst[:, :, o:o + nr * ncol].rearrange("p t (i j) -> p t i j", i=nr),
                                           first_[:, :, first:first + nr].unsqueeze(3).to_broadcast([P, 2, nr, ncol]),
                                           second[:, :, 0:ncol].unsqueeze(2).to_broadcast([P, 2, nr, ncol]), ALU.add)
                    if n == len(STAIRS) - 1:
                        i.then_inc(done, 1)
                    else:
                        i.then_inc(p_seq, 1)
                        seq.up()

            for h in range(PH + 1):
                if h < PH:
                    pool.wait_ge(d_top, h + 1)
                    staircase(cand[:, h], v16[:, h, :, 0, :], v16[:, h, :, 1, :], p_cand)
                if h == 0:
                    continue
                g, s = h - 1, (h - 1) % 2
                pool.wait_ge(n_ev, 2 * g + 2)
                staircase(cide[:, g], n16[:, g, :, 0, :], n16[:, g, :, 1, :], p_cide)
                pool.wait_ge(p_seq, seq.n)
                pool.wait_ge(p_cide, g + 1)
                pool.wait_ge(d_match, g + 1)
                tiles = 2 if g < PH - 1 else 1
                for t in range(tiles):
                    i = pool.tensor_tensor(eqs[:, s, t], eq16[:, s, t], cide[:, g, t, :].unsqueeze(2).to_broadcast([P, NCAND, TOPK]),
                                           ALU.mult)
                    if g < FOLDED:
                        i.then_inc(p_seq, 1)
                if g >= FOLDED:
                    i.then_inc(p_eq, 1)
                if g < FOLDED:
                    seq.up()
                    pool.wait_ge(p_seq, seq.up())
                    hf = NCAND // 2
                    pool.tensor_tensor(eqs[:, s, :, 0:hf], eqs[:, s, :, 0:hf], eqs[:, s, :, hf:], ALU.add).then_inc(p_eq, 1)

            def gated(s, tok):
                n = GRP - ACT_T
                pool.tensor_tensor(oh_g[:, s, ACT_T:, :], f(oh[:, s, 1, ACT_T:, :]),
                                   picks[:, 2, ds(tok + ACT_T, n)].unsqueeze(2).to_broadcast([P, n, NK]), ALU.mult)\
                    .then_inc(ohp_up, 1)

            pool.wait_ge(pk_ev, 2)
            for q in range(OHS):
                pool.wait_ge(oh_up, q + 1)
                gated(q, GRP * q)
            with pool.Fori(1, NQ // OHS) as i:
                for s in range(OHS):
                    pool.wait_ge(oh_up, OHS * i + (s + 1))
                    gated(s, GRP * OHS * i + GRP * s)
            for q in range(Q_LAST, NQ):
                pool.wait_ge(oh_up, q + 1)
                gated(q % OHS, GRP * q)

        @block.tensor
        def _(pe):
            def transpose8(t, banks, r):
                flat = psum[:, banks[0]:banks[-1] + 1, :].rearrange("p b n -> p (b n)")
                for k in range(DK):
                    i = pe.transpose(flat[:, k * r:(k + 1) * r], xs[0:r, t, k * P:(k + 1) * P], ident[0:r, 0:r])
                i.then_inc(pe_x, 1)

            def split_products(dst, lhs, rhs):
                n = 0
                for k in range(DK):
                    for a, b in ((0, 0), (0, 1), (1, 0)):
                        i = pe.matmul(dst, lhs(a, k), rhs(b, k), start=(n == 0), stop=(n == 3 * DK - 1))
                        n += 1
                return i

            def product(dst, lhs, rhs, sem_):
                split_products(dst, lhs, rhs).then_inc(sem_, 1)

            def tokens(a, k, t):
                return ht[:, a, k, t * P:(t + 1) * P] if t < 2 else hm[:, a, k, :]

            def project(s, nt, n):
                for t in range(nt):
                    project_tile(s, t, n)

            def project_tile(s, t, n):
                product(psum[0:rows[t], 3 * s + t, 0:n], lambda a, k: tokens(a, k, t), lambda b, k: w_sp[:, s, b, k, 0:n], z_done)

            pe.wait_ge(ld_cst, 16)
            pe.wait_ge(ld_small, 80)
            pe.transpose(psum[:, 5, 0:20], grow[0:20, :], ident[0:20, 0:20]).then_inc(pe_gain, 1)
            for t, b in enumerate(([0, 1], [2, 3], [4])):
                pe.wait_ge(a_xs, t + 1)
                transpose8(t, b, rows[t])
            pe.wait_ge(d_t32, 3)
            pe.wait_ge(ld_w[0], 16)
            for toks, n, at0 in ((t32, SEQ, 0), (t32m, META, SEQ)):
                for k in range(DK):
                    i = pe.matmul(psum[0:CI, 5, at0:at0 + n], wraw[:, 0, k, 0:CI], toks[:, k, :], start=(k == 0), stop=(k == DK - 1))
                i.then_inc(pe_zt, 1)
            pe.wait_ge(zt_ev, 1)
            for t, r in enumerate(rows):
                pe.transpose(psum[0:r, t, 0:CI], zt[0:CI, t * P:t * P + r], ident[0:CI, 0:CI]).then_inc(z_done, 1)
            pe.wait_ge(d_lo, 3)
            for c in range(1, 5):
                lo_ready(pe, c)
                if c >= 2:
                    pe.wait_ge(z_ev, z_after(c - 2))
                project(c % 2, 2, CW)
            pe.wait_ge(z_ev, z_after(4))
            for t in range(2):
                pe.wait_ge(d_iq, t + 1)
                for a in range(PAIRS):
                    i = pe.transpose(psum[:, t, a * P:(a + 1) * P], iqr[:, t, a * P:(a + 1) * P], ident)
                i.then_inc(pe_ix, 1)
            pe.wait_ge(d_ki, 6)
            for t, first in ((2, 0), (0, META), (1, META + P)):
                r = rows[t]
                i = pe.transpose(psum[:, 2, first:first + r], kir[0:r, t, :], ident[0:r, 0:r])
            i.then_inc(pe_ix, 1)
            pe.wait_ge(ix_tr, 3)
            for t in range(2):
                for h in range(NH):
                    lo = HD * (h % 2)
                    i = pe.matmul(psum[:, h, KOFF[t]:KOFF[t] + KEYS[t]], iqt[lo:lo + HD, h // 2, t * P:(t + 1) * P],
                                  kit[lo:lo + HD, 0:KEYS[t]], start=True, stop=True)
                i.then_inc(pe_sc, 1)
            pe.wait_ge(a_rel, 2)
            with pe.Fori(0, 2) as i:
                pe.wait_ge(w_lo_o, i + 2)
                pe.wait_ge(z_ev, 6 * i + z_after(3))
                project(1, 3, CW)
                pe.wait_ge(w_lo_e, i + 4)
                pe.wait_ge(z_ev, 6 * i + z_after(4))
                pe.wait_ge(a_rel, 6)
                project(0, 3, CW)
            lo_ready(pe, 9)
            pe.wait_ge(z_ev, z_after(7))
            project(1, 3, CW)
            pe.wait_ge(z_ev, z_after(9))
            for t in range(2):
                pe.wait_ge(p_qk, t + 1)
                for a in range(PAIRS):
                    i = pe.transpose(psum[:, t, a * P:(a + 1) * P], qr[:, t, a * P:(a + 1) * P], ident)
                i.then_inc(pe_qk, 1)
            for n, t in enumerate((2, 0, 1)):
                if t == 0:
                    pe.wait_ge(p_qk, 3)
                else:
                    pe.wait_ge(d_qk, 1 if t == 2 else 2)
                r = rows[t]
                for a in range(PAIRS):
                    i = pe.transpose(psum[:, 2 + n, a * r:(a + 1) * r], kr[0:r, t, a * P:(a + 1) * P], ident[0:r, 0:r])
                i.then_inc(pe_qk, 1)
            pe.wait_ge(qk_tr, 5)
            for t in range(2):
                for h in range(NH):
                    lo = HD * (h % 2)
                    i = pe.matmul(psum[:, h, KOFF[t]:KOFF[t] + KEYS[t]], qt[lo:lo + HD, h // 2, t * P:(t + 1) * P],
                                  kt[lo:lo + HD, h // 2, 0:KEYS[t]], start=True, stop=True)
                i.then_inc(pe_log, 1)
            pe.wait_ge(d_log, 2)
            lo_ready(pe, N_IN - 1)
            project(0, 3, CW)
            pe.wait_ge(d_log, 4)
            pe.wait_ge(z_ev, z_after(N_IN - 1))
            pe.wait_ge(ld_band, 32)
            for t in range(2):
                for g in range(4):
                    dst = psum[:, 6 + t, g * P:(g + 1) * P]
                    gs = slice(g * P, (g + 1) * P)
                    pe.matmul(dst, zp[:, t, gs], band[:, 0, g, :], start=True, stop=False)
                    i = (pe.matmul(dst, zp[0:META, 2, gs], band[0:META, 2, g, :], start=False, stop=True) if t == 0
                         else pe.matmul(dst, zp[:, 0, gs], band[:, 1, g, :], start=False, stop=True))
            i.then_inc(pe_y, 1)

            for n, (t, r, first, b) in enumerate(((0, META, 0, 0), (0, P, META, 2), (1, META, 0, 4), (1, P, META, 6),
                                                  (1, P, META + P, 0))):
                if n == 2:
                    pe.wait_ge(y_ev, 1)
                    for g in range(4):
                        i = pe.matmul(psum[:, 6 + g // 2, (g % 2) * SEQ:(g % 2 + 1) * SEQ], poolw[:, g, :], yt[:, g, :],
                                      start=True, stop=True)
                    i.then_inc(pe_y, 1)
                pe.wait_ge(d_prob, t + 1)
                if n == 3:
                    pe.wait_ge(d_p32, 1)
                if n == 4:
                    pe.wait_ge(pt_ev, 1)
                for h in range(NH):
                    a = NH * KOFF[t] + h * KEYS[t] + first
                    i = pe.transpose(psum[0:r, b + h // 4, (h % 4) * P:(h % 4 + 1) * P], rel[:, a:a + r], ident)
                i.then_inc(pe_pt, 1)
            for t in range(2):
                chunks = ((0, 2, META), (1, 0, P)) if t == 0 else ((2, 2, META), (3, 0, P), (4, 1, P))
                pe.wait_ge(pt_ev, 2 if t == 0 else 5)
                for h in range(NH):
                    lo = HD * (h % 2)
                    for n, (c, vt, r) in enumerate(chunks):
                        i = pe.matmul(psum[lo:lo + HD, CAT_BANK[t], (h // 2) * P:(h // 2 + 1) * P], zv[0:r, vt, h * HD:(h + 1) * HD],
                                      pt[0:r, c, h, :], start=(n == 0), stop=(n == len(chunks) - 1))
                i.then_inc(pe_cat, 1)
            pe.wait_ge(pc_lo, 1)
            for c in range(OUT0, WQ0):
                lo_ready(pe, c)
                if c >= OUT0 + 2:
                    pe.wait_ge(h_ev, 2 * (c - OUT0 - 1))
                for t in range(2):
                    if c == OUT0:
                        pe.wait_ge(cat_lo, t + 1)
                    project_tile(c % 2, t, CW)
            pe.wait_ge(ld_g2, 32)
            for a in range(2):
                i = pe.transpose(psum[:, 5, a * P:(a + 1) * P], ksub[:, a, :], ident)
            i.then_inc(pe_ks, 1)
            pe.wait_ge(h_ev, 2 * N_OUT)
            for t, b in enumerate(([6, 7], [0, 1])):
                if t == 0:
                    pe.wait_ge(d_xs, 1)
                else:
                    pe.wait_ge(a_xs, 4)
                transpose8(t, b, P)
            pe.wait_ge(d_t32, 5)
            pe.wait_ge(ks_ev, 1)

            def queries(c, a):
                dst = psum[:, 3 * (c % 2), a * SEQ:(a + 1) * SEQ]
                cols = slice(a * P, (a + 1) * P)
                if c in (WQ0 + 1, WQ0 + 2):
                    i = split_products(dst, lambda u, k: w_sp[:, c % 2, u, k, cols], lambda w, k: ht[:, w, k, :])
                else:
                    for k in range(DK):
                        i = pe.matmul(dst, wraw[:, c % 3, k, cols], t32[:, k, :], start=(k == 0), stop=(k == DK - 1))
                if a == 1:
                    i.then_inc(z_done, 1)

            def sub_scores(s, q):
                for t in range(2):
                    for a in range(2):
                        i = pe.matmul(psum[:, 3 * s + 1, (2 * t + a) * P:(2 * t + a + 1) * P], qp[:, q, a, t * P:(t + 1) * P],
                                      kt_sub[:, a, :], start=True, stop=True)
                i.then_inc(pe_s, 1)

            for h in range(PH + 1):
                c = WQ0 + h
                if h < PH:
                    if h in (1, 2):
                        pe.wait_ge(d_lo, 5)
                        lo_ready(pe, c)
                    else:
                        pe.wait_ge(ld_w[c % 3], 16 * (c // 3 + 1))
                    queries(c, 0)
                    if h < 2:
                        queries(c, 1)
                if h != 2:
                    g = h if h < 2 else h - 1
                    pe.wait_ge(qp_ev, g + 1)
                    if g >= 2:
                        pe.wait_ge(s_ev, g - 1)
                    sub_scores((WQ0 + g) % 2, g % 2)
                if 2 <= h < PH:
                    queries(c, 1)
            def turn_u(s, landed):
                pe.wait_ge(ld_u[s], landed)
                for k in range(DK):
                    i = pe.transpose(psum[:, k // 4, (k % 4) * P:(k % 4 + 1) * P], u_raw[:, s, k, :], ident)
                i.then_inc(t_done, 1)

            pe.wait_ge(s_ev, PH)
            turn_u(0, 16)
            pe.wait_ge(ut_lo, 2)
            turn_u(1, 16)
            pe.wait_ge(d_pick, PH + 1)
            for a in range(3):
                for t in range(2):
                    i = pe.transpose(psum[:, 6 + a // 2, (a % 2) * SEQ + t * P:(a % 2) * SEQ + (t + 1) * P],
                                     pick3[:, a, t].rearrange("p h k -> p (h k)"), ident)
                if a:
                    i.then_inc(pe_pk, 1)

            def gate_group(q, s, first=False):
                pe.wait_ge(ohg_up, q + 1)
                pe.wait_ge(ohp_up, q + 1)
                if not first:
                    pe.wait_ge(b_ev, q - OHS + 1)
                for j in range(GRP):
                    i = pe.matmul(psum[:, 2 + 2 * s + j // 4, (j % 4) * P:(j % 4 + 1) * P], f(oh[:, s, 0, j, :]), oh_g[:, s, j, :],
                                  start=True, stop=True)
                i.then_inc(b_done, 1)

            for q in range(OHS):
                gate_group(q, q, True)
            with pe.Fori(1, NQ // OHS) as i:
                for s in range(OHS):
                    gate_group(OHS * i + s, s)
            for q in range(Q_LAST, NQ):
                gate_group(q, q % OHS)

            def up(s):
                product(psum[:, 2 + s, 0:SEQ], lambda a, k: ut[:, a, k, :], lambda b, k: ht[:, b, k, :], a_done)

            def down(s, first, last):
                for t in range(2):
                    for n in range(2):
                        for m, (a, b) in enumerate(((0, 0), (0, 1), (1, 0))):
                            i = pe.matmul(psum[:, 4 + 2 * t + n, :], g_sp[:, s, a, t * P:(t + 1) * P],
                                          v_sp[:, s, b, n * 512:(n + 1) * 512], start=(first and m == 0), stop=(last and m == 2))
                i.then_inc(c_done, 1)

            def turn(b, s, first, last, more=True):
                if more:
                    pe.wait_ge(ut_lo, 2 * b + 2)
                    turn_u(1 - s, 8 * b + 16 + 8 * s)
                pe.wait_ge(g_lo, b)
                pe.wait_ge(v_lo, b)
                down(1 - s, first, last)
                if more:
                    pe.wait_ge(ut_lo, 2 * b + 4)
                    pe.wait_ge(a_gel, b)
                    up(1 - s)

            pe.wait_ge(d_lo, 5)
            pe.wait_ge(b_ev, NQ - 1)
            up(0)
            pe.wait_ge(b_ev, NQ)
            pe.wait_ge(ut_lo, 4)
            up(1)
            turn(1, 1, True, False)
            turn(2, 0, False, False)
            with pe.Fori(1, NK // 2 - 1) as i:
                turn(2 * i + 1, 1, False, False)
                turn(2 * i + 2, 0, False, False)
            turn(NK - 1, 1, False, False, more=False)
            turn(NK, 0, False, True, more=False)


_INS = ['x', 'meta_tokens', 'norm1_g', 'w_in', 'q_norm_g', 'k_norm_g', 'pool_w', 'pool_scale', 'w_out', 'norm2_g',
        'peer_wq', 'sub_keys1', 'sub_keys2', 'peer_u', 'peer_v']


def constants():
    import numpy as np
    c = np.zeros((P, N_CONST), np.float32)
    c[:, K_ID:K_ID + P] = np.eye(P)
    c[:, K_IOTA:K_IOTA + P] = np.arange(P)
    inv = (np.float32(10000.0) ** (-np.arange(0, HD, 2, dtype=np.float32) / np.float32(HD))).astype(np.float32)
    ang = (np.arange(T, dtype=np.float32)[:, None] * inv[None, :]).astype(np.float32)
    cs = np.cos(ang.astype(np.float64)).astype(np.float32)
    sn = np.sin(ang.astype(np.float64)).astype(np.float32)
    for n, (first, r) in enumerate(((0, META), (META, P), (META + P, P))):
        for at, a, b in ((K_COS, cs, cs), (K_SIN, -sn, sn)):
            c[0:r, at + n * HD:at + n * HD + HD // 2] = a[first:first + r]
            c[0:r, at + n * HD + HD // 2:at + (n + 1) * HD] = b[first:first + r]
    band = np.zeros((P, 3, 4, P), np.float32)
    for g, w in enumerate((2, 4, 8, 16)):
        for t in range(P):
            for s in range(t - w + 1, t + 1):
                if s >= 0:
                    band[s, 0, g, t] += 1.0 / w
                else:
                    band[P + s, 1, g, t] += 1.0 / w
                    band[META + s, 2, g, t] += 1.0 / w
            band[t, 0, g, t] -= 1.0
    c[:, K_BAND:] = band.reshape(P, -1)
    return c


def kernel(**inputs):
    import numpy as _np
    import concourse.bacc as _bacc
    from concourse import mybir as _mybir
    from concourse.bass_utils import run_bass_kernel_spmd as _run

    nc = _bacc.Bacc("TRN2", target_bir_lowering=False, num_devices=1)
    arrays, args = {}, []
    for name in _INS + ["const"]:
        a = constants() if name == "const" else _np.ascontiguousarray(inputs[name])
        arrays[f"in_{name}_dram"] = a
        args.append(nc.dram_tensor(f"in_{name}_dram", a.shape, _mybir.dt.from_np(a.dtype), kind="ExternalInput").ap())
    args.append(nc.dram_tensor("out_0_dram", (1, SEQ, D), _mybir.dt.float32, kind="ExternalOutput").ap())
    layer(nc, *args)
    r = _run(nc, [arrays], core_ids=[0])
    return r.results[0]["out_0_dram"]
```
